# Optimizing a Trainium2 kernel written in Bass

```python
import math
import jax, jax.numpy as jnp
from jax import lax
import numpy as np

D_MODEL = 1024
BATCH = 1
SEQ = 1024
DEPTH = 2
DEC_BATCH = 8
DEC_SEQ = 4
PAST_LEN = 4096
PAGE_SIZE = 128

N_EVEN = (DEPTH + 1) // 2
N_ODD = DEPTH // 2
D_A = D_MODEL // 2
CONV_A = 3
D_B = D_MODEL // 2
B_HEADS = 8
B_HEAD_DIM = D_B // B_HEADS
CONV_B = 4
LRU_C = 8.0
D_C = D_MODEL // 2
CONV_C = 31
MLA_HEADS = 8
QK_NOPE = 64
QK_ROPE = 32
V_DIM = D_MODEL // (2 * MLA_HEADS)
Q_RANK = 3 * D_MODEL // 8
KV_RANK = D_MODEL // 4
ROPE_THETA = 10000.0
ATTN_SCALE = (QK_NOPE + QK_ROPE) ** -0.5
Q_BLOCK = 128
N_EXPERTS = 16
N_GROUPS = 4
EXPERTS_PER_GROUP = N_EXPERTS // N_GROUPS
TOP_K = 2
D_EXPERT = D_MODEL // 2
MOE_BLOCK = 128
ALPHA = (2 * DEPTH) ** 0.25
BETA = (8 * DEPTH) ** -0.25
EVEN_IN = 3 * D_A + 2 * D_B
ODD_IN = 2 * D_C + Q_RANK + KV_RANK + QK_ROPE
MIX_OUT_EVEN = D_A + D_B
MIX_OUT_ODD = D_C + MLA_HEADS * V_DIM

kernel_name = 'hybrid_conv_rglru_conformer_mla_moe_step'

def layer_norm(x, g, b, eps=1e-5):
    xf = x.astype(jnp.float32)
    mu = xf.mean(-1, keepdims=True)
    var = jnp.square(xf - mu).mean(-1, keepdims=True)
    return ((xf - mu) * lax.rsqrt(var + eps) * g + b).astype(x.dtype)

def rms_norm(x, g, eps=1e-6):
    xf = x.astype(jnp.float32)
    return (xf * lax.rsqrt(jnp.square(xf).mean(-1, keepdims=True) + eps) * g).astype(x.dtype)

def causal_dwconv(x, buf, w, b=None):
    xp = jnp.concatenate([buf.astype(x.dtype), x], axis=1)
    width, ch = w.shape
    y = lax.conv_general_dilated(xp, w[:, None, :].astype(x.dtype), window_strides=(1,), padding='VALID',
                                 dimension_numbers=('NWC', 'WIO', 'NWC'), feature_group_count=ch)
    if b is not None:
        y = y + b
    return y, xp[:, xp.shape[1] - (width - 1):]

def apply_rope(x, pos):
    half = x.shape[-1] // 2
    inv = ROPE_THETA ** (-jnp.arange(half, dtype=jnp.float32) / half)
    ang = pos.astype(jnp.float32)[:, None] * inv
    ang = ang.reshape(ang.shape[0], *([1] * (x.ndim - 3)), half)
    cos, sin = jnp.cos(ang).astype(x.dtype), jnp.sin(ang).astype(x.dtype)
    x1, x2 = x[..., :half], x[..., half:]
    return jnp.concatenate([x1 * cos - x2 * sin, x1 * sin + x2 * cos], axis=-1)

def rg_lru(u, h0, wa, ba, wx, bx, lam):
    bsz, t, dr = u.shape
    uh = u.reshape(bsz, t, B_HEADS, B_HEAD_DIM)
    r = jax.nn.sigmoid(jnp.einsum('bthi,hij->bthj', uh, wa).reshape(bsz, t, dr) + ba)
    i = jax.nn.sigmoid(jnp.einsum('bthi,hij->bthj', uh, wx).reshape(bsz, t, dr) + bx)
    log_a = (-LRU_C * r.astype(jnp.float32)) * jax.nn.softplus(-lam.astype(jnp.float32))
    a = jnp.exp(log_a)
    b = jnp.sqrt(-jnp.expm1(2.0 * log_a)) * (i * u).astype(jnp.float32)

    def step(h, ab):
        a_t, b_t = ab
        h = a_t * h + b_t
        return h, h

    h_last, hs = lax.scan(step, h0.astype(jnp.float32), (jnp.swapaxes(a, 0, 1), jnp.swapaxes(b, 0, 1)))
    return jnp.swapaxes(hs, 0, 1).astype(u.dtype), h_last.astype(u.dtype)

def even_mixer(x, buf_a, buf_b, h0, w_in, conv_a_w, conv_b_w, conv_b_b, lru_wa, lru_ba, lru_wx, lru_bx,
               lru_lambda, w_out):
    z = x @ w_in
    g_b, g_c, v_a, gate_b, v_b = jnp.split(z, [D_A, 2 * D_A, 3 * D_A, 3 * D_A + D_B], axis=-1)
    u_a, new_buf_a = causal_dwconv(g_c * v_a, buf_a, conv_a_w)
    y_a = g_b * u_a
    u_b, new_buf_b = causal_dwconv(v_b, buf_b, conv_b_w, conv_b_b)
    y_lru, h_last = rg_lru(u_b, h0, lru_wa, lru_ba, lru_wx, lru_bx, lru_lambda)
    y_b = jax.nn.gelu(gate_b) * y_lru
    return jnp.concatenate([y_a, y_b], axis=-1) @ w_out, new_buf_a, new_buf_b, h_last

def mla_attend(q_lat, q_pe, ckv, kpe, q_pos, k_pos):
    def block(args):
        ql, qp, qpos = args
        s = (jnp.einsum('bthr,bsr->bhts', ql, ckv) + jnp.einsum('bthp,bsp->bhts', qp, kpe)).astype(jnp.float32)
        s = jnp.where(k_pos[None, None, None, :] <= qpos[None, None, :, None], s * ATTN_SCALE, -jnp.inf)
        p = jax.nn.softmax(s, axis=-1).astype(ckv.dtype)
        return jnp.einsum('bhts,bsr->bthr', p, ckv)

    t = q_lat.shape[1]
    if t > Q_BLOCK and t % Q_BLOCK == 0:
        nb = t // Q_BLOCK

        def split(a):
            return jnp.moveaxis(a.reshape(a.shape[0], nb, Q_BLOCK, *a.shape[2:]), 1, 0)

        o = lax.map(block, (split(q_lat), split(q_pe), q_pos.reshape(nb, Q_BLOCK)))
        return jnp.moveaxis(o, 0, 1).reshape(q_lat.shape)
    return block((q_lat, q_pe, q_pos))

def odd_mixer(x, buf_c, past_ckv, past_kpe, pos0, w_in, conv_c_w, conv_c_b, ln_c_g, ln_c_b, q_norm_g, w_q_b,
              kv_norm_g, w_uk, w_uv, w_out):
    bsz, t, _ = x.shape
    z = x @ w_in
    glu_a, glu_b, q_a, kv_a, k_pe = jnp.split(
        z, [D_C, 2 * D_C, 2 * D_C + Q_RANK, 2 * D_C + Q_RANK + KV_RANK], axis=-1)
    u_c, new_buf_c = causal_dwconv(glu_a * jax.nn.sigmoid(glu_b), buf_c, conv_c_w, conv_c_b)
    y_c = jax.nn.silu(layer_norm(u_c, ln_c_g, ln_c_b))
    pos = pos0 + jnp.arange(t)
    q = (rms_norm(q_a, q_norm_g) @ w_q_b).reshape(bsz, t, MLA_HEADS, QK_NOPE + QK_ROPE)
    q_nope, q_pe = q[..., :QK_NOPE], apply_rope(q[..., QK_NOPE:], pos)
    ckv_new = rms_norm(kv_a, kv_norm_g)
    kpe_new = apply_rope(k_pe, pos)
    if past_ckv is None:
        ckv_all, kpe_all, k_pos = ckv_new, kpe_new, pos
    else:
        ckv_all = jnp.concatenate([past_ckv.astype(x.dtype), ckv_new], axis=1)
        kpe_all = jnp.concatenate([past_kpe.astype(x.dtype), kpe_new], axis=1)
        k_pos = jnp.arange(past_ckv.shape[1] + t)
    q_lat = jnp.einsum('bthn,rhn->bthr', q_nope, w_uk)
    o_lat = mla_attend(q_lat, q_pe, ckv_all, kpe_all, pos, k_pos)
    y_d = jnp.einsum('bthr,rhv->bthv', o_lat, w_uv).reshape(bsz, t, MLA_HEADS * V_DIM)
    return jnp.concatenate([y_c, y_d], axis=-1) @ w_out, new_buf_c, ckv_new, kpe_new

def moe(x, w_router, b_router, w_exp_in, w_exp_out):
    shape = x.shape
    xt = x.reshape(-1, shape[-1])
    n_tok = xt.shape[0]
    scores = jax.nn.sigmoid((xt @ w_router).astype(jnp.float32))
    sel = (scores + b_router.astype(jnp.float32)).reshape(n_tok, N_GROUPS, EXPERTS_PER_GROUP)
    group_score = lax.top_k(sel, 2)[0].sum(-1)
    grp = jnp.argmax(group_score, axis=-1).astype(jnp.int32)
    in_grp = jnp.take_along_axis(sel, grp[:, None, None], axis=1)[:, 0]
    _, local = lax.top_k(in_grp, TOP_K)
    expert_idx = grp[:, None] * EXPERTS_PER_GROUP + local.astype(jnp.int32)
    gate = jnp.take_along_axis(scores, expert_idx, axis=1)
    gate = gate / gate.sum(-1, keepdims=True)
    n_assign = n_tok * TOP_K
    flat_e = expert_idx.reshape(-1)
    order = jnp.argsort(flat_e).astype(jnp.int32)
    sorted_e = flat_e[order]
    counts = jnp.bincount(flat_e, length=N_EXPERTS)
    starts = jnp.cumsum(counts) - counts
    padded = (counts + MOE_BLOCK - 1) // MOE_BLOCK * MOE_BLOCK
    pad_ends = jnp.cumsum(padded)
    pad_starts = pad_ends - padded
    dest_sorted = (pad_starts[sorted_e] + jnp.arange(n_assign) - starts[sorted_e]).astype(jnp.int32)
    pad_total = (n_assign + N_EXPERTS * (MOE_BLOCK - 1) + MOE_BLOCK - 1) // MOE_BLOCK * MOE_BLOCK
    n_blocks = pad_total // MOE_BLOCK
    tok_buf = jnp.full((pad_total,), n_tok, jnp.int32).at[dest_sorted].set(order // TOP_K)
    dest = jnp.zeros((n_assign,), jnp.int32).at[order].set(dest_sorted)
    blk_e = jnp.minimum(jnp.searchsorted(pad_ends, jnp.arange(n_blocks) * MOE_BLOCK, side='right'),
                        N_EXPERTS - 1)
    x_pad = jnp.concatenate([xt, jnp.zeros((1, xt.shape[1]), xt.dtype)], axis=0)
    xb = x_pad[tok_buf].reshape(n_blocks, MOE_BLOCK, xt.shape[1])

    def expert_block(args):
        xblk, e = args
        hg, hu = jnp.split(xblk @ w_exp_in[e], 2, axis=-1)
        return (jax.nn.silu(hg) * hu) @ w_exp_out[e]

    yb = lax.map(expert_block, (xb, blk_e)).reshape(pad_total, -1)
    y_assign = yb[dest].reshape(n_tok, TOP_K, -1)
    return jnp.einsum('tk,tkd->td', gate.astype(x.dtype), y_assign).reshape(shape)

def setup_inputs(seed: int = 0) -> dict:
    key = jax.random.key(seed)
    ks = iter(jax.random.split(key, 48))

    def nrm(shape, scale):
        return jax.random.normal(next(ks), shape, jnp.float32) * scale

    n_pages = PAST_LEN // PAGE_SIZE
    n_used = DEC_BATCH * n_pages
    n_phys = n_used + max(1, n_used // 4)
    page_table = jax.random.permutation(next(ks), n_phys)[:n_used].reshape(DEC_BATCH, n_pages).astype(jnp.int32)
    u = jax.random.uniform(next(ks), (N_EVEN, D_B), jnp.float32, 0.9, 0.999)
    a_base = u ** (1.0 / LRU_C)
    lru_lambda = jnp.log(a_base) - jnp.log1p(-a_base)
    return {
        'x_prompt': nrm((BATCH, SEQ, D_MODEL), 1.0),
        'x_sample': nrm((DEC_BATCH, DEC_SEQ, D_MODEL), 1.0),
        'state_conv_a': nrm((N_EVEN, DEC_BATCH, CONV_A - 1, D_A), 1.0),
        'state_conv_b': nrm((N_EVEN, DEC_BATCH, CONV_B - 1, D_B), 1.0),
        'state_rglru_h': nrm((N_EVEN, DEC_BATCH, D_B), 0.5),
        'state_conv_c': nrm((N_ODD, DEC_BATCH, CONV_C - 1, D_C), 1.0),
        'cache_ckv': nrm((n_phys, N_ODD, PAGE_SIZE, KV_RANK), 1.0),
        'cache_kpe': nrm((n_phys, N_ODD, PAGE_SIZE, QK_ROPE), 1.0),
        'page_table': page_table,
        'w_in_even': nrm((N_EVEN, D_MODEL, EVEN_IN), D_MODEL ** -0.5),
        'conv_a_w': nrm((N_EVEN, CONV_A, D_A), CONV_A ** -0.5),
        'conv_b_w': nrm((N_EVEN, CONV_B, D_B), CONV_B ** -0.5),
        'conv_b_b': nrm((N_EVEN, D_B), 0.02),
        'lru_wa': nrm((N_EVEN, B_HEADS, B_HEAD_DIM, B_HEAD_DIM), B_HEAD_DIM ** -0.5),
        'lru_ba': nrm((N_EVEN, D_B), 0.1),
        'lru_wx': nrm((N_EVEN, B_HEADS, B_HEAD_DIM, B_HEAD_DIM), B_HEAD_DIM ** -0.5),
        'lru_bx': nrm((N_EVEN, D_B), 0.1),
        'lru_lambda': lru_lambda,
        'w_out_even': nrm((N_EVEN, MIX_OUT_EVEN, D_MODEL), BETA * MIX_OUT_EVEN ** -0.5),
        'w_in_odd': nrm((N_ODD, D_MODEL, ODD_IN), D_MODEL ** -0.5),
        'conv_c_w': nrm((N_ODD, CONV_C, D_C), CONV_C ** -0.5),
        'conv_c_b': nrm((N_ODD, D_C), 0.02),
        'ln_c_g': 1.0 + nrm((N_ODD, D_C), 0.02),
        'ln_c_b': nrm((N_ODD, D_C), 0.02),
        'q_norm_g': 1.0 + nrm((N_ODD, Q_RANK), 0.02),
        'w_q_b': nrm((N_ODD, Q_RANK, MLA_HEADS * (QK_NOPE + QK_ROPE)), Q_RANK ** -0.5),
        'kv_norm_g': 1.0 + nrm((N_ODD, KV_RANK), 0.02),
        'w_uk': nrm((N_ODD, KV_RANK, MLA_HEADS, QK_NOPE), KV_RANK ** -0.5),
        'w_uv': nrm((N_ODD, KV_RANK, MLA_HEADS, V_DIM), BETA * KV_RANK ** -0.5),
        'w_out_odd': nrm((N_ODD, MIX_OUT_ODD, D_MODEL), BETA * MIX_OUT_ODD ** -0.5),
        'ln_mix_g': 1.0 + nrm((DEPTH, D_MODEL), 0.02),
        'ln_mix_b': nrm((DEPTH, D_MODEL), 0.02),
        'ln_ffn_g': 1.0 + nrm((DEPTH, D_MODEL), 0.02),
        'ln_ffn_b': nrm((DEPTH, D_MODEL), 0.02),
        'w_router': nrm((D_MODEL, N_EXPERTS), D_MODEL ** -0.5),
        'b_router': nrm((N_EXPERTS,), 0.01),
        'w_exp_in': nrm((DEPTH, N_EXPERTS, D_MODEL, 2 * D_EXPERT), BETA * D_MODEL ** -0.5),
        'w_exp_out': nrm((DEPTH, N_EXPERTS, D_EXPERT, D_MODEL), BETA * D_EXPERT ** -0.5),
    }

def reference(x_prompt, x_sample, state_conv_a, state_conv_b, state_rglru_h, state_conv_c, cache_ckv, cache_kpe,
              page_table, w_in_even, conv_a_w, conv_b_w, conv_b_b, lru_wa, lru_ba, lru_wx, lru_bx, lru_lambda,
              w_out_even, w_in_odd, conv_c_w, conv_c_b, ln_c_g, ln_c_b, q_norm_g, w_q_b, kv_norm_g, w_uk, w_uv,
              w_out_odd, ln_mix_g, ln_mix_b, ln_ffn_g, ln_ffn_b, w_router, b_router, w_exp_in, w_exp_out):
    bp, dbs = x_prompt.shape[0], x_sample.shape[0]
    past_len = page_table.shape[1] * PAGE_SIZE
    dt = x_prompt.dtype
    xp, xs = x_prompt, x_sample
    ca_p, ca_s, cb_p, cb_s, h_p, h_s = [], [], [], [], [], []
    cc_p, cc_s, ckv_p, ckv_s, kpe_p, kpe_s = [], [], [], [], [], []
    for l in range(DEPTH):
        j = l // 2
        if l % 2 == 0:
            ev = (w_in_even[j], conv_a_w[j], conv_b_w[j], conv_b_b[j], lru_wa[j], lru_ba[j], lru_wx[j], lru_bx[j],
                  lru_lambda[j], w_out_even[j])
            mp, a1, b1, h1 = even_mixer(xp, jnp.zeros((bp, CONV_A - 1, D_A), dt), jnp.zeros((bp, CONV_B - 1, D_B), dt),
                                        jnp.zeros((bp, D_B), dt), *ev)
            ms, a2, b2, h2 = even_mixer(xs, state_conv_a[j], state_conv_b[j], state_rglru_h[j], *ev)
            ca_p.append(a1); ca_s.append(a2); cb_p.append(b1); cb_s.append(b2); h_p.append(h1); h_s.append(h2)
        else:
            od = (w_in_odd[j], conv_c_w[j], conv_c_b[j], ln_c_g[j], ln_c_b[j], q_norm_g[j], w_q_b[j], kv_norm_g[j],
                  w_uk[j], w_uv[j], w_out_odd[j])
            mp, c1, k1, p1 = odd_mixer(xp, jnp.zeros((bp, CONV_C - 1, D_C), dt), None, None, 0, *od)
            past_ckv = cache_ckv[page_table, j].reshape(dbs, past_len, KV_RANK)
            past_kpe = cache_kpe[page_table, j].reshape(dbs, past_len, QK_ROPE)
            ms, c2, k2, p2 = odd_mixer(xs, state_conv_c[j], past_ckv, past_kpe, past_len, *od)
            cc_p.append(c1); cc_s.append(c2); ckv_p.append(k1); ckv_s.append(k2); kpe_p.append(p1); kpe_s.append(p2)
        xp = layer_norm(ALPHA * xp + mp, ln_mix_g[l], ln_mix_b[l])
        xs = layer_norm(ALPHA * xs + ms, ln_mix_g[l], ln_mix_b[l])
        xp = layer_norm(ALPHA * xp + moe(xp, w_router, b_router, w_exp_in[l], w_exp_out[l]), ln_ffn_g[l], ln_ffn_b[l])
        xs = layer_norm(ALPHA * xs + moe(xs, w_router, b_router, w_exp_in[l], w_exp_out[l]), ln_ffn_g[l], ln_ffn_b[l])
    y_prompt, y_sample = xp, xs
    new_conv_a_prompt, new_conv_a_sample = jnp.stack(ca_p), jnp.stack(ca_s)
    new_conv_b_prompt, new_conv_b_sample = jnp.stack(cb_p), jnp.stack(cb_s)
    new_h_prompt, new_h_sample = jnp.stack(h_p), jnp.stack(h_s)
    new_conv_c_prompt, new_conv_c_sample = jnp.stack(cc_p), jnp.stack(cc_s)
    new_ckv_prompt, new_ckv_sample = jnp.stack(ckv_p, axis=1), jnp.stack(ckv_s, axis=1)
    new_kpe_prompt, new_kpe_sample = jnp.stack(kpe_p, axis=1), jnp.stack(kpe_s, axis=1)
    return (y_prompt, y_sample, new_conv_a_prompt, new_conv_a_sample, new_conv_b_prompt, new_conv_b_sample,
            new_h_prompt, new_h_sample, new_conv_c_prompt, new_conv_c_sample, new_ckv_prompt, new_ckv_sample,
            new_kpe_prompt, new_kpe_sample)


_drawn_inputs = setup_inputs


def setup_inputs(seed=0):
    import zlib

    import numpy as np

    out = dict(_drawn_inputs(seed))
    spreads = {}
    factors = {'cache_ckv': 8.0,
     'cache_kpe': 8.0,
     'conv_c_b': 8.0,
     'ln_c_g': 81.261,
     'ln_c_b': 86.122,
     'q_norm_g': 8.0,
     'w_q_b': 4.096,
     'kv_norm_g': 2.993,
     'w_uk': 4.478,
     'w_uv': 3.233,
     'b_router': 4.326}
    for name, (base, spread) in spreads.items():
        noise = np.random.default_rng([zlib.crc32(name.encode()), seed]).standard_normal(out[name].shape)
        drawn = base * np.exp(spread * noise) if base else spread * noise
        out[name] = __import__('jax').numpy.asarray(drawn.astype(out[name].dtype))
    for name, factor in factors.items():
        out[name] = (out[name] * factor).astype(out[name].dtype)
    return out
```

```python
import contextlib

import numpy as np

import concourse.bass as bass
from concourse import mybir
from concourse.alu_op_type import AluOpType as ALU

F32 = mybir.dt.float32
I32 = mybir.dt.int32
U32 = mybir.dt.uint32
ACT = mybir.ActivationFunctionType
AX = mybir.AxisListType

P = 128
D = 1024
KD = D // P
PROMPT, SEQS, STEP = 1024, 8, 4
SAMPLE = SEQS * STEP
TOK = PROMPT + SAMPLE
NT = 9
TOKP = NT * P
NC, CW = 3, TOK // 3
TAIL = PROMPT - 2 * CW
ALPHA = 4.0 ** 0.25
EXPERTS, GROUPS, PER_GROUP = 16, 4, 4
F_EXP = 512
MAX_BLOCKS = 32
BIG = 1.0e30
HEADS, NOPE, ROPE, V_DIM = 8, 64, 32, 64
QK = NOPE + ROPE
QS = HEADS * STEP
Q_RANK, KV_RANK = 384, 256
SCALE = float(QK) ** -0.5
PAGE, PAST = 128, 4096
PAGES = PAST // PAGE
ROW = KV_RANK + ROPE
CONV_C = 31
OD_W, OD_B, OD_G, OD_LB, OD_S, OD_N = 0, 31, 32, 33, 34, 274
EV_CA, EV_CB, EV_BB, EV_BA, EV_BX, EV_LAM, EV_SA, EV_SB, EV_H0, EV_N = 0, 3, 7, 8, 9, 10, 11, 27, 51, 59
C_ID, C_ONE, C_TRI, C_IOTA, C_IOTA4, C_TOK, C_VALID, C_CAUSAL, C_NEW, C_FOLD, C_N = 0, 128, 256, 384, 400, 404, 413, 422, 550, 806, 838


class Steps:

    def __init__(self, eng, sem):
        self.eng, self.sem, self.base, self.n = eng, sem, 0, 0

    def __call__(self, ins):
        ins.then_inc(self.sem, 1)
        self.n += 1
        self.eng.wait_ge(self.sem, self.base + self.n)

    @contextlib.contextmanager
    def rounds(self, i, per, count):
        start = self.base + self.n
        self.base, self.n = start + i * per, 0
        yield
        assert self.n == per, f"{self.n} steps in a round, not {per}"
        self.base, self.n = start + count * per, 0


def build(nc, io):
    ctx = contextlib.ExitStack()
    with ctx:
        sems = {}

        def sem(name):
            if name not in sems:
                sems[name] = ctx.enter_context(nc.semaphore(name))
            return sems[name]

        def keep(name, shape, dt=F32):
            return ctx.enter_context(nc.sbuf_tensor(name, shape, dt))

        def phase(stack):
            return lambda name, shape, dt=F32: stack.enter_context(nc.sbuf_tensor(name, shape, dt))

        PS = ctx.enter_context(nc.psum_tensor("PS", [P, 8, 512], F32))

        xT = keep("xT", [P, KD, TOKP])
        yT = keep("yT", [P, KD, TOKP])
        cst = keep("cst", [P, C_N])
        ident, ones, tri = cst[:, C_ID:C_ID + P], cst[:, C_ONE:C_ONE + P], cst[:, C_TRI:C_TRI + P]
        wr = keep("wr", [P, KD, EXPERTS])
        brt = keep("brt", [P, EXPERTS])
        logits = keep("logits", [P, NT, EXPERTS])
        gate = keep("gate", [P, NT, 2])
        dest = keep("dest", [P, NT, 2], I32)
        plan = keep("plan", [P, 3 * EXPERTS + 1], I32)
        stat = keep("stat", [P, 2, 6])
        mv = keep("mv", [P, 2])
        rstd = keep("rstd", [P, 1])
        sd = keep("sd", [P, 1])
        epsc = keep("epsc", [P, 1])
        lng = keep("lng", [P, D])
        lnb = keep("lnb", [P, D])

        with contextlib.ExitStack() as st:
            sb = phase(st)
            W5 = sb("W5", [P, 5, KD, P])
            evp = sb("evp", [P, 4, EV_N])
            s8 = sb("s8", [P, 8, 4])
            lruw = sb("lruw", [P, 2, P])
            cbp, cbs = sb("cbp", [P, 3 + PROMPT]), sb("cbs", [P, SEQS, 3 + STEP])
            cap, cas = sb("cap", [P, 2 + PROMPT]), sb("cas", [P, SEQS, 2 + STEP])
            zC, zV, zB, zG = (sb(n, [P, TOK]) for n in ("zC", "zV", "zB", "zG"))
            ub, ua, rr, ii, aa, th, sq, hh = (sb(n, [P, TOK]) for n in ("ub", "ua", "rr", "ii", "aa", "th", "sq", "hh"))
            t1 = sb("t1", [P, TOK])
            h8 = sb("h8", [P, SEQS])
            evo = sb("evo", [P, 4, 54])
        odd = contextlib.ExitStack()
        sb = phase(odd)
        odp = sb("odp", [P, 4, OD_N])
        gqk = sb("gqk", [P, 5])
        eps6 = sb("eps6", [P, 1])
        wuv = sb("wuv", [P, 2, HEADS * V_DIM])
        ckvT = sb("ckvT", [P, 2, TOKP])
        peT = sb("peT", [P, 2, TOK])
        qns = sb("qns", [NOPE, HEADS, SAMPLE])
        kpeS = sb("kpeS", [ROPE, SAMPLE])
        pages = sb("pages", [1, SEQS * PAGES], I32)
        with contextlib.ExitStack() as st:
            sb = phase(st)
            qT = sb("qT", [P, 3, TOK])
            kraw = sb("kraw", [2 * ROPE, TOK])
            kpeT = sb("kpeT", [ROPE, TOK])
            cosq, sinq = sb("cosq", [P, TOK]), sb("sinq", [P, TOK])
            wqp, wqs = sb("wqp", [P, 3, 2 * P]), sb("wqs", [P, 3, 2 * P])
            sqb = sb("sqb", [P, 2, TOK])
            with contextlib.ExitStack() as st2:
                sb = phase(st2)
                W4 = sb("W4", [P, 4, KD, P])
                uc = yT[:, 4:8, 0:TOK]
                za, zs = sb("za", [P, TOK]), sb("zs", [P, TOK])
                hp, hs = sb("hp", [P, 2, CONV_C - 1 + PROMPT]), sb("hs", [P, 2, SEQS, CONV_C - 1 + STEP])
                hw = sb("hw", [P, STEP, SEQS, CONV_C])
                oso = sb("oso", [P, 4, (1 + SEQS) * 30])
            with contextlib.ExitStack() as st2:
                sb = phase(st2)
                wqn = sb("wqn", [P, 2, 3, P])
                wuk = sb("wuk", [P, 2, 2, P])
                V = sb("V", [P, 8, 2 * V_DIM])
                Q = [sb(f"Q{j}", [QK, TOK]) for j in range(2)]
                K = [sb(f"K{j}", [QK, PROMPT]) for j in range(2)]
                Pb = sb("Pb", [P, 2, PROMPT])
                PT = sb("PT", [P, 2, 8, P])
                nmax, nms, den, rden = (sb(n, [P, 2]) for n in ("nmax", "nms", "den", "rden"))
        with contextlib.ExitStack() as st:
            sb = phase(st)
            kv1, kpr = sb("kv1", [P, KD, TOKP]), sb("kpr", [P, 2, 4, 4, ROPE])
            CT, KT = sb("CT", [P, 2, 2, 512]), sb("KT", [P, 8, P])
            wukT = sb("wukT", [NOPE, HEADS, KV_RANK])
            qlat = sb("qlat", [P, 2, SEQS, QS])
            qpz = sb("qpz", [P, SEQS, 4, QS])
            qb, qpb = sb("qb", [P, 2, 2, QS]), sb("qpb", [P, 2, 4, QS])
            ckn = sb("ckn", [SAMPLE, KV_RANK])
            olat, olr = sb("olat", [P, 2, SEQS, QS]), sb("olr", [QS, KV_RANK])
            Pd, PTd = sb("Pd", [P, 2 * 512]), sb("PTd", [P, 8, P])
            Pn, PTn, sn = (sb(n, [QS, SAMPLE]) for n in ("Pn", "PTn", "sn"))
            mxa, mxd, nmd, dend = (sb(n, [P, 1]) for n in ("mxa", "mxd", "nmd", "dend"))
            mxn, denn, rdd = (sb(n, [QS, 1]) for n in ("mxn", "denn", "rdd"))
            mrow, m4 = sb("mrow", [1, QS]), sb("m4", [1, 4, QS])
        odd.close()
        with contextlib.ExitStack() as st:
            sb = phase(st)
            wo = sb("wo", [P, KD, D])
            yst = sb("yst", [P, 3, KD, P])
            xres = sb("xres", [P, 3, D])
            xn = sb("xn", [P, 3, D])
            sx = sb("sx", [P, D])
            xts = sb("xts", [P, KD, P])
            y1 = sb("y1", [P, 3, D])
            y2 = sb("y2", [P, 3, D])
            rt = [sb(f"rt{n}", [P, NT, EXPERTS]) for n in range(9)]
            rs = [sb(f"rs{n}", [P, NT, 4]) for n in range(6)]
            rk = [sb(f"rk{n}", [P, NT, 1]) for n in range(5)]
            cum = sb("cum", [P, NT + 1, EXPERTS])
            cnt = [sb(f"cnt{n}", [P, EXPERTS]) for n in range(4)]
            cnti = sb("cnti", [P, EXPERTS], I32)
            tokid = sb("tokid", [P, NT], I32)
            zid = sb("zid", [P, MAX_BLOCKS + 1], I32)
        with contextlib.ExitStack() as st:
            sb = phase(st)
            w1 = sb("w1", [P, 2, KD, 2 * F_EXP])
            w2 = sb("w2", [P, 2, F_EXP // P, D])
            gx = sb("gx", [P, D])
            idx = sb("idx", [P, 1], I32)
            xtb = sb("xtb", [P, KD, P])
            sg = sb("sg", [P, 4, P])
            ht = sb("ht", [P, 4, P])
            ysb = sb("ysb", [P, D])
            zrow = sb("zrow", [P, D])

        xm = [io["xm0"], io["xm1"]]
        tokbuf, yb = io["tokbuf"], io["yb"]
        block = ctx.enter_context(nc.Block())

        def part(eng):
            eng.sem_inc(sem("apart"), 1)

        def smp(x):
            return x[:, PROMPT:TOK].rearrange("p (b t) -> p b t", t=STEP)

        def mul_add(out, x, scalar, acc):
            return nc.vector.scalar_tensor_tensor(out, x, scalar, acc, ALU.mult, ALU.add)

        TT = nc.vector.tensor_tensor
        TS = nc.vector.tensor_scalar

        def sp_even(sp):
            w_in = io["w_in_even"].rearrange("(k p) n -> p k n", p=P)
            sp.dma_start(xT[:, 0:4, 0:TOK], io["xT0"].rearrange("(k p) t -> p k t", p=P)[:, 0:4, :]).then_inc(sem("in_xT"), 16)
            sp.dma_start(xT[:, 4:8, 0:TOK], io["xT0"].rearrange("(k p) t -> p k t", p=P)[:, 4:8, :]).then_inc(sem("in_xT"), 16)
            sp.wait_ge(sem("lru_zero"), 1)
            with sp.Fori(0, 4) as g:
                for p, j in enumerate((4, 1, 2, 0, 3)):
                    sp.wait_ge(sem("z_mm"), g * 15 + 3 * p)
                    part(sp)
                    sp.dma_start(W5[:, p, :, :], w_in[:, :, bass.ds(g * P + j * 512, P)]).then_inc(sem(f"in_w_{p}"), 16)
                    if p == 0:
                        sp.wait_ge(sem("lru_mm"), g * 6)
                        for n, w in enumerate(("lru_wa", "lru_wx")):
                            for h in range(2):
                                sp.dma_start(lruw[64 * h:64 * h + 64, n, 64 * h:64 * h + 64],
                                             io[w][bass.ds((g * 2 + h) * 64, 64), :]).then_inc(sem("in_lruw"), 16)

        def pe_even(pe):
            pe.sem_inc(sem("z_mm"), 12)
            pe.wait_ge(sem("in_xT"), 32)
            with pe.Fori(0, 4) as g:
                for p in range(5):
                    if p == 3:
                        pe.wait_ge(sem("ub_ready"), g + 1)
                        pe.wait_ge(sem("in_lruw"), g * 64 + 64)
                        for q in range(6):
                            pe.wait_ge(sem("lru_out"), g * 6 + q + 1)
                            nc.tensor.matmul(PS[:, 5 + q % 3, 0:CW], lruw[:, q % 2, :],
                                             ub[:, q // 2 * CW:(q // 2 + 1) * CW], start=True, stop=True
                                             ).then_inc(sem("lru_mm"), 1)
                    pe.wait_ge(sem(f"in_w_{p}"), g * 16 + 16)
                    for c in range(NC):
                        n = 3 * p + c
                        pe.wait_ge(sem("z_out"), g * 15 + n + 1)
                        for k in range(KD):
                            ins = nc.tensor.matmul(PS[:, n % 5, 0:CW], W5[:, p, k, :], xT[:, k, c * CW:(c + 1) * CW],
                                                   start=(k == 0), stop=(k == KD - 1))
                        ins.then_inc(sem("z_mm"), 1)

        def act_even(act, A):
            AC = nc.scalar.activation
            act.sem_inc(sem("z_out"), 5)
            act.sem_inc(sem("lru_out"), 3)
            act.wait_ge(sem("softplus_abs"), 1)
            AC(s8[:, 1, :], s8[:, 0, :], ACT.Exp, scale=-1.0).then_inc(sem("softplus_exp"), 1)

            def take(g, p, c, dst, fn, src=None):
                ins = AC(dst, PS[:, (3 * p + c) % 5, 0:CW] if src is None else src, fn)
                ins.then_inc(sem("z_out"), 1)

            with act.Fori(0, 4) as g, A.rounds(g, 4, 4):
                act.wait_ge(sem("states_kept"), g)
                for c in range(NC):
                    act.wait_ge(sem("z_mm"), g * 15 + 12 + c + 1)
                    if c < 2:
                        take(g, 0, c, cbp[:, 3 + c * CW:3 + (c + 1) * CW], ACT.Copy)
                A(AC(cbp[:, 3 + 2 * CW:3 + PROMPT], PS[:, 2, 0:TAIL], ACT.Copy))
                take(g, 0, 2, cbs[:, :, 3:7], ACT.Copy, PS[:, 2, TAIL:CW].rearrange("p (b t) -> p b t", t=STEP))
                A(AC(cbs[:, :, 0:3], evp[:, g, EV_SB:EV_H0].rearrange("p (b t) -> p b t", t=3), ACT.Copy))
                act.wait_ge(sem("z_out"), g * 15 + 5 + 3)
                part(act)
                A(AC(ub[:, 0:PROMPT], cbp[:, 0:PROMPT], ACT.Identity, bias=evp[:, g, EV_BB:EV_BB + 1], scale=evp[:, g, EV_CB:EV_CB + 1]))
                part(act)
                AC(smp(ub), cbs[:, :, 0:STEP], ACT.Identity, bias=evp[:, g, EV_BB:EV_BB + 1],
                   scale=evp[:, g, EV_CB:EV_CB + 1]).then_inc(sem("tap_ready"), 1)
                for p, dst in ((1, zC), (2, zV)):
                    for c in range(NC):
                        act.wait_ge(sem("z_mm"), g * 15 + 12 + 3 * p + c + 1)
                        take(g, p, c, dst[:, c * CW:(c + 1) * CW], ACT.Copy)
                for q in range(6):
                    act.wait_ge(sem("lru_mm"), g * 6 + q + 1)
                    part(act)
                    k = EV_BX if q % 2 else EV_BA
                    AC((ii if q % 2 else rr)[:, q // 2 * CW:(q // 2 + 1) * CW], PS[:, 5 + q % 3, 0:CW], ACT.Sigmoid,
                       bias=evp[:, g, k:k + 1]).then_inc(sem("lru_out"), 1)
                act.wait_ge(sem("lru_out"), g * 6 + 3 + 6)
                part(act)
                AC(th[:, :], rr[:, :], ACT.Tanh, scale=s8[:, 7, bass.ds(g, 1)]).then_inc(sem("th_ready"), 1)
                A(AC(aa[:, :], rr[:, :], ACT.Exp, scale=s8[:, 6, bass.ds(g, 1)]))
                for p, dst, fn in ((3, zB, ACT.Copy), (4, zG, ACT.Gelu_apprx_tanh)):
                    for c in range(NC):
                        act.wait_ge(sem("z_mm"), g * 15 + 12 + 3 * p + c + 1)
                        take(g, p, c, dst[:, c * CW:(c + 1) * CW], fn)
                act.wait_ge(sem("m_ready"), g + 1)
                AC(sq[:, :], th[:, :], ACT.Sqrt, scale=2.0).then_inc(sem("sq_ready"), 1)

        def dve_even(dve, D):
            D(nc.vector.memset(lruw[:, :, :], 0.0))
            dve.sem_inc(sem("lru_zero"), 1)
            D(nc.vector.memset(cbp[:, 0:3], 0.0))
            D(nc.vector.memset(cap[:, 0:2], 0.0))
            D(nc.vector.memset(yT[:, :, TOK:TOKP], 0.0))
            D(nc.vector.memset(epsc[:, :], 1e-5))
            dve.wait_ge(sem("in_const"), 64)
            lam = evp[:, :, EV_LAM]
            D(TS(s8[:, 2, :], lam, -1.0, None, ALU.mult))
            TT(s8[:, 0, :], s8[:, 2, :], lam, ALU.max).then_inc(sem("softplus_abs"), 1)
            dve.wait_ge(sem("softplus_exp"), 1)
            D(TS(s8[:, 3, :], s8[:, 1, :], 2.0, None, ALU.add))
            D(nc.vector.reciprocal(s8[:, 3, :], s8[:, 3, :]))
            D(TT(s8[:, 3, :], s8[:, 3, :], s8[:, 1, :], ALU.mult))
            D(TT(s8[:, 4, :], s8[:, 3, :], s8[:, 3, :], ALU.mult))
            D(TS(s8[:, 5, :], s8[:, 4, :], 1.0 / 15, 1.0 / 13, ALU.mult, ALU.add))
            for n in (11, 9, 7, 5, 3, 1):
                D(TT(s8[:, 5, :], s8[:, 5, :], s8[:, 4, :], ALU.mult))
                D(TS(s8[:, 5, :], s8[:, 5, :], 1.0 / n, None, ALU.add))
            D(TT(s8[:, 5, :], s8[:, 5, :], s8[:, 3, :], ALU.mult))
            D(TS(s8[:, 2, :], s8[:, 2, :], 0.0, 8.0, ALU.max, ALU.mult))
            D(mul_add(s8[:, 7, :], s8[:, 5, :], 16.0, s8[:, 2, :]))
            D(TS(s8[:, 6, :], s8[:, 7, :], -1.0, None, ALU.mult))
            dve.sem_inc(sem("softplus_done"), 1)
            PR = slice(0, PROMPT)
            with dve.Fori(0, 4) as g, D.rounds(g, 23, 4):
                def col(k):
                    return evp[:, g, k:k + 1]
                dve.wait_ge(sem("tap_ready"), g + 1)
                for k in range(1, 4):
                    D(mul_add(smp(ub), cbs[:, :, k:k + STEP], col(EV_CB + k), smp(ub)))
                    if k < 3:
                        D(mul_add(ub[:, PR], cbp[:, k:k + PROMPT], col(EV_CB + k), ub[:, PR]))
                mul_add(ub[:, PR], cbp[:, 3:3 + PROMPT], col(EV_CB + 3), ub[:, PR]).then_inc(sem("ub_ready"), 1)
                dve.wait_ge(sem("z_out"), g * 15 + 5 + 9)
                dve.wait_ge(sem("states_kept"), g)
                D(nc.vector.tensor_copy(cas[:, :, 0:2], evp[:, g, EV_SA:EV_SB].rearrange("p (b t) -> p b t", t=2)))
                D(TT(cas[:, :, 2:6], smp(zC), smp(zV), ALU.mult))
                D(TT(cap[:, 2:2 + PROMPT], zC[:, PR], zV[:, PR], ALU.mult))
                D(TS(ua[:, PR], cap[:, 0:PROMPT], col(EV_CA), None, ALU.mult))
                D(TS(smp(ua), cas[:, :, 0:STEP], col(EV_CA), None, ALU.mult))
                for k in range(1, 3):
                    D(mul_add(ua[:, PR], cap[:, k:k + PROMPT], col(EV_CA + k), ua[:, PR]))
                    D(mul_add(smp(ua), cas[:, :, k:k + STEP], col(EV_CA + k), smp(ua)))
                dve.wait_ge(sem("th_ready"), g + 1)
                D(TS(t1[:, :], th[:, :], 1.0, None, ALU.add))
                D(nc.vector.reciprocal(t1[:, :], t1[:, :]))
                TT(th[:, :], th[:, :], t1[:, :], ALU.mult).then_inc(sem("m_ready"), 1)
                D(TT(ii[:, :], ii[:, :], ub[:, :], ALU.mult))
                dve.wait_ge(sem("z_out"), g * 15 + 5 + 12)
                D(TT(yT[:, g, 0:TOK], ua[:, :], zB[:, :], ALU.mult))
                dve.wait_ge(sem("sq_ready"), g + 1)
                D(TT(t1[:, :], sq[:, :], ii[:, :], ALU.mult))
                D(TT(h8[:, :], smp(aa)[:, :, 0], evp[:, g, EV_H0:EV_N], ALU.mult))
                D(TT(smp(t1)[:, :, 0], smp(t1)[:, :, 0], h8[:, :], ALU.add))
                D(nc.vector.memset(smp(aa)[:, :, 0], 0.0))
                D(nc.vector.tensor_tensor_scan(hh[:, :], aa[:, :], t1[:, :], 0.0, ALU.mult, ALU.add))
                TT(yT[:, g + 4, 0:TOK], zG[:, :], hh[:, :], ALU.mult).then_inc(sem("yb_done"), 1)

        def pool_even(pool, G):
            CP = nc.gpsimd.tensor_copy
            with pool.Fori(0, 4) as g, G.rounds(g, 5, 4):
                pool.wait_ge(sem("yb_done"), g + 1)
                G(CP(evo[:, g, 0:2], cap[:, PROMPT:PROMPT + 2]))
                G(CP(evo[:, g, 2:18].rearrange("p (b t) -> p b t", t=2), cas[:, :, STEP:STEP + 2]))
                G(CP(evo[:, g, 18:21], cbp[:, PROMPT:PROMPT + 3]))
                G(CP(evo[:, g, 21:45].rearrange("p (b t) -> p b t", t=3), cbs[:, :, STEP:STEP + 3]))
                G(CP(evo[:, g, 45:46], hh[:, PROMPT - 1:PROMPT]))
                CP(evo[:, g, 46:54], smp(hh)[:, :, STEP - 1]).then_inc(sem("states_kept"), 1)
            pool.wait_ge(sem("states_kept"), 4)
            pool.dma_start(io["even_states"], evo[:, :, :]).then_inc(sem("out_states"), 16)
            pool.wait_ge(sem("out_states"), 16)

        def rows(t):
            return bass.ds(t * P, P)

        def sp_mix(sp, l):
            u = f"m{l}_"
            x = io["xtok"] if l == 0 else io["x1"]
            wout = io["w_out_even" if l == 0 else "w_out_odd"].rearrange("(k p) n -> p k n", p=P)
            for n in range(2):
                sp.dma_start(wo[:, :, n * 512:(n + 1) * 512], wout[:, :, n * 512:(n + 1) * 512]).then_inc(sem("n_in_w"), 16)
            sp.dma_start(lng[:], io["ln_mix_g"][l, :].partition_broadcast(P)).then_inc(sem("n_in_w"), 16)
            sp.dma_start(lnb[:], io["ln_mix_b"][l, :].partition_broadcast(P)).then_inc(sem("n_in_w"), 16)
            for s in range(3):
                sp.dma_start(xres[:, s, :], x[rows(s), :]).then_inc(sem(f"n_in_x{s}"), 16)

            def store(t, s):
                sp.wait_ge(sem("n_ln"), 18 * l + t + 1)
                sp.dma_start(xm[l][rows(t), :], xn[:, s, :]).then_inc(sem(f"n_out{s}"), 16)

            with sp.Fori(0, 2) as i:
                for s in range(3):
                    store(i * 3 + s, s)
                    sp.dma_start(xres[:, s, :], x[rows(i * 3 + s + 3), :]).then_inc(sem(f"n_in_x{s}"), 16)
            for s in range(3):
                store(6 + s, s)
            for s in range(3):
                sp.wait_ge(sem(f"n_out{s}"), 96 * l + 48)
            sp.sem_inc(sem("m_kept"), 1)

        def pool_mix(pool, l):
            u = f"m{l}_"
            with pool.Fori(0, 3) as i:
                for s in range(3):
                    t = i * 3 + s
                    pool.wait_ge(sem("m_mm"), 9 * l + t + 1)
                    nc.gpsimd.tensor_copy(yst[:, s, :, :], yT[:, :, rows(t)]).then_inc(sem("m_st"), 1)

        def pe_transpose(src):
            for k in range(KD):
                ins = nc.tensor.transpose(PS[:, 4 + k // 4, k % 4 * P:k % 4 * P + P], src[:, k * P:(k + 1) * P], ident)
            ins.then_inc(sem("n_tp"), 1)

        def pe_mix(pe, l):
            u = f"m{l}_"
            if l == 0:
                pe.sem_inc(sem("m_mm"), 3)
            pe.wait_ge(sem("n_in_w"), 96 * l + 64)

            def multiply(t, s):
                pe.wait_ge(sem("m_st"), 9 * l + t + 1)
                pe.wait_ge(sem("m_ps"), 9 * l + t + 1)
                for n in range(2):
                    for k in range(KD):
                        ins = nc.tensor.matmul(PS[:, (t % 2) * 2 + n, :], yst[:, s, k, :], wo[:, k, n * 512:(n + 1) * 512],
                                               start=(k == 0), stop=(k == KD - 1))
                ins.then_inc(sem("m_mm"), 1)

            def post(t, s):
                pe.wait_ge(sem("n_ln"), 18 * l + t + 1)
                pe.wait_ge(sem("n_tpo"), 18 * l + t)
                pe_transpose(xn[:, s, :])
                pe.wait_ge(sem("n_tpo"), 18 * l + t + 1)
                pe.wait_ge(sem("m_lg"), 9 * l + t)
                for k in range(KD):
                    ins = nc.tensor.matmul(PS[:, 6, 0:EXPERTS], xts[:, k, :], wr[:, k, :], start=(k == 0), stop=(k == KD - 1))
                ins.then_inc(sem("m_rm"), 1)

            multiply(0, 0)
            with pe.Fori(0, 2) as i:
                for s in range(3):
                    multiply(i * 3 + s + 1, (s + 1) % 3)
                    post(i * 3 + s, s)
            for t in (6, 7):
                multiply(t + 1, (t + 1) % 3)
                post(t, t % 3)
            post(8, 2)

        def act_mix(act, l):
            u = f"m{l}_"
            with act.Fori(0, NT) as t:
                act.wait_ge(sem("n_var"), 18 * l + t + 1)
                nc.scalar.activation(sd[:, :], mv[:, 1:2], ACT.Sqrt, bias=epsc[:, :]).then_inc(sem("n_sd"), 1)
                act.wait_ge(sem("n_tp"), 18 * l + t + 1)
                nc.scalar.activation(xts[:, :, :].rearrange("p (a b) c -> p a (b c)", a=2), PS[:, 4:6, :], ACT.Copy).then_inc(sem("n_tpo"), 1)
                act.wait_ge(sem("m_rm"), 9 * l + t + 1)
                part(act)
                nc.scalar.activation(logits[:, t, :], PS[:, 6, 0:EXPERTS], ACT.Copy).then_inc(sem("m_lg"), 1)

        def normalize(dve, D, n, s):
            for h in range(2):
                D(nc.vector.bn_stats(stat[:, h, :], sx[:, h * 512:(h + 1) * 512]))
            part(dve)
            nc.vector.bn_aggr(mv[:, :], stat[:, :, :].rearrange("p a b -> p (a b)")).then_inc(sem("n_var"), 1)
            dve.wait_ge(sem("n_sd"), n + 1)
            D(nc.vector.reciprocal(rstd[:, :], sd[:, :]))
            D(TS(xn[:, s, :], sx[:, :], mv[:, 0:1], rstd[:, :], ALU.subtract, ALU.mult))
            D(TT(xn[:, s, :], xn[:, s, :], lng[:, :], ALU.mult))
            TT(xn[:, s, :], xn[:, s, :], lnb[:, :], ALU.add).then_inc(sem("n_ln"), 1)

        def dve_mix(dve, D, l):
            u = f"m{l}_"
            if l == 0:
                dve.sem_inc(sem("m_ps"), 2)
            dve.wait_ge(sem("n_in_w"), 96 * l + 64)
            with dve.Fori(0, 3) as i, D.rounds(i, 15, 3):
                for s in range(3):
                    t = i * 3 + s
                    dve.wait_ge(sem(f"n_in_x{s}"), 96 * l + i * 16 + 16)
                    dve.wait_ge(sem("m_mm"), 9 * l + t + 3 + 1)
                    v = xres[:, s, :].rearrange("p (a b) -> p a b", a=2)
                    nc.vector.scalar_tensor_tensor(sx[:, :].rearrange("p (a b) -> p a b", a=2), v, ALPHA,
                                                   PS[:, bass.ds((t % 2) * 2, 2), :], ALU.mult, ALU.add).then_inc(sem("m_ps"), 1)
                    dve.wait_ge(sem("m_ps"), 9 * l + t + 2 + 1)
                    dve.wait_ge(sem(f"n_out{s}"), 96 * l + i * 16)
                    normalize(dve, D, 18 * l + t, s)

        def wide(x, n):
            return x.unsqueeze(len(x.shape)).broadcast_to(list(x.shape) + [n])

        def dve_route(dve, D, l):
            sc, sel, m, eq, oh1, oh2, A, pos, tmp = rt
            TR = nc.vector.tensor_reduce
            dve.wait_ge(sem("r_sig"), l + 1)
            D(TT(sel[:, :, :], sc[:, :, :], brt[:, :].unsqueeze(1).broadcast_to([P, NT, EXPERTS]), ALU.add))
            q = sel[:, :, :].rearrange("p t (g e) -> p (t g) e", e=PER_GROUP)
            r = [x[:, :, :].rearrange("p t g -> p (t g)") for x in rs]
            D(TT(r[0], q[:, :, 0], q[:, :, 1], ALU.max))
            D(TT(r[1], q[:, :, 0], q[:, :, 1], ALU.min))
            D(TT(r[2], q[:, :, 2], q[:, :, 3], ALU.max))
            D(TT(r[3], q[:, :, 2], q[:, :, 3], ALU.min))
            D(TT(r[4], r[0], r[2], ALU.max))
            D(TT(r[0], r[0], r[2], ALU.min))
            D(TT(r[1], r[1], r[3], ALU.max))
            D(TT(r[0], r[0], r[1], ALU.max))
            D(TT(rs[4][:, :, :], rs[4][:, :, :], rs[0][:, :, :], ALU.add))

            def first_max(dst, x, iota, n, work):
                D(TR(rk[0][:, :, :], x, AX.X, ALU.max))
                D(TT(dst, x, rk[0][:, :, 0:1].broadcast_to([P, NT, n]), ALU.is_equal))
                D(TT(work, dst, iota.unsqueeze(1).broadcast_to([P, NT, n]), ALU.mult))
                D(TR(rk[1][:, :, :], work, AX.X, ALU.max))
                D(TT(dst, work, rk[1][:, :, 0:1].broadcast_to([P, NT, n]), ALU.is_equal))

            i4, i16 = cst[:, C_IOTA4:C_IOTA4 + 4], cst[:, C_IOTA:C_IOTA + 16]
            first_max(rs[1][:, :, :], rs[4][:, :, :], i4, 4, rs[2][:, :, :])
            D(TS(rs[3][:, :, :], rs[1][:, :, :], 1.0, BIG, ALU.subtract, ALU.mult))
            mq = m[:, :, :].rearrange("p t (g e) -> p (t g) e", e=PER_GROUP)
            D(TT(mq, q, wide(r[1], PER_GROUP), ALU.mult))
            D(TT(mq, mq, wide(r[3], PER_GROUP), ALU.add))
            first_max(oh1[:, :, :], m[:, :, :], i16, 16, eq[:, :, :])
            D(mul_add(m[:, :, :], oh1[:, :, :], -3.0 * BIG, m[:, :, :]))
            first_max(oh2[:, :, :], m[:, :, :], i16, 16, eq[:, :, :])
            for k, oh in enumerate((oh1, oh2)):
                D(TT(eq[:, :, :], sc[:, :, :], oh[:, :, :], ALU.mult))
                D(TR(rk[2 + k][:, :, :], eq[:, :, :], AX.X, ALU.add))
            D(TT(rk[4][:, :, :], rk[2][:, :, :], rk[3][:, :, :], ALU.add))
            D(nc.vector.reciprocal(rk[4][:, :, :], rk[4][:, :, :]))
            for k in range(2):
                D(TT(gate[:, :, k:k + 1], rk[2 + k][:, :, :], rk[4][:, :, :], ALU.mult))
            for oh in (oh1, oh2):
                D(TT(oh[:, :, :], oh[:, :, :], wide(cst[:, C_VALID:C_VALID + NT], EXPERTS), ALU.mult))
            TT(A[:, :, :], oh1[:, :, :], oh2[:, :, :], ALU.add).then_inc(sem("r_chosen"), 1)
            dve.wait_ge(sem("r_count"), l + 1)
            D(nc.vector.memset(cum[:, 0, :], 0.0))
            for t in range(NT):
                D(TT(cum[:, t + 1, :], cum[:, t, :], PS[:, 1, t * EXPERTS:(t + 1) * EXPERTS], ALU.add))
            D(TS(cnti[:, :], cum[:, NT, :], 127.0, None, ALU.add))
            D(TS(cnti[:, :], cnti[:, :], 7, None, ALU.logical_shift_right))
            D(nc.vector.tensor_copy(cnt[0][:, :], cnti[:, :]))
            D(TS(cnt[1][:, :], cnt[0][:, :], 1.0, None, ALU.max))
            D(nc.vector.tensor_tensor_scan(cnt[2][:, :], cst[:, C_ONE:C_ONE + EXPERTS], cnt[1][:, :], 0.0, ALU.mult, ALU.add))
            D(TT(cnt[3][:, :], cnt[2][:, :], cnt[1][:, :], ALU.subtract))
            D(nc.vector.tensor_copy(plan[:, 0:16], cnt[1][:, :]))
            D(nc.vector.tensor_copy(plan[:, 16:32], cnt[3][:, :]))
            D(nc.vector.tensor_copy(plan[:, 32:48], cnt[2][:, :]))
            D(TS(cnt[0][:, :], cnt[2][:, :], -1.0, MAX_BLOCKS + 1.0, ALU.mult, ALU.add))
            D(nc.vector.tensor_copy(plan[:, 48:49], cnt[0][:, EXPERTS - 1:EXPERTS]))
            D(TT(pos[:, :, :], cum[:, 0:NT, :], PS[:, 0, 0:NT * EXPERTS].rearrange("p (t e) -> p t e", e=EXPERTS), ALU.add))
            D(TS(cnt[0][:, :], cnt[3][:, :], 128.0, None, ALU.mult))
            D(TT(pos[:, :, :], pos[:, :, :], cnt[0][:, :].unsqueeze(1).broadcast_to([P, NT, EXPERTS]), ALU.add))
            for k, oh in enumerate((oh1, oh2)):
                D(TT(tmp[:, :, :], pos[:, :, :], oh[:, :, :], ALU.mult))
                D(TR(rk[k][:, :, :], tmp[:, :, :], AX.X, ALU.add))
                D(nc.vector.tensor_copy(dest[:, :, k:k + 1], rk[k][:, :, :]))
            D(nc.vector.tensor_copy(tokid[:, :], cst[:, C_TOK:C_TOK + NT]))
            dve.sem_inc(sem("r_plan"), 1)

        def act_route(act, A, l):
            act.wait_ge(sem("m_lg"), 9 * l + NT)
            nc.scalar.activation(rt[0][:, :, :], logits[:, :, :], ACT.Sigmoid).then_inc(sem("r_sig"), 1)

        def pe_route(pe, l):
            pe.wait_ge(sem("r_chosen"), l + 1)
            a = rt[6][:, :, :].rearrange("p t e -> p (t e)")
            nc.tensor.matmul(PS[:, 0, 0:NT * EXPERTS], tri, a, start=True, stop=True)
            nc.tensor.matmul(PS[:, 1, 0:NT * EXPERTS], ones, a, start=True, stop=True).then_inc(sem("r_count"), 1)

        def pool_route(pool, G, l):
            if l == 0:
                G(nc.gpsimd.memset(zid[:, :], 0))
                pool.dma_start(tokbuf.rearrange("(p n) a -> p (n a)", p=P), zid[:, :]).then_inc(sem("r_zeroed"), 16)
                pool.wait_ge(sem("r_zeroed"), 16)
            pool.wait_ge(sem("r_plan"), l + 1)
            for t in range(NT):
                n = P if t < NT - 1 else SAMPLE
                for k in range(2):
                    pool.indirect_dma_start(out=tokbuf, out_offset=bass.IndirectOffsetOnAxis(ap=dest[0:n, t, k:k + 1].bitcast(U32), axis=0),
                                            in_=tokid[0:n, t:t + 1], in_offset=None).then_inc(sem("r_rows"), 16)
            pool.wait_ge(sem("r_rows"), (l + 1) * 16 * 2 * NT)

        def expert_loop(eng, l, body, end=None):
            with eng.Fori(0, EXPERTS // 2) as i:
                for s in range(2):
                    e = i * 2 + s
                    n = eng.value_load(plan[0:1, bass.ds(e, 1)], min_val=1, max_val=NT)
                    b0 = eng.value_load(plan[0:1, bass.ds(e + EXPERTS, 1)], min_val=0, max_val=MAX_BLOCKS - 1)
                    if body_start := body.get("start"):
                        body_start(i, s)
                    with eng.Fori(0, n) as j:
                        b = nc.s_assert_within(b0 + j, 0, MAX_BLOCKS - 1, skip_runtime_bounds_check_because="first block plus count is at most the total")
                        body["block"](s, b)
                    if body_end := body.get("end"):
                        body_end(i, s, b0 + n)

        def sp_experts(sp, l):
            u = f"e{l}_"
            w1d = io["w_exp_in"].rearrange("(e k p) n -> p e k n", p=P, k=KD)
            w2d = io["w_exp_out"].rearrange("(e k p) n -> p e k n", p=P, k=F_EXP // P)
            with sp.Fori(0, EXPERTS // 2) as i:
                for s in range(2):
                    sp.wait_ge(sem("e_free"), EXPERTS * l + i * 2 + s + 1)
                    e = i * 2 + s + l * EXPERTS
                    for h in range(2):
                        sp.dma_start(w1[:, s, h * 4:h * 4 + 4, :], w1d[:, e, h * 4:h * 4 + 4, :]).then_inc(sem(f"e_in_w1_{s}"), 16)
                    sp.dma_start(w2[:, s, :, :], w2d[:, e, :, :]).then_inc(sem(f"e_in_w2_{s}"), 16)

        def pool_experts(pool, l):
            u = f"e{l}_"
            pool.wait_ge(sem("m_kept"), l + 1)
            total = pool.value_load(plan[0:1, 47:48], min_val=EXPERTS, max_val=MAX_BLOCKS)
            with pool.Fori(0, total + 1) as b:
                pool.dma_start(idx[:, :], tokbuf[rows(b), :]).then_inc(sem(u + "idx"), 16)
                pool.wait_ge(sem(u + "idx"), b * 16 + 16)
                pool.wait_ge(sem(u + "tp"), b)
                part(pool)
                pool.indirect_dma_start(out=gx[:, :], out_offset=None, in_=xm[l],
                                        in_offset=bass.IndirectOffsetOnAxis(ap=idx[:, 0:1].bitcast(U32), axis=0)
                                        ).then_inc(sem(u + "gx"), 16)
                pool.wait_ge(sem(u + "gx"), b * 16 + 16)
                part(pool)
            if l == 0:
                nc.gpsimd.memset(zrow[:, :], 0.0).then_inc(sem("zrow"), 1)
                pool.wait_ge(sem("zrow"), 1)
                rest = pool.value_load(plan[0:1, 48:49], min_val=1, max_val=MAX_BLOCKS + 1 - EXPERTS)
                with pool.Fori(0, rest) as n:
                    b = nc.s_assert_within(total + n, 0, MAX_BLOCKS, skip_runtime_bounds_check_because="total and rest are MAX_BLOCKS + 1")
                    pool.dma_start(yb[rows(b), :], zrow[:, :]).then_inc(sem("yb_rest"), 16)
                    pool.wait_ge(sem("yb_rest"), n * 16 + 16)
                    part(pool)

        def pe_experts(pe, l):
            u = f"e{l}_"
            pe.wait_ge(sem("r_plan"), l + 1)

            def transpose(b):
                pe.wait_ge(sem(u + "gx"), b * 16 + 16)
                pe.wait_ge(sem(u + "xtb"), b)
                for k in range(KD):
                    ins = nc.tensor.transpose(PS[:, k // 4, k % 4 * P:k % 4 * P + P], gx[:, k * P:(k + 1) * P], ident)
                ins.then_inc(sem(u + "tp"), 1)

            transpose(0)

            def start(i, s):
                pe.wait_ge(sem(f"e_in_w1_{s}"), 256 * l + i * 32 + 32)
                pe.wait_ge(sem(f"e_in_w2_{s}"), 128 * l + i * 16 + 16)
                part(pe)

            def block_(s, b):
                pe.wait_ge(sem(u + "xtb"), b + 1)
                for f in range(4):
                    pe.wait_ge(sem(u + "ht"), b * 4 + f + 1)
                    for half in range(2):
                        for k in range(KD):
                            c = half * F_EXP + f * P
                            ins = nc.tensor.matmul(PS[:, 2 + f % 2, half * P:(half + 1) * P], w1[:, s, k, c:c + P], xtb[:, k, :],
                                                   start=(k == 0), stop=(k == KD - 1))
                    ins.then_inc(sem(u + "h"), 1)
                transpose(b + 1)
                pe.wait_ge(sem(u + "y_out"), b)
                for f in range(4):
                    pe.wait_ge(sem(u + "ht"), b * 4 + f + 1 + 2)
                    for n in range(2):
                        ins = nc.tensor.matmul(PS[:, 4 + n, :], ht[:, f, :], w2[:, s, f, n * 512:(n + 1) * 512],
                                               start=(f == 0), stop=(f == 3))
                ins.then_inc(sem(u + "y"), 1)

            expert_loop(pe, l, {"start": start, "block": block_})

        def act_experts(act, l):
            u = f"e{l}_"
            if l == 0:
                act.sem_inc(sem("e_free"), 2)
            act.wait_ge(sem("r_plan"), l + 1)

            def stage(b):
                act.wait_ge(sem(u + "tp"), b + 1)
                nc.scalar.activation(xtb[:, :, :].rearrange("p (a b) c -> p a (b c)", a=2), PS[:, 0:2, :], ACT.Copy).then_inc(sem(u + "xtb"), 1)

            stage(0)

            def block_(s, b):
                for f in range(4):
                    act.wait_ge(sem(u + "h"), b * 4 + f + 1)
                    nc.scalar.activation(sg[:, f, :], PS[:, 2 + f % 2, 0:P], ACT.Silu).then_inc(sem(u + "sg"), 1)
                stage(b + 1)
                act.wait_ge(sem(u + "y_out"), b + 1)
                act.dma_start(yb[rows(b), :], ysb[:, :]).then_inc(sem(u + "yb"), 16)

            def end(i, s, blocks):
                act.sem_inc(sem("e_free"), 1)

            expert_loop(act, l, {"block": block_, "end": end})

        def dve_experts(dve, l):
            u = f"e{l}_"
            dve.sem_inc(sem(u + "ht"), 2)

            def block_(s, b):
                for f in range(4):
                    dve.wait_ge(sem(u + "sg"), b * 4 + f + 1)
                    TT(ht[:, f, :], sg[:, f, :], PS[:, 2 + f % 2, P:2 * P], ALU.mult).then_inc(sem(u + "ht"), 1)
                dve.wait_ge(sem(u + "y"), b + 1)
                dve.wait_ge(sem(u + "yb"), b * 16)
                nc.vector.tensor_copy(ysb[:, :].rearrange("p (a b) -> p a b", a=2), PS[:, 4:6, :]).then_inc(sem(u + "y_out"), 1)

            expert_loop(dve, l, {"block": block_})

        def sp_ffn(sp, l):
            u = f"f{l}_"
            out = io["x1"] if l == 0 else io["y"]
            total = sp.value_load(plan[0:1, 47:48], min_val=EXPERTS, max_val=MAX_BLOCKS)
            sp.wait_ge(sem(f"e{l}_yb"), total * 16)
            part(sp)
            sp.dma_start(lng[:], io["ln_ffn_g"][l, :].partition_broadcast(P)).then_inc(sem("n_in_w"), 16)
            sp.dma_start(lnb[:], io["ln_ffn_b"][l, :].partition_broadcast(P)).then_inc(sem("n_in_w"), 16)
            for s in range(3):
                sp.dma_start(xres[:, s, :], xm[l][rows(s), :]).then_inc(sem(f"n_in_x{s}"), 16)

            def store(t, s):
                sp.wait_ge(sem("n_ln"), 18 * l + 9 + t + 1)
                sp.dma_start(out[rows(t), :], xn[:, s, :]).then_inc(sem(f"n_out{s}"), 16)

            with sp.Fori(0, 2) as i:
                for s in range(3):
                    store(i * 3 + s, s)
                    sp.dma_start(xres[:, s, :], xm[l][rows(i * 3 + s + 3), :]).then_inc(sem(f"n_in_x{s}"), 16)
            for s in range(3):
                store(6 + s, s)
            for s in range(3):
                sp.wait_ge(sem(f"n_out{s}"), 96 * l + 96)

        def pool_ffn(pool, l):
            u = f"f{l}_"
            total = pool.value_load(plan[0:1, 47:48], min_val=EXPERTS, max_val=MAX_BLOCKS)
            pool.wait_ge(sem(f"e{l}_yb"), total * 16)
            part(pool)
            for t in range(NT):
                if t >= 3:
                    pool.wait_ge(sem("n_ln"), 18 * l + 9 + t - 2)
                for k, dst in enumerate((y1, y2)):
                    pool.indirect_dma_start(out=dst[:, t % 3, :], out_offset=None, in_=yb,
                                            in_offset=bass.IndirectOffsetOnAxis(ap=dest[:, t, k:k + 1].bitcast(U32), axis=0)
                                            ).then_inc(sem(f"f_g{t % 3}"), 16)

        def pe_ffn(pe, l):
            u = f"f{l}_"
            if l == 0:
                with pe.Fori(0, 3) as i:
                    for s in range(3):
                        t = i * 3 + s
                        pe.wait_ge(sem("n_ln"), 18 * l + 9 + t + 1)
                        pe.wait_ge(sem("n_tpo"), 9 + t)
                        pe_transpose(xn[:, s, :])

        def act_ffn(act, l):
            u = f"f{l}_"
            with act.Fori(0, NT) as t:
                act.wait_ge(sem("n_var"), 18 * l + 9 + t + 1)
                nc.scalar.activation(sd[:, :], mv[:, 1:2], ACT.Sqrt, bias=epsc[:, :]).then_inc(sem("n_sd"), 1)
                if l == 0:
                    act.wait_ge(sem("n_tp"), 9 + t + 1)
                    part(act)
                    nc.scalar.activation(xT[:, :, rows(t)], PS[:, 4:6, :].rearrange("p a (b c) -> p (a b) c", c=P), ACT.Copy).then_inc(sem("n_tpo"), 1)

        def dve_ffn(dve, D, l):
            u = f"f{l}_"
            dve.wait_ge(sem("n_in_w"), 96 * l + 96)
            with dve.Fori(0, 3) as i, D.rounds(i, 24, 3):
                for s in range(3):
                    t = i * 3 + s
                    dve.wait_ge(sem(f"f_g{s}"), 96 * l + i * 32 + 32)
                    D(TS(sx[:, :], y1[:, s, :], gate[:, t, 0:1], None, ALU.mult))
                    D(mul_add(sx[:, :], y2[:, s, :], gate[:, t, 1:2], sx[:, :]))
                    dve.wait_ge(sem(f"n_in_x{s}"), 96 * l + 48 + i * 16 + 16)
                    D(mul_add(sx[:, :], xres[:, s, :], ALPHA, sx[:, :]))
                    dve.wait_ge(sem(f"n_out{s}"), 96 * l + 48 + i * 16)
                    if l == 0:
                        dve.wait_ge(sem("n_tpo"), 9 + i * 3)
                    normalize(dve, D, 18 * l + 9 + t, s)


        def sp_odd(sp):
            w_in = io["w_in_odd"].rearrange("(k p) n -> p k n", p=P)
            for dst, src in ((odp[:], io["od_pack"]), (gqk[:], io["gqk"]), (cosq[:], io["cosq"]), (sinq[:], io["sinq"]),
                             (wqp[:], io["wqp"].rearrange("(k p) n -> p k n", p=P)), (wqs[:], io["wqs"].rearrange("(k p) n -> p k n", p=P)),
                             (wuv[:], io["wuv"].rearrange("(k p) n -> p k n", p=P)), (pages[:], io["page_table"])):
                sp.dma_start(dst, src).then_inc(sem("in_odd"), 16)
            with sp.Fori(0, 2) as i:
                for s in range(2):
                    for p in range(2):
                        sp.wait_ge(sem("o_mm"), i * 12 + s * 6 + p * 3)
                        part(sp)
                        sp.dma_start(W4[:, 2 * s + p, :, :], w_in[:, :, bass.ds(i * 2 * P + s * P + (1 - p) * 512, P)]
                                     ).then_inc(sem(f"in_w_{2 * s + p}"), 16)
            for q in range(6):
                sp.wait_ge(sem("o_mm"), 24 + 3 * q)
                src = w_in[:, :, 1024 + q * P:1024 + (q + 1) * P] if q < 5 else io["w_kpe"].rearrange("(k p) n -> p k n", p=P)
                sp.dma_start(W4[:, q % 4, :, 0:P if q < 5 else 2 * ROPE], src).then_inc(sem(f"in_w_{q % 4}"), 16)

        def pe_odd(pe):
            pe.sem_inc(sem("o_mm"), 9)
            pe.wait_ge(sem("n_tpo"), 2 * NT)

            def chunks(slot, n0, m=P, before=0):
                for c in range(NC):
                    pe.wait_ge(sem("o_out"), before + n0 + c + 1)
                    for k in range(KD):
                        ins = nc.tensor.matmul(PS[0:m, (n0 + c) % 6, 0:CW], W4[:, slot, k, 0:m], xT[:, k, c * CW:(c + 1) * CW],
                                               start=(k == 0), stop=(k == KD - 1))
                    ins.then_inc(sem("o_mm"), 1)

            with pe.Fori(0, 2) as i:
                for slot in range(4):
                    pe.wait_ge(sem(f"in_w_{slot}"), 64 + i * 16 + 16)
                    part(pe)
                    chunks(slot, 3 * slot, before=i * 12)
            for q in range(6):
                pe.wait_ge(sem(f"in_w_{q % 4}"), 64 + 48 + 16 * (q // 4))
                chunks(q % 4, 24 + 3 * q, P if q < 5 else 2 * ROPE)
            for q in range(5):
                pe.wait_ge(sem("o_sq"), q + 1)
                for c in range(NC):
                    ins = nc.tensor.matmul(PS[:, (0 if q < 3 else 3) + c, 0:CW], ones, sqb[:, q % 2, c * CW:(c + 1) * CW],
                                           start=(q in (0, 3)), stop=(q in (2, 4)))
                ins.then_inc(sem("o_ss"), 1)
            pe.wait_ge(sem("o_conv"), 5)
            pe.wait_ge(sem("o_rms"), 2)
            for g in range(4):
                for c in range(NC):
                    ins = nc.tensor.matmul(PS[:, c, 0:CW], ones, uc[:, g, c * CW:(c + 1) * CW], start=(g == 0), stop=(g == 3))
            ins.then_inc(sem("o_ss"), 1)
            for g in range(4):
                pe.wait_ge(sem("o_sq"), 5 + g + 1)
                for c in range(NC):
                    ins = nc.tensor.matmul(PS[:, 3 + c, 0:CW], ones, sqb[:, g % 2, c * CW:(c + 1) * CW], start=(g == 0), stop=(g == 3))
                ins.then_inc(sem("o_ss"), 1)

        def act_odd(act, A):
            AC = nc.scalar.activation
            act.sem_inc(sem("o_out"), 6)
            with act.Fori(0, 4) as g:
                act.wait_ge(sem("o_prod"), g)
                for p, dst, fn in ((0, zs, ACT.Sigmoid), (1, za, ACT.Copy)):
                    for c in range(NC):
                        act.wait_ge(sem("o_mm"), g * 6 + 9 + 3 * p + c + 1)
                        AC(dst[:, c * CW:(c + 1) * CW], PS[:, 3 * p + c, 0:CW], fn).then_inc(sem("o_out"), 1)
            for q in range(6):
                for c in range(NC):
                    cc = slice(c * CW, (c + 1) * CW)
                    act.wait_ge(sem("o_mm"), 9 + 24 + 3 * q + c + 1)
                    m, dst = (P, qT[:, q, cc]) if q < 3 else (P, ckvT[:, q - 3, cc]) if q < 5 else (2 * ROPE, kraw[:, cc])
                    AC(dst, PS[0:m, 3 * (q % 2) + c, 0:CW], ACT.Copy).then_inc(sem("o_out"), 1)
            act.wait_ge(sem("o_out"), 6 + 42)
            for q in range(5):
                if q >= 2:
                    act.wait_ge(sem("o_ss"), q - 1)
                AC(sqb[:, q % 2, :], qT[:, q, :] if q < 3 else ckvT[:, q - 3, 0:TOK], ACT.Square).then_inc(sem("o_sq"), 1)
            for n, (size, last) in enumerate(((Q_RANK, 3), (KV_RANK, 5))):
                act.wait_ge(sem("o_ss"), last)
                if n == 0:
                    act.wait_ge(sem("o_ss"), 5)
                AC(sqb[:, n, :].rearrange("p (c w) -> p c w", c=NC), PS[:, 3 * n:3 * n + 3, 0:CW], ACT.Sqrt, scale=1.0 / size, bias=eps6[:, :]).then_inc(sem("o_rms"), 1)
            for g in range(4):
                act.wait_ge(sem("o_d"), g + 1)
                if g < 2:
                    act.wait_ge(sem("o_scaled"), 2)
                else:
                    act.wait_ge(sem("o_ss"), 6 + g - 1)
                AC(sqb[:, g % 2, :], uc[:, g, :], ACT.Square).then_inc(sem("o_sq"), 1)
            act.wait_ge(sem("o_ss"), 6 + 4)
            AC(sqb[:, 0, :].rearrange("p (c w) -> p c w", c=NC), PS[:, 3:6, 0:CW], ACT.Sqrt, scale=1.0 / 512, bias=epsc[:, :]).then_inc(sem("o_rms"), 1)
            for g in range(4):
                act.wait_ge(sem("o_y"), g + 1)
                AC(yT[:, g, 0:TOK], uc[:, g, :], ACT.Silu, scale=odp[:, g, OD_G:OD_G + 1], bias=odp[:, g, OD_LB:OD_LB + 1]).then_inc(sem("o_yc"), 1)

        def pool_odd(pool, G):
            CP, T2 = nc.gpsimd.tensor_copy, nc.gpsimd.tensor_tensor
            pool.wait_ge(sem("in_odd"), 128)
            with pool.Fori(0, 4) as g, G.rounds(g, 4, 4):
                j = g % 2
                pool.wait_ge(sem("o_out"), g * 6 + 12)
                pool.wait_ge(sem("o_conv"), g)
                G(CP(hs[:, j, :, 0:30], odp[:, g, OD_S:OD_N].rearrange("p (b t) -> p b t", t=30)))
                G(T2(hs[:, j, :, 30:34], smp(za), smp(zs), ALU.mult))
                T2(hp[:, j, 30:30 + PROMPT], za[:, 0:PROMPT], zs[:, 0:PROMPT], ALU.mult).then_inc(sem("o_prod"), 1)
                pool.wait_ge(sem("o_prod"), g + 1)
                G(CP(oso[:, g, 0:30], hp[:, j, PROMPT:PROMPT + 30]))
                G(CP(oso[:, g, 30:270].rearrange("p (b t) -> p b t", t=30), hs[:, j, :, STEP:STEP + 30]))
            pool.dma_start(io["odd_states"], oso[:, :, :]).then_inc(sem("out_odd"), 16)
            pool.wait_ge(sem("o_scaled"), 3)
            pool.dma_start(io["out_ckvT"].rearrange("(k p) t -> p k t", p=P), ckvT[:, :, 0:TOK]).then_inc(sem("out_odd"), 16)
            pool.dma_start(io["out_kpeT"], kpeT[:, :]).then_inc(sem("out_odd"), 16)
            pool.wait_ge(sem("out_odd"), 48)

        def dve_odd(dve, D):
            dve.sem_inc(sem("o_conv"), 1)
            dve.wait_ge(sem("in_odd"), 128)
            D(nc.vector.memset(eps6[:, :], 1e-6))
            D(nc.vector.memset(ckvT[:, :, TOK:TOKP], 0.0))
            for j in range(2):
                D(nc.vector.memset(hp[:, j, 0:30], 0.0))
            PR = slice(0, PROMPT)
            with dve.Fori(0, 4) as g, D.rounds(g, 36, 4):
                j = g % 2
                dve.wait_ge(sem("o_prod"), g + 1)
                part(dve)
                for t in range(STEP):
                    D(TT(hw[:, t, :, :], hs[:, j, :, t:t + CONV_C], odp[:, g, 0:CONV_C].unsqueeze(1).broadcast_to([P, SEQS, CONV_C]), ALU.mult))
                D(nc.vector.tensor_reduce(uc[:, g, PROMPT:TOK].rearrange("p (b t) -> p t b", t=STEP), hw[:, :, :, :], AX.X, ALU.add))
                D(TS(uc[:, g, PROMPT:TOK], uc[:, g, PROMPT:TOK], odp[:, g, OD_B:OD_B + 1], None, ALU.add))
                D(TS(uc[:, g, PR], hp[:, j, PR], odp[:, g, 0:1], odp[:, g, OD_B:OD_B + 1], ALU.mult, ALU.add))
                for k in range(1, CONV_C):
                    ins = mul_add(uc[:, g, PR], hp[:, j, k:k + PROMPT], odp[:, g, k:k + 1], uc[:, g, PR])
                    if k < CONV_C - 1:
                        D(ins)
                ins.then_inc(sem("o_conv"), 1)
            for n, (dst, tiles, g0) in enumerate(((qT, 3, 0), (ckvT, 2, 3))):
                dve.wait_ge(sem("o_rms"), n + 1)
                D(nc.vector.reciprocal(sqb[:, n, :], sqb[:, n, :]))
                for q in range(tiles):
                    ins = nc.vector.scalar_tensor_tensor(dst[:, q, 0:TOK], dst[:, q, 0:TOK], gqk[:, g0 + q:g0 + q + 1], sqb[:, n, :], ALU.mult, ALU.mult)
                    if q < tiles - 1:
                        D(ins)
                ins.then_inc(sem("o_scaled"), 1)
            D(TT(kpeT[:, :], kraw[0:ROPE, :], cosq[0:ROPE, :], ALU.mult))
            D(TT(kraw[0:ROPE, :], kraw[ROPE:2 * ROPE, :], sinq[ROPE:2 * ROPE, :], ALU.mult))
            TT(kpeT[:, :], kpeT[:, :], kraw[0:ROPE, :], ALU.add).then_inc(sem("o_scaled"), 1)
            dve.wait_ge(sem("o_scaled"), 3)
            D(nc.vector.tensor_copy(kpeS[:, :], kpeT[:, PROMPT:TOK]))
            dve.wait_ge(sem("o_ss"), 6)
            for g in range(4):
                v = uc[:, g, :].rearrange("p (c w) -> p c w", c=NC)
                nc.vector.scalar_tensor_tensor(v, PS[:, 0:3, 0:CW], -1.0 / 512, v, ALU.mult, ALU.add).then_inc(sem("o_d"), 1)
            dve.wait_ge(sem("o_rms"), 3)
            D(nc.vector.reciprocal(sqb[:, 0, :], sqb[:, 0, :]))
            for g in range(4):
                TT(uc[:, g, :], uc[:, g, :], sqb[:, 0, :], ALU.mult).then_inc(sem("o_y"), 1)

        def sp_prompt(sp):
            sp.wait_ge(sem("o_yc"), 4)
            sp.wait_ge(sem("out_odd"), 48)
            wq, wk = io["wqn"].rearrange("(k p) n -> p k n", p=P), io["wuk"].rearrange("(k p) n -> p k n", p=P)
            with sp.Fori(0, 2) as a:
                for pp in range(2):
                    sp.wait_ge(sem("a_proj"), a * 2 + pp)
                    part(sp)
                    sp.dma_start(wqn[:, pp, :, :], wq[:, :, bass.ds(a * 2 * P + pp * P, P)]).then_inc(sem(f"in_wq{pp}"), 16)
                    sp.dma_start(wuk[:, pp, :, :], wk[:, :, bass.ds(a * 2 * P + pp * P, P)]).then_inc(sem(f"in_wq{pp}"), 16)

        def pe_prompt(pe):
            pe.wait_ge(sem("o_scaled"), 3)
            pe.wait_ge(sem("o_y"), 1)
            pe.wait_ge(sem("o_rms"), 3)
            for n in range(6):
                a, c = divmod(n, NC)
                if n >= 3:
                    pe.wait_ge(sem("a_pe"), n - 2)
                for w, half in ((wqp, 0), (wqs, 1)):
                    for k in range(3):
                        ins = nc.tensor.matmul(PS[:, 2 * (n % 3) + half, 0:CW], w[:, k, a * P:(a + 1) * P], qT[:, k, c * CW:(c + 1) * CW],
                                               start=(k == 0), stop=(k == 2))
                ins.then_inc(sem("a_pemm"), 1)
            pe.wait_ge(sem("o_yc"), 4)
            pe.wait_ge(sem("a_pe"), 6)
            pe.sem_inc(sem("a_yt"), 2)

            def scores(u, u0):
                t, j = divmod(u, 2)
                if u >= 2:
                    pe.wait_ge(sem("a_p"), u0 + u - 1)
                for c in range(0, (t + 1) * P, 512):
                    w = min(512, (t + 1) * P - c)
                    ins = nc.tensor.matmul(PS[:, u % 2 * 2 + c // 512, 0:w], Q[j][:, t * P:(t + 1) * P], K[j][:, c:c + w], start=True, stop=True)
                ins.then_inc(sem("a_s"), 1)

            def turn(u, u0):
                pe.wait_ge(sem("a_w"), u0 + u + 1)
                pe.wait_ge(sem("a_pt"), u0 + u)
                for b in range(u // 2 + 1):
                    ins = nc.tensor.transpose(PS[:, 4 + b // 4, b % 4 * P:b % 4 * P + P], Pb[:, u % 2, b * P:(b + 1) * P], ident)
                ins.then_inc(sem("a_t"), 1)

            def weigh(u, u0, t0):
                t, j = divmod(u, 2)
                pe.wait_ge(sem("a_pt"), u0 + u + 1)
                if j == 0:
                    pe.wait_ge(sem("a_yt"), t0 + t + 1)
                for b in range(t + 1):
                    ins = nc.tensor.matmul(PS[V_DIM * j:V_DIM * (j + 1), 6 + t % 2, 0:P], V[:, b, V_DIM * j:V_DIM * (j + 1)], PT[:, u % 2, b, :],
                                           start=(b == 0), stop=(b == t))
                ins.then_inc(sem("a_v"), 1)

            with pe.Fori(0, 2) as a:
                for pp in range(2):
                    u0, t0 = a * 32 + pp * 16, a * 16 + pp * 8
                    pe.wait_ge(sem(f"in_wq{pp}"), a * 32 + 32)
                    for c in range(NC):
                        for k in range(3):
                            nc.tensor.matmul(PS[:, c, 0:CW], wqn[:, pp, k, :], qT[:, k, c * CW:(c + 1) * CW], start=(k == 0), stop=(k == 2))
                    for c in range(2):
                        for k in range(2):
                            ins = nc.tensor.matmul(PS[:, 3 + c, :], wuk[:, pp, k, :], ckvT[:, k, c * 512:(c + 1) * 512], start=(k == 0), stop=(k == 1))
                    ins.then_inc(sem("a_proj"), 1)
                    pe.wait_ge(sem("a_yt"), t0 + 2)
                    part(pe)
                    for t in range(8):
                        for k in range(2):
                            ins = nc.tensor.matmul(PS[:, 5 + t // 4, t % 4 * P:t % 4 * P + P], ckvT[:, k, t * P:(t + 1) * P],
                                                   wuv[:, k, bass.ds(a * 4 * V_DIM + pp * 2 * V_DIM, 2 * V_DIM)], start=(k == 0), stop=(k == 1))
                    ins.then_inc(sem("a_vmm"), 1)
                    pe.wait_ge(sem("a_qk"), a * 4 + pp * 2 + 2)
                    scores(0, u0)
                    for u in range(18):
                        if u + 1 < 16:
                            scores(u + 1, u0)
                        if 0 <= u - 1 < 16:
                            turn(u - 1, u0)
                        if 0 <= u - 2 < 16:
                            weigh(u - 2, u0, t0)

        def act_prompt(act, A):
            AC = nc.scalar.activation
            act.wait_ge(sem("out_odd"), 48)
            for j in range(2):
                A(AC(K[j][NOPE:QK, :], kpeT[:, 0:PROMPT], ACT.Copy))

            def expo(u, u0):
                n = (u // 2 + 1) * P
                act.wait_ge(sem("a_m"), u0 + u + 1)
                if u >= 2:
                    act.wait_ge(sem("a_t"), u0 + u - 1)
                AC(Pb[:, u % 2, 0:n], PS[:, u % 2 * 2:u % 2 * 2 + 2, :].rearrange("p a b -> p (a b)")[:, 0:n], ACT.Exp, scale=SCALE,
                   bias=nms[:, u % 2:u % 2 + 1], accum_out=den[:, u % 2:u % 2 + 1]).then_inc(sem("a_p"), 1)

            def stage(u, u0):
                n = u // 2 + 1
                act.wait_ge(sem("a_t"), u0 + u + 1)
                AC(PT[:, u % 2, 0:n, :], PS[:, 4:6, :].rearrange("p a (b c) -> p (a b) c", c=P)[:, 0:n, :], ACT.Copy).then_inc(sem("a_pt"), 1)

            def result(t, a, pp, u0):
                act.wait_ge(sem("a_v"), u0 + 2 * t + 2)
                part(act)
                AC(yT[:, a * 2 + (4 + pp), t * P:(t + 1) * P], PS[:, 6 + t % 2, 0:P], ACT.Copy).then_inc(sem("a_yt"), 1)

            with act.Fori(0, 2) as a, A.rounds(a, 12, 2):
                for pp in range(2):
                    u0 = a * 32 + pp * 16
                    act.wait_ge(sem("a_proj"), a * 2 + pp + 1)
                    for j in range(2):
                        for c in range(NC):
                            A(AC(Q[j][0:NOPE, c * CW:(c + 1) * CW], PS[NOPE * j:NOPE * (j + 1), c, 0:CW], ACT.Copy))
                    for j in range(2):
                        AC(K[j][0:NOPE, :].rearrange("p (a b) -> p a b", a=2), PS[NOPE * j:NOPE * (j + 1), 3:5, :], ACT.Copy).then_inc(sem("a_k"), 1)
                    act.wait_ge(sem("a_k"), a * 4 + pp * 2 + 2)
                    act.sem_inc(sem("a_qk"), 1)
                    expo(0, u0)
                    for u in range(19):
                        if u + 1 < 16:
                            expo(u + 1, u0)
                        if u - 3 >= 0 and (u - 3) % 2 == 1:
                            result((u - 3) // 2, a, pp, u0)
                        if 0 <= u - 1 < 16:
                            stage(u - 1, u0)

        def dve_prompt(dve, D):
            for n in range(6):
                a, c = divmod(n, NC)
                cc = slice(c * CW, (c + 1) * CW)
                dve.wait_ge(sem("a_pemm"), n + 1)
                D(TT(peT[:, a, cc], PS[:, 2 * (n % 3), 0:CW], cosq[:, cc], ALU.mult))
                D(TT(sqb[:, 1, cc], PS[:, 2 * (n % 3) + 1, 0:CW], sinq[:, cc], ALU.mult))
                TT(peT[:, a, cc], peT[:, a, cc], sqb[:, 1, cc], ALU.add).then_inc(sem("a_pe"), 1)
            dve.wait_ge(sem("a_pe"), 6)

            def maximum(u, u0):
                t = u // 2
                bank, col = u % 2 * 2 + t // 4, t % 4 * P
                s_ = PS[:, u % 2 * 2:u % 2 * 2 + 2, :].rearrange("p a b -> p (a b)")[:, 0:(t + 1) * P]
                dve.wait_ge(sem("a_s"), u0 + u + 1)
                D(TT(PS[:, bank, col:col + P], PS[:, bank, col:col + P], cst[:, C_CAUSAL:C_CAUSAL + P], ALU.add))
                D(nc.vector.tensor_reduce(nmax[:, u % 2:u % 2 + 1], s_, AX.X, ALU.max))
                TS(nms[:, u % 2:u % 2 + 1], nmax[:, u % 2:u % 2 + 1], -SCALE, None, ALU.mult).then_inc(sem("a_m"), 1)

            def divide(u, u0):
                j, n = u % 2, (u // 2 + 1) * P
                dve.wait_ge(sem("a_p"), u0 + u + 1)
                D(nc.vector.reciprocal(rden[:, j:j + 1], den[:, j:j + 1]))
                TS(Pb[:, j, 0:n], Pb[:, j, 0:n], rden[:, j:j + 1], None, ALU.mult).then_inc(sem("a_w"), 1)

            with dve.Fori(0, 2) as a, D.rounds(a, 2 * (3 + 16 * 3), 2):
                for pp in range(2):
                    u0 = a * 32 + pp * 16
                    dve.wait_ge(sem("a_vmm"), a * 2 + pp + 1)
                    D(nc.vector.tensor_copy(V[:, :, :].rearrange("p (a b) c -> p a (b c)", a=2), PS[:, 5:7, :]))
                    dve.wait_ge(sem("a_qk"), a * 4 + pp * 2 + 1)
                    part(dve)
                    for j in range(2):
                        r = ROPE * (2 * pp + j)
                        D(nc.vector.tensor_copy(Q[j][NOPE:QK, :], peT[r:r + ROPE, a, :]))
                        nc.vector.tensor_copy(qns[:, a * 4 + (2 * pp + j), :], Q[j][0:NOPE, PROMPT:TOK]).then_inc(sem("a_qns"), 1)
                    dve.wait_ge(sem("a_qns"), a * 4 + pp * 2 + 2)
                    dve.sem_inc(sem("a_qk"), 1)
                    maximum(0, u0)
                    for u in range(16):
                        if u < 15:
                            maximum(u + 1, u0)
                        divide(u, u0)

        kv = [xT, kv1]

        def page(s, n):
            return kv[s][:, n // 4, n % 4 * ROW:(n % 4 + 1) * ROW]

        ROUND = [1, 2, 3, 4, 6, 7, 8, 9]

        def load_quarter(sp, b, s, h):
            for n in range(h * 8, h * 8 + 8):
                phys = sp.value_load(pages[0:1, bass.ds(b * PAGES + n, 1)], min_val=0, max_val=io["cache"].shape[0] // PAGE - 1)
                sp.dma_start(page(s, n), io["cache"][bass.ds(phys * PAGE, PAGE), :]).then_inc(sem(f"in_kv{s}{h}"), 16)

        def kv_loaded(b, s):
            return (b + (2 - s)) * 64

        def sp_sample(sp):
            for h in range(4):
                load_quarter(sp, 0, 0, h)
            sp.wait_ge(sem("a_yt"), 2 + 32)
            sp.wait_ge(sem("a_qns"), 8)
            sp.dma_start(wukT[:, :, :], io["wukT"]).then_inc(sem("in_wukT"), 16)
            for h in range(4):
                load_quarter(sp, 1, 1, h)
            with sp.Fori(0, 3) as i:
                for s in range(2):
                    for h in range(4):
                        sp.wait_ge(sem("d_pv"), i * 8 + (4 * s + h + 1))
                        load_quarter(sp, i * 2 + s + 2, s, h)

        def sequences(eng, body):
            body(0, 0, True, False)
            with eng.Fori(0, 3) as i:
                body(i * 2 + 1, 1, False, False)
                body(i * 2 + 2, 0, False, False)
            body(7, 1, False, False)
            body(8, 0, False, True)

        def pe_sample(pe):
            pe.wait_ge(sem("in_wukT"), 16)
            for r in range(2):
                for h in range(HEADS):
                    ins = nc.tensor.matmul(PS[:, r, h * SAMPLE:(h + 1) * SAMPLE], wukT[:, h, r * P:(r + 1) * P], qns[:, h, :], start=True, stop=True)
            ins.then_inc(sem("d_ql"), 1)
            for r in range(2):
                ins = nc.tensor.transpose(PS[0:SAMPLE, 2, r * P:(r + 1) * P], ckvT[:, r, PROMPT:TOK], ident)
            ins.then_inc(sem("d_ql"), 1)
            pe.wait_ge(sem("d_qa"), 2)
            pe.wait_ge(sem("d_qd"), 1)

            def body(b, s, first, last):
                sb_ = 2 + 2 * s

                def turn(k):
                    q = ROUND.index(k) if k in ROUND else None
                    if q is None:
                        pe.wait_ge(sem("d_kp"), b * 2 + k // 5 + 1)
                    else:
                        pe.wait_ge(sem(f"in_kv{s}{q // 2}"), kv_loaded(b, s))
                    pe.wait_ge(sem("d_cta"), b * 10 + k)
                    pe.wait_ge(sem("d_ctd"), b * 10 + k)
                    part(pe)
                    if q is None:
                        for n in range(4):
                            ins = nc.tensor.transpose(PS[:, n // 2, n % 2 * P:n % 2 * P + P], kpr[:, k // 5, n, :, :].rearrange("p a b -> p (a b)"), ident)
                    else:
                        for n in range(8):
                            ins = nc.tensor.transpose(PS[:, n // 4, n % 4 * P:n % 4 * P + P], page(s, 4 * q + n % 4)[:, n // 4 * P:(n // 4 + 1) * P], ident)
                    ins.then_inc(sem("d_t"), 1)

                def scores(q):
                    pe.wait_ge(sem("d_cta"), b * 10 + ROUND[q] + 1)
                    pe.wait_ge(sem("d_ctd"), b * 10 + ROUND[q] + 1)
                    g, bank = q % 4 * QS, sb_ + q // 4
                    for r in range(2):
                        nc.tensor.matmul(PS[g:g + QS, bank, :], qb[:, s, r, :], CT[:, q % 2, r, :], start=(r == 0), stop=False)
                    for j in range(4):
                        ins = nc.tensor.matmul(PS[g:g + QS, bank, j * P:(j + 1) * P], qpb[:, s, j, :], KT[:, q, :], start=False, stop=(j == 3))
                    if q in (3, 7):
                        ins.then_inc(sem("d_s"), 1)

                if not last:
                    turn(0)
                    turn(1)
                if not first:
                    pe.wait_ge(sem("d_mx"), b)
                    nc.tensor.transpose(PS[0:1, 6, P:2 * P], mxd[:, :], ident).then_inc(sem("d_mt"), 1)
                if not last:
                    turn(2)
                    pe.wait_ge(sem("d_prep"), b * 2 + 2)
                    scores(0)
                if not first:
                    pe.wait_ge(sem("d_mr"), b)
                    nc.tensor.matmul(PS[:, 6, 2 * P:2 * P + 1], m4[:, :, :].rearrange("p a b -> p (a b)"), ones[0:1, 0:1],
                                     start=True, stop=True).then_inc(sem("d_mb"), 1)
                if not last:
                    turn(3)
                    scores(1)
                if not first:
                    pe.wait_ge(sem("d_e"), b * 2)
                    if not last:
                        pe.wait_ge(sem("d_cta"), b * 10 + 4)
                        pe.wait_ge(sem("d_ctd"), b * 10 + 4)
                    for n in range(8):
                        nc.tensor.transpose(PS[:, n // 4, n % 4 * P:n % 4 * P + P], Pd[:, n * P:(n + 1) * P], ident)
                    nc.tensor.transpose(PS[0:SAMPLE, 6, 3 * P:3 * P + QS], Pn[:, :], ident[0:QS, 0:QS])
                    nc.tensor.matmul(PS[0:QS, 6, 3 * P + QS:3 * P + QS + 1], cst[:, C_FOLD:C_FOLD + QS], dend[:, :],
                                     start=True, stop=True).then_inc(sem("d_p"), 1)
                if not last:
                    scores(2)
                if not first:
                    pe.wait_ge(sem("d_pta"), b)
                    pe.wait_ge(sem("d_ptd"), b)
                if not last:
                    turn(4)
                if not first:
                    pe.wait_ge(sem("d_oc"), b)
                    for n in range(PAGES):
                        quad, p = n // 4, n % 4
                        ins = nc.tensor.matmul(PS[0:QS, 7, 0:KV_RANK], PTd[:, quad // 4 * 4 + p, quad % 4 * QS:(quad % 4 + 1) * QS], page(1 - s, n)[:, 0:KV_RANK],
                                               start=(n == 0), stop=False)
                        if n % 8 == 7 and n < PAGES - 1:
                            ins.then_inc(sem("d_pv"), 1)
                    nc.tensor.matmul(PS[0:QS, 7, 0:KV_RANK], PTn[:, :], ckn[:, :], start=False, stop=True).then_inc(sem("d_pv"), 1)
                if not last:
                    turn(5)
                    scores(3)
                    turn(6)
                if not first:
                    pe.wait_ge(sem("d_ol"), b)
                    part(pe)
                    for r in range(2):
                        ins = nc.tensor.transpose(PS[:, 7, KV_RANK + r * QS:KV_RANK + (r + 1) * QS], olr[:, r * P:(r + 1) * P], ident[0:QS, 0:QS])
                    ins.then_inc(sem("d_ot"), 1)
                if not last:
                    turn(7)
                    scores(4)
                    turn(8)
                    scores(5)
                    turn(9)
                    scores(6)
                    for r in range(2):
                        nc.tensor.matmul(PS[0:QS, 6, 0:SAMPLE], qb[:, s, r, :], ckvT[:, r, PROMPT:TOK], start=(r == 0), stop=False)
                    nc.tensor.matmul(PS[0:QS, 6, 0:SAMPLE], qpb[0:ROPE, s, 0, :], kpeS[:, :], start=False, stop=True)
                    scores(7)

            pe.sem_inc(sem("d_oc"), 1)
            sequences(pe, body)
            pe.wait_ge(sem("d_oc"), 1 + 8)
            for h in range(HEADS):
                o = V_DIM * (h % 2)
                for r in range(2):
                    ins = nc.tensor.matmul(PS[o:o + V_DIM, h // 2 % 2, h // 4 * SAMPLE:(h // 4 + 1) * SAMPLE], wuv[:, r, h * V_DIM:(h + 1) * V_DIM],
                                           olat[:, r, :, h * STEP:(h + 1) * STEP], start=(r == 0), stop=(r == 1))
            ins.then_inc(sem("d_y"), 1)

        def pool_sample(pool):
            CP = nc.gpsimd.tensor_copy
            pool.wait_ge(sem("d_qa"), 2)
            pool.wait_ge(sem("d_qp"), 1)

            def fill(b, s):
                CP(qb[:, s, :, :], qlat[:, :, b, :]).then_inc(sem("d_prep"), 1)
                CP(qpb[:, s, :, :], qpz[:, b, :, :]).then_inc(sem("d_prep"), 1)

            def rotary_keys(b, s, half):
                for h in range(2):
                    pool.wait_ge(sem(f"in_kv{s}{2 * half + h}"), kv_loaded(b, s))
                part(pool)
                CP(kpr[:, half, :, :, :], kv[s][:, 4 * half:4 * half + 4, :].rearrange("p q (a c) -> p q a c", c=ROW)[:, :, :, KV_RANK:ROW]).then_inc(sem("d_kp"), 1)

            def both(b, s):
                for half in range(2):
                    pool.wait_ge(sem("d_t"), b * 10 + (5 * half - 9))
                    rotary_keys(b, s, half)

            fill(0, 0)
            fill(1, 1)
            for half in range(2):
                rotary_keys(0, 0, half)
            both(1, 1)
            with pool.Fori(0, 3) as i:
                for s in range(2):
                    pool.wait_ge(sem("d_s"), i * 4 + 2 * s + 2)
                    part(pool)
                    fill(i * 2 + 2 + s, s)
                    both(i * 2 + 2 + s, s)

        def act_sample(act, A):
            AC = nc.scalar.activation
            act.wait_ge(sem("d_ql"), 1)
            for r in range(2):
                src = PS[:, r, 0:HEADS * SAMPLE].rearrange("p (h b t) -> p b h t", h=HEADS, t=STEP)
                AC(qlat[:, r, :, :].rearrange("p b (h t) -> p b h t", t=STEP), src, ACT.Copy).then_inc(sem("d_qa"), 1)

            def body(b, s, first, last):
                def take(k):
                    act.wait_ge(sem("d_t"), b * 10 + k + 1)
                    part(act)
                    ins = AC(CT[:, ROUND.index(k) % 2, 0, :], PS[:, 0, :], ACT.Copy) if k in ROUND else \
                        AC(KT[:, k // 5 * 4:k // 5 * 4 + 2, :].rearrange("p a b -> p (a b)"), PS[:, 0, 0:2 * P], ACT.Copy)
                    ins.then_inc(sem("d_cta"), 1)
                if not last:
                    take(0)
                    take(1)
                    take(2)
                if not first:
                    act.wait_ge(sem("d_nm"), b)
                    AC(Pd[:, :].rearrange("p (a b) -> p a b", a=2), PS[:, 4 - 2 * s:6 - 2 * s, :], ACT.Exp, scale=SCALE, bias=nmd[:, :], accum_out=dend[:, :]).then_inc(sem("d_e"), 1)
                    AC(Pn[:, :], sn[:, :], ACT.Exp, scale=SCALE, bias=nmd[0:QS, :], accum_out=denn[:, :]).then_inc(sem("d_e"), 1)
                if not last:
                    take(3)
                if not first:
                    act.wait_ge(sem("d_p"), b)
                    AC(PTd[:, 0:4, :].rearrange("p a b -> p (a b)"), PS[:, 0, :], ACT.Copy).then_inc(sem("d_pta"), 1)
                if not last:
                    take(4)
                    take(5)
                    take(6)
                if not first:
                    act.wait_ge(sem("d_ot"), b)
                    part(act)
                    AC(olat[:, :, b - 1, :], PS[:, 7, KV_RANK:KV_RANK + 2 * QS].rearrange("p (r q) -> p r q", q=QS), ACT.Copy).then_inc(sem("d_oc"), 1)
                if not last:
                    take(7)
                    take(8)
                    take(9)

            sequences(act, body)
            act.wait_ge(sem("d_y"), 1)
            for a in range(2):
                AC(yT[:, 4 + a:8:2, PROMPT:TOK], PS[:, a, 0:2 * SAMPLE].rearrange("p (c t) -> p c t", t=SAMPLE), ACT.Copy).then_inc(sem("d_yt"), 1)

        def dve_sample(dve, D):
            D(nc.vector.memset(qpz[:, :, :, :], 0.0))
            for j in range(4):
                for hh in range(4):
                    for a in range(2):
                        h = a * 4 + hh
                        D(nc.vector.tensor_copy(qpz[ROPE * j:ROPE * (j + 1), :, j, h * STEP:(h + 1) * STEP],
                                                peT[ROPE * hh:ROPE * (hh + 1), a, PROMPT:TOK].rearrange("p (b t) -> p b t", t=STEP)))
            dve.sem_inc(sem("d_qp"), 1)
            dve.wait_ge(sem("d_ql"), 2)
            nc.vector.tensor_copy(ckn[:, :], PS[0:SAMPLE, 2, 0:KV_RANK]).then_inc(sem("d_qd"), 1)
            new = cst[0:QS, C_NEW:C_NEW + SEQS * SAMPLE].rearrange("p (b k) -> p b k", k=SAMPLE)
            TR = nc.vector.tensor_reduce

            def body(b, s, first, last):
                def take(k):
                    dve.wait_ge(sem("d_t"), b * 10 + k + 1)
                    part(dve)
                    ins = nc.vector.tensor_copy(CT[:, ROUND.index(k) % 2, 1, :], PS[:, 1, :]) if k in ROUND else \
                        nc.vector.tensor_copy(KT[:, k // 5 * 4 + 2:k // 5 * 4 + 4, :].rearrange("p a b -> p (a b)"), PS[:, 1, 0:2 * P])
                    ins.then_inc(sem("d_ctd"), 1)
                if not last:
                    take(0)
                if not first:
                    dve.wait_ge(sem("d_s"), b * 2)
                    part(dve)
                    D(TT(sn[:, :], PS[0:QS, 6, 0:SAMPLE], new[:, b - 1, :], ALU.add))
                    D(TR(mxd[:, :], PS[:, 5 - 2 * s, :], AX.X, ALU.max))
                    D(TR(mxn[:, :], sn[:, :], AX.X, ALU.max))
                    D(TT(mxd[:, :], mxd[:, :], mxa[:, :], ALU.max))
                    TT(mxd[0:QS, :], mxd[0:QS, :], mxn[:, :], ALU.max).then_inc(sem("d_mx"), 1)
                if not last:
                    take(1)
                if not first:
                    dve.wait_ge(sem("d_mt"), b)
                    D(TR(mrow[:, :], PS[0:1, 6, P:2 * P].rearrange("p (j q) -> p q j", q=QS), AX.X, ALU.max))
                    TS(m4[:, :, :], mrow[:, :].unsqueeze(1).broadcast_to([1, 4, QS]), -SCALE, None, ALU.mult).then_inc(sem("d_mr"), 1)
                if not last:
                    take(2)
                if not first:
                    dve.wait_ge(sem("d_mb"), b)
                    nc.vector.tensor_copy(nmd[:, :], PS[:, 6, 2 * P:2 * P + 1]).then_inc(sem("d_nm"), 1)
                if not last:
                    take(3)
                if not first:
                    dve.wait_ge(sem("d_p"), b)
                    D(nc.vector.tensor_copy(PTn[:, :], PS[0:SAMPLE, 6, 3 * P:3 * P + QS]))
                    D(TT(rdd[:, :], PS[0:QS, 6, 3 * P + QS:3 * P + QS + 1], denn[:, :], ALU.add))
                    D(nc.vector.reciprocal(rdd[:, :], rdd[:, :]))
                    nc.vector.tensor_copy(PTd[:, 4:8, :].rearrange("p a b -> p (a b)"), PS[:, 1, :]).then_inc(sem("d_ptd"), 1)
                if not last:
                    take(4)
                if not first:
                    dve.wait_ge(sem("d_pv"), b * 4)
                    TS(olr[:, :], PS[0:QS, 7, 0:KV_RANK], rdd[:, :], None, ALU.mult).then_inc(sem("d_ol"), 1)
                if not last:
                    take(5)
                    take(6)
                    dve.wait_ge(sem("d_s"), b * 2 + 1)
                    D(TR(mxa[:, :], PS[:, 2 + 2 * s, :], AX.X, ALU.max))
                    take(7)
                    take(8)
                    take(9)

            with D.rounds(0, 1, 1):
                body(0, 0, True, False)
            with dve.Fori(0, 3) as i, D.rounds(i, 2 * 9, 3):
                body(i * 2 + 1, 1, False, False)
                body(i * 2 + 2, 0, False, False)
            body(7, 1, False, False)
            body(8, 0, False, True)

        @block.sync
        def _(sp):
            sp.dma_start(cst[:], io["cst"]).then_inc(sem("in_const"), 16)
            sp.dma_start(evp[:], io["ev_pack"]).then_inc(sem("in_const"), 16)
            sp.dma_start(wr[:], io["w_router"].rearrange("(k p) n -> p k n", p=P)).then_inc(sem("in_const"), 16)
            sp.dma_start(brt[:], io["b_router"].partition_broadcast(P)).then_inc(sem("in_const"), 16)
            sp_even(sp)
            sp.wait_ge(sem("yb_done"), 4)
            sp.wait_ge(sem("out_states"), 16)
            sp_mix(sp, 0)
            sp.wait_ge(sem("r_plan"), 1)
            sp.wait_ge(sem("r_rows"), 16 * 2 * NT)
            sp_experts(sp, 0)
            sp_ffn(sp, 0)
            sp.wait_ge(sem("n_tp"), 2 * NT)
            sp_odd(sp)
            sp_prompt(sp)
            sp_sample(sp)
            sp.wait_ge(sem("d_yt"), 2)
            sp_mix(sp, 1)
            sp.wait_ge(sem("r_plan"), 2)
            sp.wait_ge(sem("r_rows"), 32 * 2 * NT)
            sp_experts(sp, 1)
            sp_ffn(sp, 1)

        @block.gpsimd
        def _(pool):
            G = Steps(pool, sem("pool_step"))
            pool_even(pool, G)
            pool_mix(pool, 0)
            pool_route(pool, G, 0)
            pool_experts(pool, 0)
            pool_ffn(pool, 0)
            pool_odd(pool, G)
            pool_sample(pool)
            pool.wait_ge(sem("d_yt"), 2)
            pool_mix(pool, 1)
            pool_route(pool, G, 1)
            pool_experts(pool, 1)
            pool_ffn(pool, 1)

        @block.tensor
        def _(pe):
            pe.wait_ge(sem("in_const"), 64)
            pe_even(pe)
            pe_mix(pe, 0)
            pe_route(pe, 0)
            pe_experts(pe, 0)
            pe_ffn(pe, 0)
            pe_odd(pe)
            pe_prompt(pe)
            pe_sample(pe)
            pe_mix(pe, 1)
            pe_route(pe, 1)
            pe_experts(pe, 1)

        @block.scalar
        def _(act):
            A = Steps(act, sem("act_step"))
            act.wait_ge(sem("in_const"), 64)
            act_even(act, A)
            act_mix(act, 0)
            act_route(act, A, 0)
            act_experts(act, 0)
            act_ffn(act, 0)
            act_odd(act, A)
            act_prompt(act, A)
            act_sample(act, A)
            act_mix(act, 1)
            act_route(act, A, 1)
            act_experts(act, 1)
            act_ffn(act, 1)

        @block.vector
        def _(dve):
            D = Steps(dve, sem("dve_step"))
            dve_even(dve, D)
            dve_mix(dve, D, 0)
            dve_route(dve, D, 0)
            dve_experts(dve, 0)
            dve_ffn(dve, D, 0)
            dve_odd(dve, D)
            dve_prompt(dve, D)
            dve_sample(dve, D)
            dve_mix(dve, D, 1)
            dve_route(dve, D, 1)
            dve_experts(dve, 1)
            dve_ffn(dve, D, 1)


def constants():
    c = np.zeros((P, C_N), np.float32)
    c[:, C_ID:C_ID + P] = np.eye(P)
    c[:, C_ONE:C_ONE + P] = 1
    c[:, C_TRI:C_TRI + P] = np.triu(np.ones((P, P)), 1)
    c[:, C_IOTA:C_IOTA + 16] = np.arange(16, 0, -1)
    c[:, C_IOTA4:C_IOTA4 + 4] = np.arange(4, 0, -1)
    tok = np.arange(P)[:, None] + P * np.arange(NT)[None, :]
    c[:, C_TOK:C_TOK + NT] = tok
    c[:, C_VALID:C_VALID + NT] = tok < TOK
    c[:, C_CAUSAL:C_CAUSAL + P] = np.where(np.arange(P)[None, :] <= np.arange(P)[:, None], 0, -BIG)
    row = np.arange(QS)[:, None, None, None]
    b, kb, kt = np.arange(SEQS)[None, :, None, None], np.arange(SEQS)[None, None, :, None], np.arange(STEP)[None, None, None, :]
    c[:QS, C_NEW:C_NEW + SEQS * SAMPLE] = np.where((kb == b) & (kt <= row % STEP), 0, -BIG).reshape(QS, -1)
    c[:, C_FOLD:C_FOLD + QS] = np.tile(np.eye(QS), (4, 1))
    return c


def rotary():
    half = ROPE // 2
    inv = np.float32(10000.0) ** (-np.arange(half, dtype=np.float32) / np.float32(half))
    pos = np.concatenate([np.arange(PROMPT), np.tile(PAST + np.arange(STEP), SEQS)]).astype(np.float32)
    ang = (pos[None, :] * inv[:, None]).astype(np.float32)
    cos, sin = np.cos(ang).astype(np.float32), np.sin(ang).astype(np.float32)
    return np.tile(np.concatenate([cos, cos]), (4, 1)), np.tile(np.concatenate([-sin, sin]), (4, 1))


def kernel(**inp):
    import concourse.bacc as bacc
    from concourse.bass_utils import run_bass_kernel_spmd

    inp = {k: np.asarray(v) for k, v in inp.items()}
    x = np.concatenate([inp["x_prompt"].reshape(PROMPT, D), inp["x_sample"].reshape(SAMPLE, D)])
    xpad = np.concatenate([x, np.zeros((TOKP - TOK, D), x.dtype)])

    def by_channel(a):
        a = a.reshape(-1, 4, P)
        return a.transpose(2, 1, 0)

    kpe = inp["w_in_odd"][0][:, -ROPE:]
    wq = inp["w_q_b"][0].reshape(Q_RANK, HEADS, QK)
    wqp = wq[:, :, NOPE:]
    cos, sin = rotary()
    arrays = {
        "cst": constants(), "xT0": np.ascontiguousarray(x.T), "xtok": xpad,
        "w_in_even": inp["w_in_even"][0], "w_out_even": inp["w_out_even"][0],
        "lru_wa": inp["lru_wa"][0].reshape(512, 64), "lru_wx": inp["lru_wx"][0].reshape(512, 64),
        "ev_pack": np.concatenate([by_channel(a) for a in (
            inp["conv_a_w"][0], inp["conv_b_w"][0], inp["conv_b_b"][0], inp["lru_ba"][0], inp["lru_bx"][0],
            inp["lru_lambda"][0], inp["state_conv_a"][0], inp["state_conv_b"][0], inp["state_rglru_h"][0])], axis=2),
        "w_in_odd": inp["w_in_odd"][0], "w_out_odd": inp["w_out_odd"][0],
        "w_kpe": np.concatenate([kpe, kpe[:, ROPE // 2:], kpe[:, :ROPE // 2]], axis=1),
        "wqn": wq[:, :, :NOPE].reshape(Q_RANK, -1), "wqp": wqp.reshape(Q_RANK, -1),
        "wqs": np.concatenate([wqp[:, :, ROPE // 2:], wqp[:, :, :ROPE // 2]], axis=2).reshape(Q_RANK, -1),
        "wuk": inp["w_uk"][0].reshape(KV_RANK, -1), "wukT": inp["w_uk"][0].transpose(2, 1, 0),
        "wuv": inp["w_uv"][0].reshape(KV_RANK, -1), "cosq": cos, "sinq": sin,
        "od_pack": np.concatenate([by_channel(a) for a in (
            inp["conv_c_w"][0], inp["conv_c_b"][0], inp["ln_c_g"][0], inp["ln_c_b"][0], inp["state_conv_c"][0])], axis=2),
        "gqk": np.concatenate([inp["q_norm_g"][0].reshape(3, P), inp["kv_norm_g"][0].reshape(2, P)]).T,
        "page_table": inp["page_table"].reshape(1, -1),
        "cache": np.concatenate([inp["cache_ckv"].reshape(-1, KV_RANK), inp["cache_kpe"].reshape(-1, ROPE)], axis=1),
        "w_router": inp["w_router"], "b_router": inp["b_router"],
        "ln_mix_g": inp["ln_mix_g"], "ln_mix_b": inp["ln_mix_b"], "ln_ffn_g": inp["ln_ffn_g"], "ln_ffn_b": inp["ln_ffn_b"],
        "w_exp_in": inp["w_exp_in"].reshape(-1, 2 * F_EXP), "w_exp_out": inp["w_exp_out"].reshape(-1, D),
    }
    nc = bacc.Bacc("TRN2", target_bir_lowering=False, num_devices=1)
    io = {}
    arrays = {name: np.ascontiguousarray(a) for name, a in arrays.items()}
    for name, a in arrays.items():
        io[name] = nc.dram_tensor("in_" + name, list(a.shape), mybir.dt.from_np(a.dtype), kind="ExternalInput").ap()
    arrays = {"in_" + name: a for name, a in arrays.items()}
    for name, shape in (("y", [TOKP, D]), ("even_states", [P, 4, 54]), ("odd_states", [P, 4, 270]),
                        ("out_ckvT", [KV_RANK, TOK]), ("out_kpeT", [ROPE, TOK])):
        io[name] = nc.dram_tensor(name, shape, F32, kind="ExternalOutput").ap()
    for name, shape, dt in (("xm0", [TOKP, D], F32), ("xm1", [TOKP, D], F32), ("x1", [TOKP, D], F32),
                            ("yb", [(MAX_BLOCKS + 1) * P, D], F32), ("tokbuf", [(MAX_BLOCKS + 1) * P, 1], I32)):
        io[name] = nc.dram_tensor(name, shape, dt, kind="Internal").ap()
    build(nc, io)
    nc.compile()
    got = run_bass_kernel_spmd(nc, [arrays], core_ids=[0]).results[0]
    y = got["y"]
    ev, od = got["even_states"], got["odd_states"]

    def states(a, first, n):
        a = a[:, :, first:first + (1 + SEQS) * n].reshape(P, 4, 1 + SEQS, n).transpose(2, 3, 1, 0).reshape(1 + SEQS, n, 512)
        return a[None, :1], a[None, 1:]

    ca, cb, hl, cc = states(ev, 0, 2), states(ev, 18, 3), states(ev, 45, 1), states(od, 0, 30)

    def latents(a):
        return a[:, :PROMPT].T[None, None], a[:, PROMPT:].T.reshape(SEQS, 1, STEP, -1)

    ck, kp = latents(got["out_ckvT"]), latents(got["out_kpeT"])
    out = (y[:PROMPT].reshape(1, PROMPT, D), y[PROMPT:TOK].reshape(SEQS, STEP, D), ca[0], ca[1], cb[0], cb[1],
           hl[0][:, :, 0], hl[1][:, :, 0], cc[0], cc[1], ck[0], ck[1], kp[0], kp[1])
    return tuple(np.ascontiguousarray(a) for a in out)
```

```python
import contextlib

import numpy as np

import concourse.bass as bass
from concourse import mybir
from concourse.alu_op_type import AluOpType as ALU

F32 = mybir.dt.float32
I32 = mybir.dt.int32
U32 = mybir.dt.uint32
ACT = mybir.ActivationFunctionType
AX = mybir.AxisListType

P = 128
D = 1024
KD = D // P
PROMPT, SEQS, STEP = 1024, 8, 4
SAMPLE = SEQS * STEP
TOK = PROMPT + SAMPLE
NT = 9
TOKP = NT * P
NC, CW = 3, TOK // 3
TAIL = PROMPT - 2 * CW
ALPHA = 4.0 ** 0.25
EXPERTS, GROUPS, PER_GROUP = 16, 4, 4
F_EXP = 512
MAX_BLOCKS = 32
BIG = 1.0e30
HEADS, NOPE, ROPE, V_DIM = 8, 64, 32, 64
QK = NOPE + ROPE
QS = HEADS * STEP
Q_RANK, KV_RANK = 384, 256
SCALE = float(QK) ** -0.5
PAGE, PAST = 128, 4096
PAGES = PAST // PAGE
ROW = KV_RANK + ROPE
CONV_C = 31
OTHER_TAPS = 8
OD_W, OD_B, OD_G, OD_LB, OD_S, OD_N = 0, 31, 32, 33, 34, 274
EV_CA, EV_CB, EV_BB, EV_BA, EV_BX, EV_LAM, EV_SA, EV_SB, EV_H0, EV_N = 0, 3, 7, 8, 9, 10, 11, 27, 51, 59
C_ID, C_ONE, C_TRI, C_IOTA, C_IOTA4, C_TOK, C_VALID, C_CAUSAL, C_NEW, C_FOLD, C_N = 0, 128, 256, 384, 400, 404, 413, 422, 550, 806, 838


class Steps:

    def __init__(self, eng, sem, apart=None):
        self.eng, self.sem, self.base, self.n, self.apart = eng, sem, 0, 0, apart

    def __call__(self, ins):
        ins.then_inc(self.sem, 1)
        self.n += 1
        self.eng.wait_ge(self.sem, self.base + self.n)
        if self.apart is not None:
            self.eng.sem_inc(self.apart, 1)

    @contextlib.contextmanager
    def rounds(self, i, per, count):
        start = self.base + self.n
        self.base, self.n = start + i * per, 0
        yield
        assert self.n == per, f"{self.n} steps in a round, not {per}"
        self.base, self.n = start + count * per, 0


def build(nc, io):
    ctx = contextlib.ExitStack()
    with ctx:
        sems = {}

        def sem(name):
            if name not in sems:
                sems[name] = ctx.enter_context(nc.semaphore(name))
            return sems[name]

        def keep(name, shape, dt=F32):
            return ctx.enter_context(nc.sbuf_tensor(name, shape, dt))

        def phase(stack):
            return lambda name, shape, dt=F32: stack.enter_context(nc.sbuf_tensor(name, shape, dt))

        PS = ctx.enter_context(nc.psum_tensor("PS", [P, 8, 512], F32))

        xT = keep("xT", [P, KD, TOKP])
        yT = keep("yT", [P, KD, TOKP])
        cst = keep("cst", [P, C_N])
        ident, ones, tri = cst[:, C_ID:C_ID + P], cst[:, C_ONE:C_ONE + P], cst[:, C_TRI:C_TRI + P]
        wr = keep("wr", [P, KD, EXPERTS])
        brt = keep("brt", [P, EXPERTS])
        logits = keep("logits", [P, NT, EXPERTS])
        gate = keep("gate", [P, NT, 2])
        dest = keep("dest", [P, NT, 2], I32)
        plan = keep("plan", [P, 3 * EXPERTS + 1], I32)
        stat = keep("stat", [P, 2, 6])
        mv = keep("mv", [P, 2])
        rstd, nmr = keep("rstd", [P, 1]), keep("nmr", [P, 1])
        sd = keep("sd", [P, 1])
        epsc = keep("epsc", [P, 1])
        lngb = keep("lngb", [P, 2, D])
        lng, lnb = lngb[:, 0, :], lngb[:, 1, :]
        wo = keep("wo", [P, KD, D])

        with contextlib.ExitStack() as st:
            sb = phase(st)
            W5 = sb("W5", [P, 5, KD, P])
            evp = sb("evp", [P, 4, EV_N])
            s8 = sb("s8", [P, 8, 4])
            lruw = sb("lruw", [P, 2, P])
            cbp, cbs = sb("cbp", [P, 3 + PROMPT]), sb("cbs", [P, SEQS, 3 + STEP])
            cap, cas = sb("cap", [P, 2 + PROMPT]), sb("cas", [P, SEQS, 2 + STEP])
            zC, zV, zB, zG = (sb(n, [P, TOK]) for n in ("zC", "zV", "zB", "zG"))
            ub, ua, rr, ii, aa, th, sq, hh = (sb(n, [P, TOK]) for n in ("ub", "ua", "rr", "ii", "aa", "th", "sq", "hh"))
            t1 = sb("t1", [P, TOK])
            h8 = sb("h8", [P, SEQS])
            evo = sb("evo", [P, 4, 54])
        odd = contextlib.ExitStack()
        sb = phase(odd)
        gqk = sb("gqk", [P, 5])
        eps6 = sb("eps6", [P, 1])
        wuv = sb("wuv", [P, 2, HEADS * V_DIM])
        ckvT = sb("ckvT", [P, 2, TOKP])
        peT = sb("peT", [P, 2, TOK])
        qns = sb("qns", [NOPE, HEADS, SAMPLE])
        kpeS = sb("kpeS", [ROPE, SAMPLE])
        pages = sb("pages", [1, SEQS * PAGES], I32)
        with contextlib.ExitStack() as st:
            sb = phase(st)
            odp = sb("odp", [P, 4, OD_N])
            qT = sb("qT", [P, 3, TOK])
            kraw = sb("kraw", [2 * ROPE, TOK])
            kpeT = sb("kpeT", [ROPE, TOK])
            cosq, sinq = sb("cosq", [P, TOK]), sb("sinq", [P, TOK])
            sqb = yT[:, 2:4, 0:TOK]
            csq = yT[:, 0:2, 0:TOK]
            rtmp = sb("rtmp", [P, CW])
            with contextlib.ExitStack() as st2:
                sb = phase(st2)
                W4 = sb("W4", [P, 4, KD, P])
                uc = yT[:, 4:8, 0:TOK]
                za, zs = yT[:, 0, 0:TOK], yT[:, 1, 0:TOK]
                hp, hs = sb("hp", [P, 2, CONV_C - 1 + PROMPT]), sb("hs", [P, 2, SEQS, CONV_C - 1 + STEP])
                hw = sb("hw", [P, STEP, SEQS, CONV_C])
                osp = sb("osp", [P, 4, 30])
            with contextlib.ExitStack() as st2:
                sb = phase(st2)
                wqp, wqs = sb("wqp", [P, 3, 2 * P]), sb("wqs", [P, 3, 2 * P])
                wqn = sb("wqn", [P, 2, 3, P])
                wuk = sb("wuk", [P, 2, 2, P])
                V = sb("V", [P, 8, 2 * V_DIM])
                Q = [sb(f"Q{j}", [QK, TOK]) for j in range(2)]
                K = [sb(f"K{j}", [QK, PROMPT]) for j in range(2)]
                Pb = [lng, lnb]
                PT = [x[:, 0:PROMPT].rearrange("p (a b) -> p a b", b=P) for x in (cosq, sinq)]
                nmax, nms, den, rden = (sb(n, [P, 2]) for n in ("nmax", "nms", "den", "rden"))
        with contextlib.ExitStack() as st:
            sb = phase(st)
            kv1, kpr = sb("kv1", [P, KD, TOKP]), sb("kpr", [P, 2, 4, 4, ROPE])
            CT, KT = sb("CT", [P, 2, 2, 512]), sb("KT", [P, 8, P])
            wukT = [x[0:NOPE, :].rearrange("p (h r) -> p h r", h=4) for x in (lng, lnb)]
            Pd, PTd = lng, lnb[:, :].rearrange("p (a b) -> p a b", b=P)
            qlat = sb("qlat", [P, 2, SEQS, QS])
            qpz = sb("qpz", [P, SEQS, 4, QS])
            qb, qpb = sb("qb", [P, 2, 2, QS]), sb("qpb", [P, 2, 4, QS])
            ckn = sb("ckn", [SAMPLE, KV_RANK])
            olat, olr = sb("olat", [P, 2, SEQS, QS]), sb("olr", [QS, KV_RANK])
            Pn, PTn, sn = (sb(n, [QS, SAMPLE]) for n in ("Pn", "PTn", "sn"))
            mxa, mxd, nmd, dend = (sb(n, [P, 1]) for n in ("mxa", "mxd", "nmd", "dend"))
            mxn, denn, rdd = (sb(n, [QS, 1]) for n in ("mxn", "denn", "rdd"))
            mrow, m4 = sb("mrow", [1, QS]), sb("m4", [1, 4, QS])
        odd.close()
        with contextlib.ExitStack() as st:
            sb = phase(st)
            yst = sb("yst", [P, 3, KD, P])
            xres = sb("xres", [P, 3, D])
            xn = sb("xn", [P, 3, D])
            sx = sb("sx", [P, D])
            xts = sb("xts", [P, KD, P])
            rt = [sb(f"rt{n}", [P, NT, EXPERTS]) for n in range(9)]
            rs = [sb(f"rs{n}", [P, NT, 4]) for n in range(6)]
            rk = [sb(f"rk{n}", [P, NT, 1]) for n in range(5)]
            cum = sb("cum", [P, NT + 1, EXPERTS])
            cnt = [sb(f"cnt{n}", [P, EXPERTS]) for n in range(4)]
            cnti = sb("cnti", [P, EXPERTS], I32)
            tokid = sb("tokid", [P, NT], I32)
            zid = sb("zid", [P, MAX_BLOCKS + 1], I32)
            w1 = [xT[:, :, 0:2 * F_EXP], yT[:, :, 0:2 * F_EXP]]
            w2 = sb("w2", [P, 2, F_EXP // P, D])
            y1, y2 = wo[:, 0:3, :], wo[:, 3:6, :]
            xtb, gx = yst[:, 1, :, :], yst[:, 2, :, :].rearrange("p a b -> p (a b)")
            idx = sb("idx", [P, 1], I32)
            fx = [sx[:, :], yst[:, 1, :, :].rearrange("p a b -> p (a b)"), yst[:, 2, :, :].rearrange("p a b -> p (a b)")]
            sg = sb("sg", [P, 4, P])
            ht = sb("ht", [P, 4, P])
            ysb = wo[:, 6, :]
            zrow = yst[:, 0, :, :].rearrange("p a b -> p (a b)")

        xm = [io["xm0"], io["xm1"]]
        tokbuf, yb = io["tokbuf"], io["yb"]
        block = ctx.enter_context(nc.Block())

        def part(eng):
            eng.sem_inc(sem("apart"), 1)

        def smp(x):
            return x[:, PROMPT:TOK].rearrange("p (b t) -> p b t", t=STEP)

        def mul_add(out, x, scalar, acc):
            return nc.vector.scalar_tensor_tensor(out, x, scalar, acc, ALU.mult, ALU.add)

        TT = nc.vector.tensor_tensor
        TS = nc.vector.tensor_scalar

        def sp_even(sp):
            w_in = io["w_in_even"].rearrange("(k p) n -> p k n", p=P)
            sp.dma_start(xT[:, 0:4, 0:TOK], io["xT0"].rearrange("(k p) t -> p k t", p=P)[:, 0:4, :]).then_inc(sem("in_xT"), 16)
            sp.dma_start(xT[:, 4:8, 0:TOK], io["xT0"].rearrange("(k p) t -> p k t", p=P)[:, 4:8, :]).then_inc(sem("in_xT"), 16)
            sp.wait_ge(sem("lru_zero"), 1)
            with sp.Fori(0, 4) as g:
                for p, j in enumerate((4, 1, 2, 0, 3)):
                    sp.wait_ge(sem("z_mm"), 1 + g * 15 + 3 * p)
                    part(sp)
                    sp.dma_start(W5[:, p, :, :], w_in[:, :, bass.ds(g * P + j * 512, P)]).then_inc(sem(f"in_w_{p}"), 16)
                    if p == 0:
                        sp.wait_ge(sem("lru_mm"), 1 + g * 6)
                        for n, w in enumerate(("lru_wa", "lru_wx")):
                            for h in range(2):
                                sp.dma_start(lruw[64 * h:64 * h + 64, n, 64 * h:64 * h + 64],
                                             io[w][bass.ds((g * 2 + h) * 64, 64), :]).then_inc(sem("in_lruw"), 16)

        def pe_even(pe):
            pe.sem_inc(sem("z_mm"), 12)
            pe.wait_ge(sem("in_xT"), 32)
            with pe.Fori(0, 4) as g:
                for p in range(5):
                    if p == 3:
                        pe.wait_ge(sem("ub_ready"), g + 1)
                        pe.wait_ge(sem("in_lruw"), g * 64 + 64)
                        for q in range(6):
                            pe.wait_ge(sem("lru_out"), g * 6 + q + 1)
                            nc.tensor.matmul(PS[:, 5 + q % 3, 0:CW], lruw[:, q % 2, :],
                                             ub[:, q // 2 * CW:(q // 2 + 1) * CW], start=True, stop=True
                                             ).then_inc(sem("lru_mm"), 1)
                    pe.wait_ge(sem(f"in_w_{p}"), g * 16 + 16)
                    for c in range(NC):
                        n = 3 * p + c
                        pe.wait_ge(sem("z_out"), g * 15 + n + 1)
                        for k in range(KD):
                            ins = nc.tensor.matmul(PS[:, n % 5, 0:CW], W5[:, p, k, :], xT[:, k, c * CW:(c + 1) * CW],
                                                   start=(k == 0), stop=(k == KD - 1))
                        ins.then_inc(sem("z_mm"), 1)

        def act_even(act, A):
            AC = nc.scalar.activation
            act.sem_inc(sem("z_out"), 5)
            act.sem_inc(sem("lru_out"), 3)
            act.wait_ge(sem("softplus_abs"), 1)
            AC(s8[:, 1, :], s8[:, 0, :], ACT.Exp, scale=-1.0).then_inc(sem("softplus_exp"), 1)

            def take(g, p, c, dst, fn, src=None):
                ins = AC(dst, PS[:, (3 * p + c) % 5, 0:CW] if src is None else src, fn)
                ins.then_inc(sem("z_out"), 1)

            with act.Fori(0, 4) as g, A.rounds(g, 4, 4):
                act.wait_ge(sem("states_kept"), 1 + g)
                for c in range(NC):
                    act.wait_ge(sem("z_mm"), 1 + g * 15 + 12 + c + 1)
                    if c < 2:
                        take(g, 0, c, cbp[:, 3 + c * CW:3 + (c + 1) * CW], ACT.Copy)
                A(AC(cbp[:, 3 + 2 * CW:3 + PROMPT], PS[:, 2, 0:TAIL], ACT.Copy))
                take(g, 0, 2, cbs[:, :, 3:7], ACT.Copy, PS[:, 2, TAIL:CW].rearrange("p (b t) -> p b t", t=STEP))
                A(AC(cbs[:, :, 0:3], evp[:, g, EV_SB:EV_H0].rearrange("p (b t) -> p b t", t=3), ACT.Copy))
                act.wait_ge(sem("z_out"), g * 15 + 5 + 3)
                part(act)
                A(AC(ub[:, 0:PROMPT], cbp[:, 0:PROMPT], ACT.Identity, bias=evp[:, g, EV_BB:EV_BB + 1], scale=evp[:, g, EV_CB:EV_CB + 1]))
                part(act)
                AC(smp(ub), cbs[:, :, 0:STEP], ACT.Identity, bias=evp[:, g, EV_BB:EV_BB + 1],
                   scale=evp[:, g, EV_CB:EV_CB + 1]).then_inc(sem("tap_ready"), 1)
                for p, dst in ((1, zC), (2, zV)):
                    for c in range(NC):
                        act.wait_ge(sem("z_mm"), 1 + g * 15 + 12 + 3 * p + c + 1)
                        take(g, p, c, dst[:, c * CW:(c + 1) * CW], ACT.Copy)
                for q in range(6):
                    act.wait_ge(sem("lru_mm"), 1 + g * 6 + q + 1)
                    part(act)
                    k = EV_BX if q % 2 else EV_BA
                    AC((ii if q % 2 else rr)[:, q // 2 * CW:(q // 2 + 1) * CW], PS[:, 5 + q % 3, 0:CW], ACT.Sigmoid,
                       bias=evp[:, g, k:k + 1]).then_inc(sem("lru_out"), 1)
                act.wait_ge(sem("lru_out"), g * 6 + 3 + 6)
                part(act)
                AC(th[:, :], rr[:, :], ACT.Tanh, scale=s8[:, 7, bass.ds(g, 1)]).then_inc(sem("th_ready"), 1)
                A(AC(aa[:, :], rr[:, :], ACT.Exp, scale=s8[:, 6, bass.ds(g, 1)]))
                for p, dst, fn in ((3, zB, ACT.Copy), (4, zG, ACT.Gelu_apprx_tanh)):
                    for c in range(NC):
                        act.wait_ge(sem("z_mm"), 1 + g * 15 + 12 + 3 * p + c + 1)
                        take(g, p, c, dst[:, c * CW:(c + 1) * CW], fn)
                act.wait_ge(sem("m_ready"), g + 1)
                AC(sq[:, :], th[:, :], ACT.Sqrt, scale=2.0).then_inc(sem("sq_ready"), 1)

        def dve_even(dve, D):
            D(nc.vector.memset(lruw[:, :, :], 0.0))
            dve.sem_inc(sem("lru_zero"), 1)
            D(nc.vector.memset(cbp[:, 0:3], 0.0))
            D(nc.vector.memset(cap[:, 0:2], 0.0))
            D(nc.vector.memset(yT[:, :, TOK:TOKP], 0.0))
            D(nc.vector.memset(epsc[:, :], 1e-5))
            dve.wait_ge(sem("in_const"), 64)
            lam = evp[:, :, EV_LAM]
            D(TS(s8[:, 2, :], lam, -1.0, None, ALU.mult))
            TT(s8[:, 0, :], s8[:, 2, :], lam, ALU.max).then_inc(sem("softplus_abs"), 1)
            dve.wait_ge(sem("softplus_exp"), 1)
            D(TS(s8[:, 3, :], s8[:, 1, :], 2.0, None, ALU.add))
            D(nc.vector.reciprocal(s8[:, 3, :], s8[:, 3, :]))
            D(TT(s8[:, 3, :], s8[:, 3, :], s8[:, 1, :], ALU.mult))
            D(TT(s8[:, 4, :], s8[:, 3, :], s8[:, 3, :], ALU.mult))
            D(TS(s8[:, 5, :], s8[:, 4, :], 1.0 / 15, 1.0 / 13, ALU.mult, ALU.add))
            for n in (11, 9, 7, 5, 3, 1):
                D(TT(s8[:, 5, :], s8[:, 5, :], s8[:, 4, :], ALU.mult))
                D(TS(s8[:, 5, :], s8[:, 5, :], 1.0 / n, None, ALU.add))
            D(TT(s8[:, 5, :], s8[:, 5, :], s8[:, 3, :], ALU.mult))
            D(TS(s8[:, 2, :], s8[:, 2, :], 0.0, 8.0, ALU.max, ALU.mult))
            D(mul_add(s8[:, 7, :], s8[:, 5, :], 16.0, s8[:, 2, :]))
            D(TS(s8[:, 6, :], s8[:, 7, :], -1.0, None, ALU.mult))
            dve.sem_inc(sem("softplus_done"), 1)
            PR = slice(0, PROMPT)
            with dve.Fori(0, 4) as g, D.rounds(g, 23, 4):
                def col(k):
                    return evp[:, g, k:k + 1]
                dve.wait_ge(sem("tap_ready"), g + 1)
                for k in range(1, 4):
                    D(mul_add(smp(ub), cbs[:, :, k:k + STEP], col(EV_CB + k), smp(ub)))
                    if k < 3:
                        D(mul_add(ub[:, PR], cbp[:, k:k + PROMPT], col(EV_CB + k), ub[:, PR]))
                mul_add(ub[:, PR], cbp[:, 3:3 + PROMPT], col(EV_CB + 3), ub[:, PR]).then_inc(sem("ub_ready"), 1)
                dve.wait_ge(sem("z_out"), g * 15 + 5 + 9)
                dve.wait_ge(sem("states_kept"), 1 + g)
                D(nc.vector.tensor_copy(cas[:, :, 0:2], evp[:, g, EV_SA:EV_SB].rearrange("p (b t) -> p b t", t=2)))
                D(TT(cas[:, :, 2:6], smp(zC), smp(zV), ALU.mult))
                D(TT(cap[:, 2:2 + PROMPT], zC[:, PR], zV[:, PR], ALU.mult))
                D(TS(ua[:, PR], cap[:, 0:PROMPT], col(EV_CA), None, ALU.mult))
                D(TS(smp(ua), cas[:, :, 0:STEP], col(EV_CA), None, ALU.mult))
                for k in range(1, 3):
                    D(mul_add(ua[:, PR], cap[:, k:k + PROMPT], col(EV_CA + k), ua[:, PR]))
                    D(mul_add(smp(ua), cas[:, :, k:k + STEP], col(EV_CA + k), smp(ua)))
                dve.wait_ge(sem("th_ready"), g + 1)
                D(TS(t1[:, :], th[:, :], 1.0, None, ALU.add))
                D(nc.vector.reciprocal(t1[:, :], t1[:, :]))
                TT(th[:, :], th[:, :], t1[:, :], ALU.mult).then_inc(sem("m_ready"), 1)
                D(TT(ii[:, :], ii[:, :], ub[:, :], ALU.mult))
                dve.wait_ge(sem("z_out"), g * 15 + 5 + 12)
                D(TT(yT[:, g, 0:TOK], ua[:, :], zB[:, :], ALU.mult))
                dve.wait_ge(sem("sq_ready"), g + 1)
                D(TT(t1[:, :], sq[:, :], ii[:, :], ALU.mult))
                D(TT(h8[:, :], smp(aa)[:, :, 0], evp[:, g, EV_H0:EV_N], ALU.mult))
                D(TT(smp(t1)[:, :, 0], smp(t1)[:, :, 0], h8[:, :], ALU.add))
                D(nc.vector.memset(smp(aa)[:, :, 0], 0.0))
                D(nc.vector.tensor_tensor_scan(hh[:, :], aa[:, :], t1[:, :], 0.0, ALU.mult, ALU.add))
                TT(yT[:, g + 4, 0:TOK], zG[:, :], hh[:, :], ALU.mult).then_inc(sem("yb_done"), 1)

        def pool_even(pool, G):
            CP = nc.gpsimd.tensor_copy
            with pool.Fori(0, 4) as g, G.rounds(g, 5, 4):
                pool.wait_ge(sem("yb_done"), g + 1)
                G(CP(evo[:, g, 0:2], cap[:, PROMPT:PROMPT + 2]))
                G(CP(evo[:, g, 2:18].rearrange("p (b t) -> p b t", t=2), cas[:, :, STEP:STEP + 2]))
                G(CP(evo[:, g, 18:21], cbp[:, PROMPT:PROMPT + 3]))
                G(CP(evo[:, g, 21:45].rearrange("p (b t) -> p b t", t=3), cbs[:, :, STEP:STEP + 3]))
                G(CP(evo[:, g, 45:46], hh[:, PROMPT - 1:PROMPT]))
                CP(evo[:, g, 46:54], smp(hh)[:, :, STEP - 1]).then_inc(sem("states_kept"), 1)
            pool.wait_ge(sem("states_kept"), 1 + 4)
            pool.dma_start(io["even_states"], evo[:, :, :]).then_inc(sem("out_states"), 16)
            pool.wait_ge(sem("out_states"), 16)

        def rows(t):
            return bass.ds(t * P, P)

        def load_wo(sp, l):
            wout = io["w_out_even" if l == 0 else "w_out_odd"].rearrange("(k p) n -> p k n", p=P)
            for n in range(2):
                sp.dma_start(wo[:, :, n * 512:(n + 1) * 512], wout[:, :, n * 512:(n + 1) * 512]).then_inc(sem("n_in_w"), 16)

        def load_ln(sp, name, l):
            sp.dma_start(lng, io[name + "_g"][l, :].partition_broadcast(P)).then_inc(sem("n_in_w"), 16)
            sp.dma_start(lnb, io[name + "_b"][l, :].partition_broadcast(P)).then_inc(sem("n_in_w"), 16)

        def load_expert(sp, e, s):
            w1d = io["w_exp_in"].rearrange("(e k p) n -> p e k n", p=P, k=KD)
            w2d = io["w_exp_out"].rearrange("(e k p) n -> p e k n", p=P, k=F_EXP // P)
            for h in range(2):
                sp.dma_start(w1[s][:, h * 4:h * 4 + 4, :], w1d[:, e, h * 4:h * 4 + 4, :]).then_inc(sem(f"e_in_w1_{s}"), 16)
            sp.dma_start(w2[:, s, :, :], w2d[:, e, :, :]).then_inc(sem(f"e_in_w2_{s}"), 16)

        def sp_mix(sp, l):
            x = io["xtok"] if l == 0 else io["x1"]
            load_ln(sp, "ln_mix", l)
            for s in range(3):
                sp.dma_start(xres[:, s, :], x[rows(s), :]).then_inc(sem(f"n_in_x{s}"), 16)
            if l == 0:
                sp.wait_ge(sem("z_mm"), 1 + 12 + 60)
            load_expert(sp, l * EXPERTS, 0)

            def store(t, s):
                sp.wait_ge(sem("n_ln"), 18 * l + t + 1)
                sp.dma_start(xm[l][rows(t), :], xn[:, s, :]).then_inc(sem(f"n_out{s}"), 16)

            with sp.Fori(0, 2) as i:
                for s in range(3):
                    store(i * 3 + s, s)
                    sp.dma_start(xres[:, s, :], x[rows(i * 3 + s + 3), :]).then_inc(sem(f"n_in_x{s}"), 16)
            for s in range(3):
                store(6 + s, s)
                if s == 1:
                    sp.wait_ge(sem("m_st"), 9 * l + NT)
                    load_expert(sp, l * EXPERTS + 1, 1)
            for s in range(3):
                sp.wait_ge(sem(f"n_out{s}"), 16 + 96 * l + 48)
            sp.sem_inc(sem("m_kept"), 1)
            load_ln(sp, "ln_ffn", l)
            for s in range(3):
                sp.dma_start(xres[:, s, :], xm[l][rows(s), :]).then_inc(sem(f"n_in_x{s}"), 16)

        def pool_mix(pool, l):
            u = f"m{l}_"
            with pool.Fori(0, 3) as i:
                for s in range(3):
                    t = i * 3 + s
                    pool.wait_ge(sem("m_mm"), 9 * l + t + 1)
                    nc.gpsimd.tensor_copy(yst[:, s, :, :], yT[:, :, rows(t)]).then_inc(sem("m_st"), 1)

        def pe_transpose(src):
            for k in range(KD):
                ins = nc.tensor.transpose(PS[:, 4 + k // 4, k % 4 * P:k % 4 * P + P], src[:, k * P:(k + 1) * P], ident)
            ins.then_inc(sem("n_tp"), 1)

        def pe_mix(pe, l):
            u = f"m{l}_"
            if l == 0:
                pe.sem_inc(sem("m_mm"), 3)
            pe.wait_ge(sem("n_in_w"), 96 * l + 64)

            def multiply(t, s, meanwhile=None):
                pe.wait_ge(sem("m_st"), 9 * l + t + 1)
                pe.wait_ge(sem("m_ps"), 9 * l + t + 1)
                for n in range(2):
                    for k in range(KD):
                        if n == 1 and k == KD // 2 and meanwhile:
                            meanwhile()
                        ins = nc.tensor.matmul(PS[:, (t % 2) * 2 + n, :], yst[:, s, k, :], wo[:, k, n * 512:(n + 1) * 512],
                                               start=(k == 0), stop=(k == KD - 1))
                ins.then_inc(sem("m_mm"), 1)

            def turn(t, s):
                pe.wait_ge(sem("n_ln"), 18 * l + t + 1)
                pe.wait_ge(sem("n_tpo"), 1 + 18 * l + t)
                pe_transpose(xn[:, s, :])

            def route(t):
                pe.wait_ge(sem("n_tpo"), 1 + 18 * l + t + 1)
                pe.wait_ge(sem("m_lg"), 1 + 9 * l + t)
                for k in range(KD):
                    ins = nc.tensor.matmul(PS[:, 6, 0:EXPERTS], xts[:, k, :], wr[:, k, :], start=(k == 0), stop=(k == KD - 1))
                ins.then_inc(sem("m_rm"), 1)

            multiply(0, 0)
            with pe.Fori(0, 2) as i:
                for s in range(3):
                    multiply(i * 3 + s + 1, (s + 1) % 3, lambda: turn(i * 3 + s, s))
                    route(i * 3 + s)
            for t in (6, 7):
                multiply(t + 1, (t + 1) % 3, lambda: turn(t, t % 3))
                route(t)
            turn(8, 2)
            route(8)

        def root(act, n):
            act.wait_ge(sem("n_var"), n + 1)
            nc.scalar.activation(sd[:, :], mv[:, 1:2], ACT.Sqrt, bias=epsc[:, :]).then_inc(sem("n_sd"), 1)

        def shift_scale(act, n, i, s, src):
            act.wait_ge(sem("n_nmr"), n + 1)
            act.wait_ge(sem(f"n_out{s}"), 16 + i)
            part(act)
            nc.scalar.activation(xn[:, s, :], src, ACT.Identity, scale=rstd[:, :], bias=nmr[:, :]).then_inc(sem("n_xh"), 1)

        def act_mix(act, l):
            with act.Fori(0, 3) as i:
                for s in range(3):
                    t = i * 3 + s
                    root(act, 18 * l + t)
                    shift_scale(act, 18 * l + t, 96 * l + i * 16, s, sx[:, :])
                    act.wait_ge(sem("n_tp"), 18 * l + t + 1)
                    part(act)
                    nc.scalar.activation(xts[:, :, :].rearrange("p (a b) c -> p a (b c)", a=2), PS[:, 4:6, :], ACT.Copy).then_inc(sem("n_tpo"), 1)
                    act.wait_ge(sem("m_rm"), 9 * l + t + 1)
                    part(act)
                    nc.scalar.activation(logits[:, t, :], PS[:, 6, 0:EXPERTS], ACT.Copy).then_inc(sem("m_lg"), 1)

        def moments(dve, D, x):
            for h in range(2):
                D(nc.vector.bn_stats(stat[:, h, :], x[:, h * 512:(h + 1) * 512]))
            part(dve)
            nc.vector.bn_aggr(mv[:, :], stat[:, :, :].rearrange("p a b -> p (a b)")).then_inc(sem("n_var"), 1)

        def reciprocal_sd(dve, D, n):
            dve.wait_ge(sem("n_sd"), n + 1)
            D(nc.vector.reciprocal(rstd[:, :], sd[:, :]))
            TS(nmr[:, :], mv[:, 0:1], rstd[:, :], -1.0, ALU.mult, ALU.mult).then_inc(sem("n_nmr"), 1)

        def affine(dve, D, n, s):
            dve.wait_ge(sem("n_xh"), n + 1)
            D(TT(xn[:, s, :], xn[:, s, :], lng[:, :], ALU.mult))
            TT(xn[:, s, :], xn[:, s, :], lnb[:, :], ALU.add).then_inc(sem("n_ln"), 1)

        def dve_mix(dve, D, l):
            if l == 0:
                dve.sem_inc(sem("m_ps"), 2)
            dve.wait_ge(sem("n_in_w"), 96 * l + 64)
            with dve.Fori(0, 3) as i, D.rounds(i, 12, 3):
                for s in range(3):
                    t = i * 3 + s
                    dve.wait_ge(sem(f"n_in_x{s}"), 96 * l + i * 16 + 16)
                    dve.wait_ge(sem("m_mm"), 9 * l + t + 3 + 1)
                    v = xres[:, s, :].rearrange("p (a b) -> p a b", a=2)
                    nc.vector.scalar_tensor_tensor(sx[:, :].rearrange("p (a b) -> p a b", a=2), v, ALPHA,
                                                   PS[:, bass.ds((t % 2) * 2, 2), :], ALU.mult, ALU.add).then_inc(sem("m_ps"), 1)
                    dve.wait_ge(sem("m_ps"), 9 * l + t + 2 + 1)
                    moments(dve, D, sx)
                    reciprocal_sd(dve, D, 18 * l + t)
                    affine(dve, D, 18 * l + t, s)

        def wide(x, n):
            return x.unsqueeze(len(x.shape)).broadcast_to(list(x.shape) + [n])

        def dve_route(dve, D, l):
            sc, sel, m, eq, oh1, oh2, A, pos, tmp = rt
            TR = nc.vector.tensor_reduce
            dve.wait_ge(sem("r_sig"), l + 1)
            D(TT(sel[:, :, :], sc[:, :, :], brt[:, :].unsqueeze(1).broadcast_to([P, NT, EXPERTS]), ALU.add))
            q = sel[:, :, :].rearrange("p t (g e) -> p (t g) e", e=PER_GROUP)
            r = [x[:, :, :].rearrange("p t g -> p (t g)") for x in rs]
            D(TT(r[0], q[:, :, 0], q[:, :, 1], ALU.max))
            D(TT(r[1], q[:, :, 0], q[:, :, 1], ALU.min))
            D(TT(r[2], q[:, :, 2], q[:, :, 3], ALU.max))
            D(TT(r[3], q[:, :, 2], q[:, :, 3], ALU.min))
            D(TT(r[4], r[0], r[2], ALU.max))
            D(TT(r[0], r[0], r[2], ALU.min))
            D(TT(r[1], r[1], r[3], ALU.max))
            D(TT(r[0], r[0], r[1], ALU.max))
            D(TT(rs[4][:, :, :], rs[4][:, :, :], rs[0][:, :, :], ALU.add))

            def first_max(dst, x, iota, n, work):
                D(TR(rk[0][:, :, :], x, AX.X, ALU.max))
                D(TT(dst, x, rk[0][:, :, 0:1].broadcast_to([P, NT, n]), ALU.is_equal))
                D(TT(work, dst, iota.unsqueeze(1).broadcast_to([P, NT, n]), ALU.mult))
                D(TR(rk[1][:, :, :], work, AX.X, ALU.max))
                D(TT(dst, work, rk[1][:, :, 0:1].broadcast_to([P, NT, n]), ALU.is_equal))

            i4, i16 = cst[:, C_IOTA4:C_IOTA4 + 4], cst[:, C_IOTA:C_IOTA + 16]
            first_max(rs[1][:, :, :], rs[4][:, :, :], i4, 4, rs[2][:, :, :])
            D(TS(rs[3][:, :, :], rs[1][:, :, :], 1.0, BIG, ALU.subtract, ALU.mult))
            mq = m[:, :, :].rearrange("p t (g e) -> p (t g) e", e=PER_GROUP)
            D(TT(mq, q, wide(r[1], PER_GROUP), ALU.mult))
            D(TT(mq, mq, wide(r[3], PER_GROUP), ALU.add))
            first_max(oh1[:, :, :], m[:, :, :], i16, 16, eq[:, :, :])
            D(mul_add(m[:, :, :], oh1[:, :, :], -3.0 * BIG, m[:, :, :]))
            first_max(oh2[:, :, :], m[:, :, :], i16, 16, eq[:, :, :])
            for k, oh in enumerate((oh1, oh2)):
                D(TT(eq[:, :, :], sc[:, :, :], oh[:, :, :], ALU.mult))
                D(TR(rk[2 + k][:, :, :], eq[:, :, :], AX.X, ALU.add))
            D(TT(rk[4][:, :, :], rk[2][:, :, :], rk[3][:, :, :], ALU.add))
            D(nc.vector.reciprocal(rk[4][:, :, :], rk[4][:, :, :]))
            for k in range(2):
                D(TT(gate[:, :, k:k + 1], rk[2 + k][:, :, :], rk[4][:, :, :], ALU.mult))
            for oh in (oh1, oh2):
                D(TT(oh[:, :, :], oh[:, :, :], wide(cst[:, C_VALID:C_VALID + NT], EXPERTS), ALU.mult))
            TT(A[:, :, :], oh1[:, :, :], oh2[:, :, :], ALU.add).then_inc(sem("r_chosen"), 1)
            dve.wait_ge(sem("r_count"), l + 1)
            D(nc.vector.memset(cum[:, 0, :], 0.0))
            for t in range(NT):
                D(TT(cum[:, t + 1, :], cum[:, t, :], PS[:, 1, t * EXPERTS:(t + 1) * EXPERTS], ALU.add))
            D(TS(cnti[:, :], cum[:, NT, :], 127.0, None, ALU.add))
            D(TS(cnti[:, :], cnti[:, :], 7, None, ALU.logical_shift_right))
            D(nc.vector.tensor_copy(cnt[0][:, :], cnti[:, :]))
            D(TS(cnt[1][:, :], cnt[0][:, :], 1.0, None, ALU.max))
            D(nc.vector.tensor_tensor_scan(cnt[2][:, :], cst[:, C_ONE:C_ONE + EXPERTS], cnt[1][:, :], 0.0, ALU.mult, ALU.add))
            D(TT(cnt[3][:, :], cnt[2][:, :], cnt[1][:, :], ALU.subtract))
            D(nc.vector.tensor_copy(plan[:, 0:16], cnt[1][:, :]))
            D(nc.vector.tensor_copy(plan[:, 16:32], cnt[3][:, :]))
            D(nc.vector.tensor_copy(plan[:, 32:48], cnt[2][:, :]))
            D(TS(cnt[0][:, :], cnt[2][:, :], -1.0, MAX_BLOCKS + 1.0, ALU.mult, ALU.add))
            D(nc.vector.tensor_copy(plan[:, 48:49], cnt[0][:, EXPERTS - 1:EXPERTS]))
            D(TT(pos[:, :, :], cum[:, 0:NT, :], PS[:, 0, 0:NT * EXPERTS].rearrange("p (t e) -> p t e", e=EXPERTS), ALU.add))
            D(TS(cnt[0][:, :], cnt[3][:, :], 128.0, None, ALU.mult))
            D(TT(pos[:, :, :], pos[:, :, :], cnt[0][:, :].unsqueeze(1).broadcast_to([P, NT, EXPERTS]), ALU.add))
            for k, oh in enumerate((oh1, oh2)):
                D(TT(tmp[:, :, :], pos[:, :, :], oh[:, :, :], ALU.mult))
                D(TR(rk[k][:, :, :], tmp[:, :, :], AX.X, ALU.add))
                D(nc.vector.tensor_copy(dest[:, :, k:k + 1], rk[k][:, :, :]))
            D(nc.vector.tensor_copy(tokid[:, :], cst[:, C_TOK:C_TOK + NT]))
            dve.sem_inc(sem("r_plan"), 1)

        def act_route(act, A, l):
            act.wait_ge(sem("m_lg"), 1 + 9 * l + NT)
            nc.scalar.activation(rt[0][:, :, :], logits[:, :, :], ACT.Sigmoid).then_inc(sem("r_sig"), 1)

        def pe_route(pe, l):
            pe.wait_ge(sem("r_chosen"), l + 1)
            a = rt[6][:, :, :].rearrange("p t e -> p (t e)")
            nc.tensor.matmul(PS[:, 0, 0:NT * EXPERTS], tri, a, start=True, stop=True)
            nc.tensor.matmul(PS[:, 1, 0:NT * EXPERTS], ones, a, start=True, stop=True).then_inc(sem("r_count"), 1)

        def pool_route(pool, G, l):
            if l == 0:
                G(nc.gpsimd.memset(zid[:, :], 0))
                pool.dma_start(tokbuf.rearrange("(p n) a -> p (n a)", p=P), zid[:, :]).then_inc(sem("r_zeroed"), 16)
                pool.wait_ge(sem("r_zeroed"), 16)
            pool.wait_ge(sem("r_plan"), l + 1)
            for t in range(NT):
                n = P if t < NT - 1 else SAMPLE
                for k in range(2):
                    pool.indirect_dma_start(out=tokbuf, out_offset=bass.IndirectOffsetOnAxis(ap=dest[0:n, t, k:k + 1].bitcast(U32), axis=0),
                                            in_=tokid[0:n, t:t + 1], in_offset=None).then_inc(sem("r_rows"), 16)
            pool.wait_ge(sem("r_rows"), (l + 1) * 16 * 2 * NT)

        def expert_loop(eng, l, body, end=None):
            with eng.Fori(0, EXPERTS // 2) as i:
                for s in range(2):
                    e = i * 2 + s
                    n = eng.value_load(plan[0:1, bass.ds(e, 1)], min_val=1, max_val=NT)
                    b0 = eng.value_load(plan[0:1, bass.ds(e + EXPERTS, 1)], min_val=0, max_val=MAX_BLOCKS - 1)
                    if body_start := body.get("start"):
                        body_start(i, s)
                    with eng.Fori(0, n) as j:
                        b = nc.s_assert_within(b0 + j, 0, MAX_BLOCKS - 1, skip_runtime_bounds_check_because="first block plus count is at most the total")
                        body["block"](s, b)
                    if body_end := body.get("end"):
                        body_end(i, s, b0 + n)

        def sp_experts(sp, l):
            with sp.Fori(0, EXPERTS // 2 - 1) as i:
                for s in range(2):
                    sp.wait_ge(sem("e_free"), EXPERTS * l + i * 2 + s + 1)
                    load_expert(sp, i * 2 + (2 + s + l * EXPERTS), s)

        def pool_experts(pool, l):
            u = f"e{l}_"
            pool.wait_ge(sem("m_kept"), l + 1)
            total = pool.value_load(plan[0:1, 47:48], min_val=EXPERTS, max_val=MAX_BLOCKS)
            with pool.Fori(0, total + 1) as b:
                pool.dma_start(idx[:, :], tokbuf[rows(b), :]).then_inc(sem(u + "idx"), 16)
                pool.wait_ge(sem(u + "idx"), b * 16 + 16)
                pool.wait_ge(sem(u + "tp"), 1 + b)
                part(pool)
                pool.indirect_dma_start(out=gx, out_offset=None, in_=xm[l],
                                        in_offset=bass.IndirectOffsetOnAxis(ap=idx[:, 0:1].bitcast(U32), axis=0)
                                        ).then_inc(sem(u + "gx"), 16)
                pool.wait_ge(sem(u + "gx"), b * 16 + 16)
                part(pool)
            if l == 0:
                nc.gpsimd.memset(zrow, 0.0).then_inc(sem("zrow"), 1)
                pool.wait_ge(sem("zrow"), 1)
                rest = pool.value_load(plan[0:1, 48:49], min_val=1, max_val=MAX_BLOCKS + 1 - EXPERTS)
                with pool.Fori(0, rest) as n:
                    b = nc.s_assert_within(total + n, 0, MAX_BLOCKS, skip_runtime_bounds_check_because="total and rest are MAX_BLOCKS + 1")
                    pool.dma_start(yb[rows(b), :], zrow).then_inc(sem("yb_rest"), 16)
                pool.wait_ge(sem("yb_rest"), rest * 16)
                part(pool)

        def pe_experts(pe, l):
            u = f"e{l}_"
            pe.wait_ge(sem("r_plan"), l + 1)

            def transpose(b):
                pe.wait_ge(sem(u + "gx"), b * 16 + 16)
                pe.wait_ge(sem(u + "xtb"), b)
                for k in range(KD):
                    ins = nc.tensor.transpose(PS[:, k // 4, k % 4 * P:k % 4 * P + P], gx[:, k * P:(k + 1) * P], ident)
                ins.then_inc(sem(u + "tp"), 1)

            transpose(0)

            def start(i, s):
                pe.wait_ge(sem(f"e_in_w1_{s}"), 256 * l + i * 32 + 32)
                pe.wait_ge(sem(f"e_in_w2_{s}"), 128 * l + i * 16 + 16)
                part(pe)

            def block_(s, b):
                pe.wait_ge(sem(u + "xtb"), b + 1)
                for f in range(4):
                    pe.wait_ge(sem(u + "ht"), b * 4 + f + 1)
                    for half in range(2):
                        for k in range(KD):
                            c = half * F_EXP + f * P
                            ins = nc.tensor.matmul(PS[:, 2 + f % 2, half * P:(half + 1) * P], w1[s][:, k, c:c + P], xtb[:, k, :],
                                                   start=(k == 0), stop=(k == KD - 1))
                    ins.then_inc(sem(u + "h"), 1)
                transpose(b + 1)
                pe.wait_ge(sem(u + "y_out"), 1 + b)
                for f in range(4):
                    pe.wait_ge(sem(u + "ht"), b * 4 + f + 1 + 2)
                    for n in range(2):
                        ins = nc.tensor.matmul(PS[:, 4 + n, :], ht[:, f, :], w2[:, s, f, n * 512:(n + 1) * 512],
                                               start=(f == 0), stop=(f == 3))
                ins.then_inc(sem(u + "y"), 1)

            expert_loop(pe, l, {"start": start, "block": block_})

        def act_experts(act, l):
            u = f"e{l}_"
            act.wait_ge(sem("r_plan"), l + 1)

            def stage(b):
                act.wait_ge(sem(u + "tp"), 1 + b + 1)
                nc.scalar.activation(xtb[:, :, :].rearrange("p (a b) c -> p a (b c)", a=2), PS[:, 0:2, :], ACT.Copy).then_inc(sem(u + "xtb"), 1)

            stage(0)

            def block_(s, b):
                for f in range(4):
                    act.wait_ge(sem(u + "h"), b * 4 + f + 1)
                    nc.scalar.activation(sg[:, f, :], PS[:, 2 + f % 2, 0:P], ACT.Silu).then_inc(sem(u + "sg"), 1)
                stage(b + 1)
                act.wait_ge(sem(u + "y_out"), 1 + b + 1)
                act.dma_start(yb[rows(b), :], ysb[:, :]).then_inc(sem(u + "yb"), 16)

            def end(i, s, blocks):
                act.sem_inc(sem("e_free"), 1)

            expert_loop(act, l, {"block": block_, "end": end})

        def dve_experts(dve, l):
            u = f"e{l}_"
            dve.sem_inc(sem(u + "ht"), 2)

            def block_(s, b):
                for f in range(4):
                    dve.wait_ge(sem(u + "sg"), b * 4 + f + 1)
                    TT(ht[:, f, :], sg[:, f, :], PS[:, 2 + f % 2, P:2 * P], ALU.mult).then_inc(sem(u + "ht"), 1)
                dve.wait_ge(sem(u + "y"), b + 1)
                dve.wait_ge(sem(u + "yb"), 16 + b * 16)
                nc.vector.tensor_copy(ysb[:, :].rearrange("p (a b) -> p a b", a=2), PS[:, 4:6, :]).then_inc(sem(u + "y_out"), 1)

            expert_loop(dve, l, {"block": block_})

        def sp_ffn(sp, l):
            out = io["x1"] if l == 0 else io["y"]

            def store(t, s):
                sp.wait_ge(sem("n_ln"), 18 * l + 9 + t + 1)
                sp.dma_start(out[rows(t), :], xn[:, s, :]).then_inc(sem(f"n_out{s}"), 16)

            with sp.Fori(0, 2) as i:
                for s in range(3):
                    store(i * 3 + s, s)
                    sp.dma_start(xres[:, s, :], xm[l][rows(i * 3 + s + 3), :]).then_inc(sem(f"n_in_x{s}"), 16)
            for s in range(3):
                store(6 + s, s)
            for s in range(3):
                sp.wait_ge(sem(f"n_out{s}"), 16 + 96 * l + 96)

        def pool_ffn(pool, l):
            u = f"f{l}_"
            total = pool.value_load(plan[0:1, 47:48], min_val=EXPERTS, max_val=MAX_BLOCKS)
            pool.wait_ge(sem(f"e{l}_yb"), 16 + total * 16)
            pool.wait_ge(sem(f"e{l}_xtb"), total + 1)
            part(pool)

            def gather(t):
                for k, dst in enumerate((y1, y2)):
                    pool.indirect_dma_start(out=dst[:, t % 3, :], out_offset=None, in_=yb,
                                            in_offset=bass.IndirectOffsetOnAxis(ap=dest[:, t, k:k + 1].bitcast(U32), axis=0)
                                            ).then_inc(sem(f"f_g{t % 3}"), 16)

            for t in range(3):
                gather(t)
            for t in range(NT):
                if t + 3 < NT:
                    pool.wait_ge(sem("f_y"), 9 * l + t + 1)
                    gather(t + 3)
                pool.wait_ge(sem("f_xg"), 9 * l + t + 1)
                nc.gpsimd.tensor_tensor(xn[:, t % 3, :], xn[:, t % 3, :], lnb, ALU.add).then_inc(sem("n_ln"), 1)

        def pe_ffn(pe, l):
            u = f"f{l}_"
            if l == 0:
                with pe.Fori(0, 3) as i:
                    for s in range(3):
                        t = i * 3 + s
                        pe.wait_ge(sem("n_ln"), 18 * l + 9 + t + 1)
                        pe.wait_ge(sem("n_tpo"), 1 + 9 + t)
                        pe_transpose(xn[:, s, :])

        def tiles(eng, body):
            body(0, 0, 0, False)
            with eng.Fori(0, 2) as i:
                body(i * 3 + 1, i, 1, False)
                body(i * 3 + 2, i, 2, False)
                body(i * 3 + 3, i + 1, 0, False)
            body(7, 2, 1, False)
            body(8, 2, 2, True)

        def act_ffn(act, l):
            n0 = 18 * l + 9

            def weigh(t, i, s):
                act.wait_ge(sem(f"f_g{s}"), 96 * l + i * 32 + 32)
                part(act)
                nc.scalar.activation(y1[:, s, :], y1[:, s, :], ACT.Copy, scale=gate[:, t, 0:1]).then_inc(sem("f_y1"), 1)

            def channel_major(t):
                if l == 0:
                    act.wait_ge(sem("n_tp"), 9 + t + 1)
                    part(act)
                    nc.scalar.activation(xT[:, :, rows(t)], PS[:, 4:6, :].rearrange("p a (b c) -> p (a b) c", c=P), ACT.Copy).then_inc(sem("n_tpo"), 1)

            def body(t, i, s, last):
                root(act, n0 + t)
                if not last:
                    weigh(t + 1, i + (s == 2), (s + 1) % 3)
                if l == 0:
                    act.wait_ge(sem("n_tp"), t + (9 - 3 + 1))
                shift_scale(act, n0 + t, 96 * l + 48 + i * 16, s, fx[s])
                if not isinstance(t, int) or t > 0:
                    channel_major(t - 1)

            weigh(0, 0, 0)
            tiles(act, body)
            channel_major(8)

        def dve_ffn(dve, D, l):
            n0 = 18 * l + 9
            dve.wait_ge(sem("n_in_w"), 96 * l + 96)

            def gain(t, s):
                dve.wait_ge(sem("n_xh"), n0 + t + 1)
                part(dve)
                TT(xn[:, s, :], xn[:, s, :], lng, ALU.mult).then_inc(sem("f_xg"), 1)

            def body(t, i, s, last):
                dve.wait_ge(sem("f_y1"), 9 * l + t + 1)
                part(dve)
                mul_add(fx[s], y2[:, s, :], gate[:, t, 1:2], y1[:, s, :]).then_inc(sem("f_y"), 1)
                dve.wait_ge(sem("f_y"), 9 * l + t + 1)
                dve.wait_ge(sem(f"n_in_x{s}"), 96 * l + 48 + i * 16 + 16)
                D(mul_add(fx[s], xres[:, s, :], ALPHA, fx[s]))
                moments(dve, D, fx[s])
                if not isinstance(t, int) or t > 0:
                    gain(t - 1, (s + 2) % 3)
                reciprocal_sd(dve, D, n0 + t)

            with D.rounds(0, 4, 1):
                body(0, 0, 0, False)
            with dve.Fori(0, 2) as i, D.rounds(i, 12, 2):
                body(i * 3 + 1, i, 1, False)
                body(i * 3 + 2, i, 2, False)
                body(i * 3 + 3, i + 1, 0, False)
            body(7, 2, 1, False)
            body(8, 2, 2, True)
            gain(8, 2)

        def sp_odd(sp):
            w_in = io["w_in_odd"].rearrange("(k p) n -> p k n", p=P)
            for dst, src in ((odp[:], io["od_pack"]), (gqk[:], io["gqk"]), (cosq[:], io["cosq"]), (sinq[:], io["sinq"]),
                             (wuv[:], io["wuv"].rearrange("(k p) n -> p k n", p=P)), (pages[:], io["page_table"])):
                sp.dma_start(dst, src).then_inc(sem("in_odd"), 16)
            with sp.Fori(0, 2) as i:
                for s in range(2):
                    for p in range(2):
                        sp.wait_ge(sem("o_mm"), 1 + i * 12 + s * 6 + p * 3)
                        part(sp)
                        sp.dma_start(W4[:, 2 * s + p, :, :], w_in[:, :, bass.ds(i * 2 * P + s * P + (1 - p) * 512, P)]
                                     ).then_inc(sem(f"in_w_{2 * s + p}"), 16)
            for q in range(6):
                sp.wait_ge(sem("o_mm"), 1 + 24 + 3 * q)
                src = w_in[:, :, 1024 + q * P:1024 + (q + 1) * P] if q < 5 else io["w_kpe"].rearrange("(k p) n -> p k n", p=P)
                sp.dma_start(W4[:, q % 4, :, 0:P if q < 5 else 2 * ROPE], src).then_inc(sem(f"in_w_{q % 4}"), 16)

        def pe_odd(pe):
            pe.sem_inc(sem("o_mm"), 9)
            pe.wait_ge(sem("n_tpo"), 1 + 2 * NT)

            def chunks(slot, n0, m=P, before=0):
                for c in range(NC):
                    pe.wait_ge(sem("o_out"), before + n0 + c + 1)
                    for k in range(KD):
                        ins = nc.tensor.matmul(PS[0:m, (n0 + c) % 6, 0:CW], W4[:, slot, k, 0:m], xT[:, k, c * CW:(c + 1) * CW],
                                               start=(k == 0), stop=(k == KD - 1))
                    ins.then_inc(sem("o_mm"), 1)

            with pe.Fori(0, 2) as i:
                for slot in range(4):
                    pe.wait_ge(sem(f"in_w_{slot}"), 64 + i * 16 + 16)
                    part(pe)
                    chunks(slot, 3 * slot, before=i * 12)
            for q in range(6):
                pe.wait_ge(sem(f"in_w_{q % 4}"), 64 + 48 + 16 * (q // 4))
                chunks(q % 4, 24 + 3 * q, P if q < 5 else 2 * ROPE)
            for q in range(5):
                pe.wait_ge(sem("o_sq"), q + 1)
                for c in range(NC):
                    ins = nc.tensor.matmul(PS[:, (0 if q < 3 else 3) + c, 0:CW], ones, sqb[:, q % 2, c * CW:(c + 1) * CW],
                                           start=(q in (0, 3)), stop=(q in (2, 4)))
                ins.then_inc(sem("o_ss"), 1)
            pe.wait_ge(sem("o_conv"), 1 + 5)
            pe.wait_ge(sem("o_rms"), 1)
            for g in range(4):
                for c in range(NC):
                    ins = nc.tensor.matmul(PS[:, c, 0:CW], ones, uc[:, g, c * CW:(c + 1) * CW], start=(g == 0), stop=(g == 3))
            ins.then_inc(sem("o_ss"), 1)

            def rotary_part(n):
                a, c = divmod(n, NC)
                if n >= 2:
                    pe.wait_ge(sem("a_pe"), n - 1)
                for w, half in ((wqp, 0), (wqs, 1)):
                    for k in range(3):
                        ins = nc.tensor.matmul(PS[:, 3 + 2 * (n % 2) + half, 0:CW], w[:, k, a * P:(a + 1) * P], qT[:, k, c * CW:(c + 1) * CW],
                                               start=(k == 0), stop=(k == 2))
                ins.then_inc(sem("a_pemm"), 1)

            pe.wait_ge(sem("in_wqr"), 32)
            pe.wait_ge(sem("o_scaled"), 1)
            pe.wait_ge(sem("o_rms"), 2)
            for n in range(3):
                rotary_part(n)
            pe.wait_ge(sem("o_d"), 4)
            for g in range(4):
                pe.wait_ge(sem("o_sq"), 5 + g + 1)
                for c in range(NC):
                    ins = nc.tensor.matmul(PS[:, c, 0:CW], ones, csq[:, g % 2, c * CW:(c + 1) * CW], start=(g == 0), stop=(g == 3))
                ins.then_inc(sem("o_ss"), 1)
            for n in range(3, 6):
                rotary_part(n)

        def act_odd(act, A):
            AC = nc.scalar.activation
            act.sem_inc(sem("o_out"), 6)
            act.wait_ge(sem("o_zero"), 1)
            with act.Fori(0, 4) as g:
                act.wait_ge(sem("o_prods"), 1 + g)
                for p, dst, fn in ((0, zs, ACT.Sigmoid), (1, za, ACT.Copy)):
                    for c in range(NC):
                        act.wait_ge(sem("o_mm"), 1 + g * 6 + 9 + 3 * p + c + 1)
                        AC(dst[:, c * CW:(c + 1) * CW], PS[:, 3 * p + c, 0:CW], fn).then_inc(sem("o_out"), 1)
                act.wait_ge(sem("o_prod"), g + 1)
                act.wait_ge(sem("o_pc"), 1 + g)
                part(act)
                for k in range(OTHER_TAPS):
                    tap = CONV_C - OTHER_TAPS + k
                    AC(wo[:, k, :], hp[:, g % 2, tap:tap + PROMPT], ACT.Copy, scale=odp[:, g, tap:tap + 1]).then_inc(sem("o_tap"), 1)
            for q in range(6):
                for c in range(NC):
                    cc = slice(c * CW, (c + 1) * CW)
                    act.wait_ge(sem("o_mm"), 1 + 9 + 24 + 3 * q + c + 1)
                    m, dst = (P, qT[:, q, cc]) if q < 3 else (P, ckvT[:, q - 3, cc]) if q < 5 else (2 * ROPE, kraw[:, cc])
                    AC(dst, PS[0:m, 3 * (q % 2) + c, 0:CW], ACT.Copy).then_inc(sem("o_out"), 1)
            act.wait_ge(sem("o_out"), 6 + 42)
            for q in range(5):
                if q >= 2:
                    act.wait_ge(sem("o_ss"), q - 1)
                AC(sqb[:, q % 2, :], qT[:, q, :] if q < 3 else ckvT[:, q - 3, 0:TOK], ACT.Square).then_inc(sem("o_sq"), 1)
            for n, (size, last) in enumerate(((Q_RANK, 3), (KV_RANK, 5))):
                act.wait_ge(sem("o_ss"), last)
                if n == 0:
                    act.wait_ge(sem("o_ss"), 5)
                AC(sqb[:, n, :].rearrange("p (c w) -> p c w", c=NC), PS[:, 3 * n:3 * n + 3, 0:CW], ACT.Sqrt, scale=1.0 / size, bias=eps6[:, :]).then_inc(sem("o_rms"), 1)
            for g in range(4):
                act.wait_ge(sem("o_d"), g + 1)
                if g >= 2:
                    act.wait_ge(sem("o_ss"), 6 + g - 1)
                AC(csq[:, g % 2, :], uc[:, g, :], ACT.Square).then_inc(sem("o_sq"), 1)
            act.wait_ge(sem("o_ss"), 6 + 4)
            act.wait_ge(sem("o_scaled"), 1)
            AC(sqb[:, 0, :].rearrange("p (c w) -> p c w", c=NC), PS[:, 0:3, 0:CW], ACT.Sqrt, scale=1.0 / 512, bias=epsc[:, :]).then_inc(sem("o_rms"), 1)
            for g in range(4):
                act.wait_ge(sem("o_y"), g + 1 if g < 2 else 4)
                AC(yT[:, g, 0:TOK], uc[:, g, :], ACT.Silu, scale=odp[:, g, OD_G:OD_G + 1], bias=odp[:, g, OD_LB:OD_LB + 1]).then_inc(sem("o_yc"), 1)

        def pool_odd(pool, G):
            CP, T2 = nc.gpsimd.tensor_copy, nc.gpsimd.tensor_tensor
            pool.wait_ge(sem("in_odd"), 96)
            with pool.Fori(0, 2) as i, G.rounds(i, 2 * (3 + OTHER_TAPS - 2), 2):
                for j in range(2):
                    g = i * 2 + j
                    pool.wait_ge(sem("o_out"), i * 12 + (j * 6 + 12))
                    pool.wait_ge(sem("o_conv"), 1 + i * 2 + j)
                    part(pool)
                    T2(hp[:, j, 30:30 + PROMPT], za[:, 0:PROMPT], zs[:, 0:PROMPT], ALU.mult).then_inc(sem("o_prod"), 1)
                    G(CP(hs[:, j, :, 0:30], odp[:, g, OD_S:OD_N].rearrange("p (b t) -> p b t", t=30)))
                    T2(hs[:, j, :, 30:34], smp(za), smp(zs), ALU.mult).then_inc(sem("o_prods"), 1)
                    pool.wait_ge(sem("o_prods"), 1 + i * 2 + j + 1)
                    part(pool)
                    G(CP(osp[:, g, :], hp[:, j, PROMPT:PROMPT + 30]))
                    G(CP(odp[:, g, OD_S:OD_N].rearrange("p (b t) -> p b t", t=30), hs[:, j, :, STEP:STEP + 30]))
                    for k in range(1, OTHER_TAPS):
                        pool.wait_ge(sem("o_tap"), i * 2 * OTHER_TAPS + (j * OTHER_TAPS + k + 1))
                        part(pool)
                        ins = T2(lngb[:, j, :], wo[:, 0, :] if k == 1 else lngb[:, j, :], wo[:, k, :], ALU.add)
                        if k < OTHER_TAPS - 1:
                            G(ins)
                    ins.then_inc(sem("o_pc"), 1)
            pool.dma_start(io["odd_states"][:, :, 0:30], osp[:, :, :]).then_inc(sem("out_odd"), 16)
            pool.dma_start(io["odd_states"][:, :, 30:270], odp[:, :, OD_S:OD_N]).then_inc(sem("out_odd"), 16)
            pool.wait_ge(sem("o_scaled"), 3)
            pool.dma_start(io["out_ckvT"].rearrange("(k p) t -> p k t", p=P), ckvT[:, :, 0:TOK]).then_inc(sem("out_odd"), 16)
            pool.dma_start(io["out_kpeT"], kpeT[:, :]).then_inc(sem("out_odd"), 16)
            pool.wait_ge(sem("out_odd"), 64)

        def dve_odd(dve, D):
            dve.sem_inc(sem("o_conv"), 1)
            dve.wait_ge(sem("in_odd"), 96)
            D(nc.vector.memset(eps6[:, :], 1e-6))
            D(nc.vector.memset(ckvT[:, :, TOK:TOKP], 0.0))
            for j in range(2):
                D(nc.vector.memset(hp[:, j, 0:30], 0.0))
            dve.sem_inc(sem("o_zero"), 1)
            PR = slice(0, PROMPT)
            last = CONV_C - OTHER_TAPS - 1
            with dve.Fori(0, 4) as g, D.rounds(g, 4 + 1 + 1 + 1 + last, 4):
                j = g % 2
                dve.wait_ge(sem("o_prods"), 1 + g + 1)
                part(dve)
                for t in range(STEP):
                    D(TT(hw[:, t, :, :], hs[:, j, :, t:t + CONV_C], odp[:, g, 0:CONV_C].unsqueeze(1).broadcast_to([P, SEQS, CONV_C]), ALU.mult))
                D(nc.vector.tensor_reduce(uc[:, g, PROMPT:TOK].rearrange("p (b t) -> p t b", t=STEP), hw[:, :, :, :], AX.X, ALU.add))
                D(TS(uc[:, g, PROMPT:TOK], uc[:, g, PROMPT:TOK], odp[:, g, OD_B:OD_B + 1], None, ALU.add))
                D(TS(uc[:, g, PR], hp[:, j, PR], odp[:, g, 0:1], odp[:, g, OD_B:OD_B + 1], ALU.mult, ALU.add))
                for k in range(1, last + 1):
                    D(mul_add(uc[:, g, PR], hp[:, j, k:k + PROMPT], odp[:, g, k:k + 1], uc[:, g, PR]))
                dve.wait_ge(sem("o_pc"), 1 + g + 1)
                TT(uc[:, g, PR], uc[:, g, PR], lngb[:, j, :], ALU.add).then_inc(sem("o_conv"), 1)

            def rotary_part(n):
                a, c = divmod(n, NC)
                cc = slice(c * CW, (c + 1) * CW)
                bank = 3 + 2 * (n % 2)
                dve.wait_ge(sem("a_pemm"), n + 1)
                D(TT(peT[:, a, cc], PS[:, bank, 0:CW], cosq[:, cc], ALU.mult))
                D(TT(rtmp[:, :], PS[:, bank + 1, 0:CW], sinq[:, cc], ALU.mult))
                TT(peT[:, a, cc], peT[:, a, cc], rtmp[:, :], ALU.add).then_inc(sem("a_pe"), 1)

            def invert(slot, c):
                x = sqb[:, slot, c * CW:(c + 1) * CW]
                D(nc.vector.reciprocal(x, x))

            def scale(x, g):
                return nc.vector.scalar_tensor_tensor(x, x, gqk[:, g:g + 1], sqb[:, 0 if g < 3 else 1, :], ALU.mult, ALU.mult)

            dve.wait_ge(sem("o_rms"), 1)
            for c in range(NC):
                invert(0, c)
            for q in range(2):
                D(scale(qT[:, q, :], q))
            scale(qT[:, 2, :], 2).then_inc(sem("o_scaled"), 1)
            dve.wait_ge(sem("o_ss"), 6)
            for g in range(4):
                v = uc[:, g, :].rearrange("p (c w) -> p c w", c=NC)
                nc.vector.scalar_tensor_tensor(v, PS[:, 0:3, 0:CW], -1.0 / 512, v, ALU.mult, ALU.add).then_inc(sem("o_d"), 1)
            dve.wait_ge(sem("o_rms"), 2)
            for n in range(3):
                rotary_part(n)
                invert(1, n)
            D(scale(ckvT[:, 0, 0:TOK], 3))
            scale(ckvT[:, 1, 0:TOK], 4).then_inc(sem("o_scaled"), 1)
            D(TT(kpeT[:, :], kraw[0:ROPE, :], cosq[0:ROPE, :], ALU.mult))
            D(TT(kraw[0:ROPE, :], kraw[ROPE:2 * ROPE, :], sinq[ROPE:2 * ROPE, :], ALU.mult))
            TT(kpeT[:, :], kpeT[:, :], kraw[0:ROPE, :], ALU.add).then_inc(sem("o_scaled"), 1)
            dve.wait_ge(sem("o_scaled"), 3)
            D(nc.vector.tensor_copy(kpeS[:, :], kpeT[:, PROMPT:TOK]))
            rotary_part(3)
            dve.wait_ge(sem("o_rms"), 3)
            invert(0, 0)
            rotary_part(4)
            invert(0, 1)
            rotary_part(5)
            invert(0, 2)
            for g in range(4):
                TT(uc[:, g, :], uc[:, g, :], sqb[:, 0, :], ALU.mult).then_inc(sem("o_y"), 1)

        def sp_prompt(sp):
            sp.wait_ge(sem("o_pc"), 1 + 4)
            load_wo(sp, 1)
            sp.wait_ge(sem("o_mm"), 1 + 9 + 42)
            for dst, name in ((wqp, "wqp"), (wqs, "wqs")):
                sp.dma_start(dst[:], io[name].rearrange("(k p) n -> p k n", p=P)).then_inc(sem("in_wqr"), 16)
            wq, wk = io["wqn"].rearrange("(k p) n -> p k n", p=P), io["wuk"].rearrange("(k p) n -> p k n", p=P)
            with sp.Fori(0, 2) as a:
                for pp in range(2):
                    sp.wait_ge(sem("a_proj"), 1 + a * 2 + pp)
                    part(sp)
                    sp.dma_start(wqn[:, pp, :, :], wq[:, :, bass.ds(a * 2 * P + pp * P, P)]).then_inc(sem(f"in_wq{pp}"), 16)
                    sp.dma_start(wuk[:, pp, :, :], wk[:, :, bass.ds(a * 2 * P + pp * P, P)]).then_inc(sem(f"in_wq{pp}"), 16)

        def pe_prompt(pe):
            pe.wait_ge(sem("o_scaled"), 3)
            pe.wait_ge(sem("o_rms"), 3)
            pe.wait_ge(sem("out_odd"), 64)
            pe.wait_ge(sem("a_pe"), 6)
            pe.sem_inc(sem("a_yt"), 2)

            def scores(u, u0):
                t, j = divmod(u, 2)
                if u >= 2:
                    pe.wait_ge(sem("a_p"), u0 + u - 1)
                for c in range(0, (t + 1) * P, 512):
                    w = min(512, (t + 1) * P - c)
                    ins = nc.tensor.matmul(PS[:, u % 2 * 2 + c // 512, 0:w], Q[j][:, t * P:(t + 1) * P], K[j][:, c:c + w], start=True, stop=True)
                ins.then_inc(sem("a_s"), 1)

            def turn(u, u0):
                pe.wait_ge(sem("a_w"), u0 + u + 1)
                pe.wait_ge(sem("a_pt"), 1 + u0 + u)
                for b in range(u // 2 + 1):
                    ins = nc.tensor.transpose(PS[:, 4 + b // 4, b % 4 * P:b % 4 * P + P], Pb[u % 2][:, b * P:(b + 1) * P], ident)
                ins.then_inc(sem("a_t"), 1)

            def weigh(u, u0, t0):
                t, j = divmod(u, 2)
                pe.wait_ge(sem("a_pt"), 1 + u0 + u + 1)
                if j == 0:
                    pe.wait_ge(sem("a_yt"), t0 + t + 1)
                for b in range(t + 1):
                    ins = nc.tensor.matmul(PS[V_DIM * j:V_DIM * (j + 1), 6 + t % 2, 0:P], V[:, b, V_DIM * j:V_DIM * (j + 1)], PT[u % 2][:, b, :],
                                           start=(b == 0), stop=(b == t))
                ins.then_inc(sem("a_v"), 1)

            with pe.Fori(0, 2) as a:
                for pp in range(2):
                    u0, t0 = a * 32 + pp * 16, a * 16 + pp * 8
                    pe.wait_ge(sem(f"in_wq{pp}"), a * 32 + 32)
                    for c in range(NC):
                        for k in range(3):
                            nc.tensor.matmul(PS[:, c, 0:CW], wqn[:, pp, k, :], qT[:, k, c * CW:(c + 1) * CW], start=(k == 0), stop=(k == 2))
                    for c in range(2):
                        for k in range(2):
                            ins = nc.tensor.matmul(PS[:, 3 + c, :], wuk[:, pp, k, :], ckvT[:, k, c * 512:(c + 1) * 512], start=(k == 0), stop=(k == 1))
                    ins.then_inc(sem("a_proj"), 1)
                    pe.wait_ge(sem("a_yt"), t0 + 2)
                    part(pe)
                    for t in range(8):
                        for k in range(2):
                            ins = nc.tensor.matmul(PS[:, 5 + t // 4, t % 4 * P:t % 4 * P + P], ckvT[:, k, t * P:(t + 1) * P],
                                                   wuv[:, k, bass.ds(a * 4 * V_DIM + pp * 2 * V_DIM, 2 * V_DIM)], start=(k == 0), stop=(k == 1))
                    ins.then_inc(sem("a_vmm"), 1)
                    pe.wait_ge(sem("a_qk"), a * 4 + pp * 2 + 2)
                    scores(0, u0)
                    for u in range(18):
                        if u + 1 < 16:
                            scores(u + 1, u0)
                        if 0 <= u - 1 < 16:
                            turn(u - 1, u0)
                        if 0 <= u - 2 < 16:
                            weigh(u - 2, u0, t0)

        def act_prompt(act, A):
            AC = nc.scalar.activation
            act.wait_ge(sem("out_odd"), 64)
            for j in range(2):
                A(AC(K[j][NOPE:QK, :], kpeT[:, 0:PROMPT], ACT.Copy))

            def expo(u, u0):
                n = (u // 2 + 1) * P
                act.wait_ge(sem("a_m"), u0 + u + 1)
                if u >= 2:
                    act.wait_ge(sem("a_t"), u0 + u - 1)
                AC(Pb[u % 2][:, 0:n], PS[:, u % 2 * 2:u % 2 * 2 + 2, :].rearrange("p a b -> p (a b)")[:, 0:n], ACT.Exp, scale=SCALE,
                   bias=nms[:, u % 2:u % 2 + 1], accum_out=den[:, u % 2:u % 2 + 1]).then_inc(sem("a_p"), 1)

            def stage(u, u0):
                n = u // 2 + 1
                act.wait_ge(sem("a_t"), u0 + u + 1)
                AC(PT[u % 2][:, 0:n, :], PS[:, 4:6, :].rearrange("p a (b c) -> p (a b) c", c=P)[:, 0:n, :], ACT.Copy).then_inc(sem("a_pt"), 1)

            def result(t, a, pp, u0):
                act.wait_ge(sem("a_v"), u0 + 2 * t + 2)
                part(act)
                AC(yT[:, a * 2 + (4 + pp), t * P:(t + 1) * P], PS[:, 6 + t % 2, 0:P], ACT.Copy).then_inc(sem("a_yt"), 1)

            with act.Fori(0, 2) as a, A.rounds(a, 12, 2):
                for pp in range(2):
                    u0 = a * 32 + pp * 16
                    act.wait_ge(sem("a_proj"), 1 + a * 2 + pp + 1)
                    for j in range(2):
                        for c in range(NC):
                            A(AC(Q[j][0:NOPE, c * CW:(c + 1) * CW], PS[NOPE * j:NOPE * (j + 1), c, 0:CW], ACT.Copy))
                    for j in range(2):
                        AC(K[j][0:NOPE, :].rearrange("p (a b) -> p a b", a=2), PS[NOPE * j:NOPE * (j + 1), 3:5, :], ACT.Copy).then_inc(sem("a_k"), 1)
                    act.wait_ge(sem("a_k"), a * 4 + pp * 2 + 2)
                    act.sem_inc(sem("a_qk"), 1)
                    expo(0, u0)
                    for u in range(19):
                        if u + 1 < 16:
                            expo(u + 1, u0)
                        if u - 3 >= 0 and (u - 3) % 2 == 1:
                            result((u - 3) // 2, a, pp, u0)
                        if 0 <= u - 1 < 16:
                            stage(u - 1, u0)

        def dve_prompt(dve, D):
            dve.wait_ge(sem("a_pe"), 6)

            def maximum(u, u0):
                t = u // 2
                bank, col = u % 2 * 2 + t // 4, t % 4 * P
                s_ = PS[:, u % 2 * 2:u % 2 * 2 + 2, :].rearrange("p a b -> p (a b)")[:, 0:(t + 1) * P]
                dve.wait_ge(sem("a_s"), u0 + u + 1)
                D(TT(PS[:, bank, col:col + P], PS[:, bank, col:col + P], cst[:, C_CAUSAL:C_CAUSAL + P], ALU.add))
                D(nc.vector.tensor_reduce(nmax[:, u % 2:u % 2 + 1], s_, AX.X, ALU.max))
                TS(nms[:, u % 2:u % 2 + 1], nmax[:, u % 2:u % 2 + 1], -SCALE, None, ALU.mult).then_inc(sem("a_m"), 1)

            def divide(u, u0):
                j, n = u % 2, (u // 2 + 1) * P
                dve.wait_ge(sem("a_p"), u0 + u + 1)
                D(nc.vector.reciprocal(rden[:, j:j + 1], den[:, j:j + 1]))
                TS(Pb[j][:, 0:n], Pb[j][:, 0:n], rden[:, j:j + 1], None, ALU.mult).then_inc(sem("a_w"), 1)

            with dve.Fori(0, 2) as a, D.rounds(a, 2 * (3 + 16 * 3), 2):
                for pp in range(2):
                    u0 = a * 32 + pp * 16
                    dve.wait_ge(sem("a_vmm"), a * 2 + pp + 1)
                    D(nc.vector.tensor_copy(V[:, :, :].rearrange("p (a b) c -> p a (b c)", a=2), PS[:, 5:7, :]))
                    dve.wait_ge(sem("a_qk"), a * 4 + pp * 2 + 1)
                    part(dve)
                    for j in range(2):
                        r = ROPE * (2 * pp + j)
                        D(nc.vector.tensor_copy(Q[j][NOPE:QK, :], peT[r:r + ROPE, a, :]))
                        nc.vector.tensor_copy(qns[:, a * 4 + (2 * pp + j), :], Q[j][0:NOPE, PROMPT:TOK]).then_inc(sem("a_qns"), 1)
                    dve.wait_ge(sem("a_qns"), a * 4 + pp * 2 + 2)
                    dve.sem_inc(sem("a_qk"), 1)
                    maximum(0, u0)
                    for u in range(16):
                        if u < 15:
                            maximum(u + 1, u0)
                        divide(u, u0)

        kv = [xT, kv1]

        def page(s, n):
            return kv[s][:, n // 4, n % 4 * ROW:(n % 4 + 1) * ROW]

        ROUND = [1, 2, 3, 4, 6, 7, 8, 9]

        def load_quarter(sp, b, s, h):
            for n in range(h * 8, h * 8 + 8):
                phys = sp.value_load(pages[0:1, bass.ds(b * PAGES + n, 1)], min_val=0, max_val=io["cache"].shape[0] // PAGE - 1)
                sp.dma_start(page(s, n), io["cache"][bass.ds(phys * PAGE, PAGE), :]).then_inc(sem(f"in_kv{s}{h}"), 16)

        def kv_loaded(b, s):
            return (b + (2 - s)) * 64

        def sp_sample(sp):
            for h in range(4):
                load_quarter(sp, 0, 0, h)
            sp.wait_ge(sem("a_yt"), 2 + 32)
            sp.wait_ge(sem("a_qns"), 8)
            for n in range(2):
                sp.dma_start(wukT[n], io["wukT"][:, 4 * n:4 * n + 4, :]).then_inc(sem("in_wukT"), 16)
            for h in range(4):
                load_quarter(sp, 1, 1, h)
            with sp.Fori(0, 3) as i:
                for s in range(2):
                    for h in range(4):
                        sp.wait_ge(sem("d_pv"), i * 8 + (4 * s + h + 1))
                        load_quarter(sp, i * 2 + s + 2, s, h)

        def sequences(eng, body):
            body(0, 0, True, False)
            with eng.Fori(0, 3) as i:
                body(i * 2 + 1, 1, False, False)
                body(i * 2 + 2, 0, False, False)
            body(7, 1, False, False)
            body(8, 0, False, True)

        def pe_sample(pe):
            pe.wait_ge(sem("in_wukT"), 32)
            for r in range(2):
                for h in range(HEADS):
                    ins = nc.tensor.matmul(PS[:, r, h * SAMPLE:(h + 1) * SAMPLE], wukT[h // 4][:, h % 4, r * P:(r + 1) * P], qns[:, h, :], start=True, stop=True)
            ins.then_inc(sem("d_ql"), 1)
            for r in range(2):
                ins = nc.tensor.transpose(PS[0:SAMPLE, 2, r * P:(r + 1) * P], ckvT[:, r, PROMPT:TOK], ident)
            ins.then_inc(sem("d_ql"), 1)
            pe.wait_ge(sem("d_qa"), 2)
            pe.wait_ge(sem("d_qd"), 1)

            def body(b, s, first, last):
                sb_ = 2 + 2 * s

                def turn(k):
                    q = ROUND.index(k) if k in ROUND else None
                    if q is None:
                        pe.wait_ge(sem("d_kp"), b * 2 + k // 5 + 1)
                    else:
                        pe.wait_ge(sem(f"in_kv{s}{q // 2}"), kv_loaded(b, s))
                    pe.wait_ge(sem("d_cta"), b * 10 + k)
                    pe.wait_ge(sem("d_ctd"), b * 10 + k)
                    part(pe)
                    if q is None:
                        for n in range(4):
                            ins = nc.tensor.transpose(PS[:, n // 2, n % 2 * P:n % 2 * P + P], kpr[:, k // 5, n, :, :].rearrange("p a b -> p (a b)"), ident)
                    else:
                        for n in range(8):
                            ins = nc.tensor.transpose(PS[:, n // 4, n % 4 * P:n % 4 * P + P], page(s, 4 * q + n % 4)[:, n // 4 * P:(n // 4 + 1) * P], ident)
                    ins.then_inc(sem("d_t"), 1)

                def scores(q):
                    pe.wait_ge(sem("d_cta"), b * 10 + ROUND[q] + 1)
                    pe.wait_ge(sem("d_ctd"), b * 10 + ROUND[q] + 1)
                    g, bank = q % 4 * QS, sb_ + q // 4
                    for r in range(2):
                        nc.tensor.matmul(PS[g:g + QS, bank, :], qb[:, s, r, :], CT[:, q % 2, r, :], start=(r == 0), stop=False)
                    for j in range(4):
                        ins = nc.tensor.matmul(PS[g:g + QS, bank, j * P:(j + 1) * P], qpb[:, s, j, :], KT[:, q, :], start=False, stop=(j == 3))
                    if q in (3, 7):
                        ins.then_inc(sem("d_s"), 1)

                if not last:
                    turn(0)
                    turn(1)
                if not first:
                    pe.wait_ge(sem("d_mx"), b)
                    nc.tensor.transpose(PS[0:1, 6, P:2 * P], mxd[:, :], ident).then_inc(sem("d_mt"), 1)
                if not last:
                    turn(2)
                    pe.wait_ge(sem("d_prep"), b * 2 + 2)
                    scores(0)
                if not first:
                    pe.wait_ge(sem("d_mr"), b)
                    nc.tensor.matmul(PS[:, 6, 2 * P:2 * P + 1], m4[:, :, :].rearrange("p a b -> p (a b)"), ones[0:1, 0:1],
                                     start=True, stop=True).then_inc(sem("d_mb"), 1)
                if not last:
                    turn(3)
                    scores(1)
                if not first:
                    pe.wait_ge(sem("d_e"), b * 2)
                    if not last:
                        pe.wait_ge(sem("d_cta"), b * 10 + 4)
                        pe.wait_ge(sem("d_ctd"), b * 10 + 4)
                    for n in range(8):
                        nc.tensor.transpose(PS[:, n // 4, n % 4 * P:n % 4 * P + P], Pd[:, n * P:(n + 1) * P], ident)
                    nc.tensor.transpose(PS[0:SAMPLE, 6, 3 * P:3 * P + QS], Pn[:, :], ident[0:QS, 0:QS])
                    nc.tensor.matmul(PS[0:QS, 6, 3 * P + QS:3 * P + QS + 1], cst[:, C_FOLD:C_FOLD + QS], dend[:, :],
                                     start=True, stop=True).then_inc(sem("d_p"), 1)
                if not last:
                    scores(2)
                if not first:
                    pe.wait_ge(sem("d_pta"), b)
                    pe.wait_ge(sem("d_ptd"), b)
                if not last:
                    turn(4)
                if not first:
                    pe.wait_ge(sem("d_oc"), b)
                    for n in range(PAGES):
                        quad, p = n // 4, n % 4
                        ins = nc.tensor.matmul(PS[0:QS, 7, 0:KV_RANK], PTd[:, quad // 4 * 4 + p, quad % 4 * QS:(quad % 4 + 1) * QS], page(1 - s, n)[:, 0:KV_RANK],
                                               start=(n == 0), stop=False)
                        if n % 8 == 7 and n < PAGES - 1:
                            ins.then_inc(sem("d_pv"), 1)
                    nc.tensor.matmul(PS[0:QS, 7, 0:KV_RANK], PTn[:, :], ckn[:, :], start=False, stop=True).then_inc(sem("d_pv"), 1)
                if not last:
                    turn(5)
                    scores(3)
                    turn(6)
                if not first:
                    pe.wait_ge(sem("d_ol"), b)
                    part(pe)
                    for r in range(2):
                        ins = nc.tensor.transpose(PS[:, 7, KV_RANK + r * QS:KV_RANK + (r + 1) * QS], olr[:, r * P:(r + 1) * P], ident[0:QS, 0:QS])
                    ins.then_inc(sem("d_ot"), 1)
                if not last:
                    turn(7)
                    scores(4)
                    turn(8)
                    scores(5)
                    turn(9)
                    scores(6)
                    for r in range(2):
                        nc.tensor.matmul(PS[0:QS, 6, 0:SAMPLE], qb[:, s, r, :], ckvT[:, r, PROMPT:TOK], start=(r == 0), stop=False)
                    nc.tensor.matmul(PS[0:QS, 6, 0:SAMPLE], qpb[0:ROPE, s, 0, :], kpeS[:, :], start=False, stop=True)
                    scores(7)

            pe.sem_inc(sem("d_oc"), 1)
            sequences(pe, body)
            pe.wait_ge(sem("d_oc"), 1 + 8)
            for h in range(HEADS):
                o = V_DIM * (h % 2)
                for r in range(2):
                    ins = nc.tensor.matmul(PS[o:o + V_DIM, h // 2 % 2, h // 4 * SAMPLE:(h // 4 + 1) * SAMPLE], wuv[:, r, h * V_DIM:(h + 1) * V_DIM],
                                           olat[:, r, :, h * STEP:(h + 1) * STEP], start=(r == 0), stop=(r == 1))
            ins.then_inc(sem("d_y"), 1)

        def pool_sample(pool):
            CP = nc.gpsimd.tensor_copy
            pool.wait_ge(sem("d_qa"), 2)
            pool.wait_ge(sem("d_qp"), 1)

            def fill(b, s):
                CP(qb[:, s, :, :], qlat[:, :, b, :]).then_inc(sem("d_prep"), 1)
                CP(qpb[:, s, :, :], qpz[:, b, :, :]).then_inc(sem("d_prep"), 1)

            def rotary_keys(b, s, half):
                for h in range(2):
                    pool.wait_ge(sem(f"in_kv{s}{2 * half + h}"), kv_loaded(b, s))
                part(pool)
                CP(kpr[:, half, :, :, :], kv[s][:, 4 * half:4 * half + 4, :].rearrange("p q (a c) -> p q a c", c=ROW)[:, :, :, KV_RANK:ROW]).then_inc(sem("d_kp"), 1)

            def both(b, s):
                for half in range(2):
                    pool.wait_ge(sem("d_t"), b * 10 + (5 * half - 9))
                    rotary_keys(b, s, half)

            fill(0, 0)
            fill(1, 1)
            for half in range(2):
                rotary_keys(0, 0, half)
            both(1, 1)
            with pool.Fori(0, 3) as i:
                for s in range(2):
                    pool.wait_ge(sem("d_s"), i * 4 + 2 * s + 2)
                    part(pool)
                    fill(i * 2 + 2 + s, s)
                    both(i * 2 + 2 + s, s)

        def act_sample(act, A):
            AC = nc.scalar.activation
            act.wait_ge(sem("d_ql"), 1)
            for r in range(2):
                src = PS[:, r, 0:HEADS * SAMPLE].rearrange("p (h b t) -> p b h t", h=HEADS, t=STEP)
                AC(qlat[:, r, :, :].rearrange("p b (h t) -> p b h t", t=STEP), src, ACT.Copy).then_inc(sem("d_qa"), 1)

            def body(b, s, first, last):
                def take(k):
                    act.wait_ge(sem("d_t"), b * 10 + k + 1)
                    part(act)
                    ins = AC(CT[:, ROUND.index(k) % 2, 0, :], PS[:, 0, :], ACT.Copy) if k in ROUND else \
                        AC(KT[:, k // 5 * 4:k // 5 * 4 + 2, :].rearrange("p a b -> p (a b)"), PS[:, 0, 0:2 * P], ACT.Copy)
                    ins.then_inc(sem("d_cta"), 1)
                if not last:
                    take(0)
                    take(1)
                    take(2)
                if not first:
                    act.wait_ge(sem("d_nm"), b)
                    AC(Pd[:, :].rearrange("p (a b) -> p a b", a=2), PS[:, 4 - 2 * s:6 - 2 * s, :], ACT.Exp, scale=SCALE, bias=nmd[:, :], accum_out=dend[:, :]).then_inc(sem("d_e"), 1)
                    AC(Pn[:, :], sn[:, :], ACT.Exp, scale=SCALE, bias=nmd[0:QS, :], accum_out=denn[:, :]).then_inc(sem("d_e"), 1)
                if not last:
                    take(3)
                if not first:
                    act.wait_ge(sem("d_p"), b)
                    AC(PTd[:, 0:4, :].rearrange("p a b -> p (a b)"), PS[:, 0, :], ACT.Copy).then_inc(sem("d_pta"), 1)
                if not last:
                    take(4)
                    take(5)
                    take(6)
                if not first:
                    act.wait_ge(sem("d_ot"), b)
                    part(act)
                    AC(olat[:, :, b - 1, :], PS[:, 7, KV_RANK:KV_RANK + 2 * QS].rearrange("p (r q) -> p r q", q=QS), ACT.Copy).then_inc(sem("d_oc"), 1)
                if not last:
                    take(7)
                    take(8)
                    take(9)

            sequences(act, body)
            act.wait_ge(sem("d_y"), 1)
            for a in range(2):
                AC(yT[:, 4 + a:8:2, PROMPT:TOK], PS[:, a, 0:2 * SAMPLE].rearrange("p (c t) -> p c t", t=SAMPLE), ACT.Copy).then_inc(sem("d_yt"), 1)

        def dve_sample(dve, D):
            D(nc.vector.memset(qpz[:, :, :, :], 0.0))
            for j in range(4):
                for hh in range(4):
                    for a in range(2):
                        h = a * 4 + hh
                        D(nc.vector.tensor_copy(qpz[ROPE * j:ROPE * (j + 1), :, j, h * STEP:(h + 1) * STEP],
                                                peT[ROPE * hh:ROPE * (hh + 1), a, PROMPT:TOK].rearrange("p (b t) -> p b t", t=STEP)))
            dve.sem_inc(sem("d_qp"), 1)
            dve.wait_ge(sem("d_ql"), 2)
            nc.vector.tensor_copy(ckn[:, :], PS[0:SAMPLE, 2, 0:KV_RANK]).then_inc(sem("d_qd"), 1)
            new = cst[0:QS, C_NEW:C_NEW + SEQS * SAMPLE].rearrange("p (b k) -> p b k", k=SAMPLE)
            TR = nc.vector.tensor_reduce

            def body(b, s, first, last):
                def take(k):
                    dve.wait_ge(sem("d_t"), b * 10 + k + 1)
                    part(dve)
                    ins = nc.vector.tensor_copy(CT[:, ROUND.index(k) % 2, 1, :], PS[:, 1, :]) if k in ROUND else \
                        nc.vector.tensor_copy(KT[:, k // 5 * 4 + 2:k // 5 * 4 + 4, :].rearrange("p a b -> p (a b)"), PS[:, 1, 0:2 * P])
                    ins.then_inc(sem("d_ctd"), 1)
                if not last:
                    take(0)
                if not first:
                    dve.wait_ge(sem("d_s"), b * 2)
                    part(dve)
                    D(TT(sn[:, :], PS[0:QS, 6, 0:SAMPLE], new[:, b - 1, :], ALU.add))
                    D(TR(mxd[:, :], PS[:, 5 - 2 * s, :], AX.X, ALU.max))
                    D(TR(mxn[:, :], sn[:, :], AX.X, ALU.max))
                    D(TT(mxd[:, :], mxd[:, :], mxa[:, :], ALU.max))
                    TT(mxd[0:QS, :], mxd[0:QS, :], mxn[:, :], ALU.max).then_inc(sem("d_mx"), 1)
                if not last:
                    take(1)
                if not first:
                    dve.wait_ge(sem("d_mt"), b)
                    D(TR(mrow[:, :], PS[0:1, 6, P:2 * P].rearrange("p (j q) -> p q j", q=QS), AX.X, ALU.max))
                    TS(m4[:, :, :], mrow[:, :].unsqueeze(1).broadcast_to([1, 4, QS]), -SCALE, None, ALU.mult).then_inc(sem("d_mr"), 1)
                if not last:
                    take(2)
                if not first:
                    dve.wait_ge(sem("d_mb"), b)
                    nc.vector.tensor_copy(nmd[:, :], PS[:, 6, 2 * P:2 * P + 1]).then_inc(sem("d_nm"), 1)
                if not last:
                    take(3)
                if not first:
                    dve.wait_ge(sem("d_p"), b)
                    D(nc.vector.tensor_copy(PTn[:, :], PS[0:SAMPLE, 6, 3 * P:3 * P + QS]))
                    D(TT(rdd[:, :], PS[0:QS, 6, 3 * P + QS:3 * P + QS + 1], denn[:, :], ALU.add))
                    D(nc.vector.reciprocal(rdd[:, :], rdd[:, :]))
                    nc.vector.tensor_copy(PTd[:, 4:8, :].rearrange("p a b -> p (a b)"), PS[:, 1, :]).then_inc(sem("d_ptd"), 1)
                if not last:
                    take(4)
                if not first:
                    dve.wait_ge(sem("d_pv"), b * 4)
                    TS(olr[:, :], PS[0:QS, 7, 0:KV_RANK], rdd[:, :], None, ALU.mult).then_inc(sem("d_ol"), 1)
                if not last:
                    take(5)
                    take(6)
                    dve.wait_ge(sem("d_s"), b * 2 + 1)
                    D(TR(mxa[:, :], PS[:, 2 + 2 * s, :], AX.X, ALU.max))
                    take(7)
                    take(8)
                    take(9)

            with D.rounds(0, 1, 1):
                body(0, 0, True, False)
            with dve.Fori(0, 3) as i, D.rounds(i, 2 * 9, 3):
                body(i * 2 + 1, 1, False, False)
                body(i * 2 + 2, 0, False, False)
            body(7, 1, False, False)
            body(8, 0, False, True)

        @block.sync
        def _(sp):
            for s in range(3):
                sp.sem_inc(sem(f"n_out{s}"), 16)
            sp.dma_start(cst[:], io["cst"]).then_inc(sem("in_const"), 16)
            sp.dma_start(evp[:], io["ev_pack"]).then_inc(sem("in_const"), 16)
            sp.dma_start(wr[:], io["w_router"].rearrange("(k p) n -> p k n", p=P)).then_inc(sem("in_const"), 16)
            sp.dma_start(brt[:], io["b_router"].partition_broadcast(P)).then_inc(sem("in_const"), 16)
            sp_even(sp)
            load_wo(sp, 0)
            sp.wait_ge(sem("yb_done"), 4)
            sp.wait_ge(sem("out_states"), 16)
            sp_mix(sp, 0)
            sp_experts(sp, 0)
            sp_ffn(sp, 0)
            sp.wait_ge(sem("n_tp"), 2 * NT)
            sp_odd(sp)
            sp_prompt(sp)
            sp_sample(sp)
            sp.wait_ge(sem("d_yt"), 2)
            sp_mix(sp, 1)
            sp_experts(sp, 1)
            sp_ffn(sp, 1)

        @block.gpsimd
        def _(pool):
            G = Steps(pool, sem("pool_step"), sem("apart"))
            for name in ("states_kept", "o_prods", "o_pc"):
                pool.sem_inc(sem(name), 1)
            pool_even(pool, G)
            pool_mix(pool, 0)
            pool_route(pool, G, 0)
            pool_experts(pool, 0)
            pool_ffn(pool, 0)
            pool_odd(pool, G)
            pool_sample(pool)
            pool.wait_ge(sem("d_yt"), 2)
            pool_mix(pool, 1)
            pool_route(pool, G, 1)
            pool_experts(pool, 1)
            pool_ffn(pool, 1)

        @block.tensor
        def _(pe):
            for name in ("z_mm", "lru_mm", "e0_tp", "e1_tp", "o_mm", "a_proj"):
                pe.sem_inc(sem(name), 1)
            pe.wait_ge(sem("in_const"), 64)
            pe_even(pe)
            pe_mix(pe, 0)
            pe_route(pe, 0)
            pe_experts(pe, 0)
            pe_ffn(pe, 0)
            pe_odd(pe)
            pe_prompt(pe)
            pe_sample(pe)
            pe_mix(pe, 1)
            pe_route(pe, 1)
            pe_experts(pe, 1)

        @block.scalar
        def _(act):
            A = Steps(act, sem("act_step"))
            for name in ("n_tpo", "m_lg", "a_pt"):
                act.sem_inc(sem(name), 1)
            for l in range(2):
                act.sem_inc(sem(f"e{l}_yb"), 16)
            act.wait_ge(sem("in_const"), 64)
            act_even(act, A)
            act_mix(act, 0)
            act_route(act, A, 0)
            act_experts(act, 0)
            act_ffn(act, 0)
            act_odd(act, A)
            act_prompt(act, A)
            act_sample(act, A)
            act_mix(act, 1)
            act_route(act, A, 1)
            act_experts(act, 1)
            act_ffn(act, 1)

        @block.vector
        def _(dve):
            D = Steps(dve, sem("dve_step"))
            for name in ("e0_y_out", "e1_y_out", "o_conv"):
                dve.sem_inc(sem(name), 1)
            dve_even(dve, D)
            dve_mix(dve, D, 0)
            dve_route(dve, D, 0)
            dve_experts(dve, 0)
            dve_ffn(dve, D, 0)
            dve_odd(dve, D)
            dve_prompt(dve, D)
            dve_sample(dve, D)
            dve_mix(dve, D, 1)
            dve_route(dve, D, 1)
            dve_experts(dve, 1)
            dve_ffn(dve, D, 1)


def constants():
    c = np.zeros((P, C_N), np.float32)
    c[:, C_ID:C_ID + P] = np.eye(P)
    c[:, C_ONE:C_ONE + P] = 1
    c[:, C_TRI:C_TRI + P] = np.triu(np.ones((P, P)), 1)
    c[:, C_IOTA:C_IOTA + 16] = np.arange(16, 0, -1)
    c[:, C_IOTA4:C_IOTA4 + 4] = np.arange(4, 0, -1)
    tok = np.arange(P)[:, None] + P * np.arange(NT)[None, :]
    c[:, C_TOK:C_TOK + NT] = tok
    c[:, C_VALID:C_VALID + NT] = tok < TOK
    c[:, C_CAUSAL:C_CAUSAL + P] = np.where(np.arange(P)[None, :] <= np.arange(P)[:, None], 0, -BIG)
    row = np.arange(QS)[:, None, None, None]
    b, kb, kt = np.arange(SEQS)[None, :, None, None], np.arange(SEQS)[None, None, :, None], np.arange(STEP)[None, None, None, :]
    c[:QS, C_NEW:C_NEW + SEQS * SAMPLE] = np.where((kb == b) & (kt <= row % STEP), 0, -BIG).reshape(QS, -1)
    c[:, C_FOLD:C_FOLD + QS] = np.tile(np.eye(QS), (4, 1))
    return c


def rotary():
    half = ROPE // 2
    inv = np.float32(10000.0) ** (-np.arange(half, dtype=np.float32) / np.float32(half))
    pos = np.concatenate([np.arange(PROMPT), np.tile(PAST + np.arange(STEP), SEQS)]).astype(np.float32)
    ang = (pos[None, :] * inv[:, None]).astype(np.float32)
    cos, sin = np.cos(ang).astype(np.float32), np.sin(ang).astype(np.float32)
    return np.tile(np.concatenate([cos, cos]), (4, 1)), np.tile(np.concatenate([-sin, sin]), (4, 1))


def kernel(**inp):
    import concourse.bacc as bacc
    from concourse.bass_utils import run_bass_kernel_spmd

    inp = {k: np.asarray(v) for k, v in inp.items()}
    x = np.concatenate([inp["x_prompt"].reshape(PROMPT, D), inp["x_sample"].reshape(SAMPLE, D)])
    xpad = np.concatenate([x, np.zeros((TOKP - TOK, D), x.dtype)])

    def by_channel(a):
        a = a.reshape(-1, 4, P)
        return a.transpose(2, 1, 0)

    kpe = inp["w_in_odd"][0][:, -ROPE:]
    wq = inp["w_q_b"][0].reshape(Q_RANK, HEADS, QK)
    wqp = wq[:, :, NOPE:]
    cos, sin = rotary()
    arrays = {
        "cst": constants(), "xT0": np.ascontiguousarray(x.T), "xtok": xpad,
        "w_in_even": inp["w_in_even"][0], "w_out_even": inp["w_out_even"][0],
        "lru_wa": inp["lru_wa"][0].reshape(512, 64), "lru_wx": inp["lru_wx"][0].reshape(512, 64),
        "ev_pack": np.concatenate([by_channel(a) for a in (
            inp["conv_a_w"][0], inp["conv_b_w"][0], inp["conv_b_b"][0], inp["lru_ba"][0], inp["lru_bx"][0],
            inp["lru_lambda"][0], inp["state_conv_a"][0], inp["state_conv_b"][0], inp["state_rglru_h"][0])], axis=2),
        "w_in_odd": inp["w_in_odd"][0], "w_out_odd": inp["w_out_odd"][0],
        "w_kpe": np.concatenate([kpe, kpe[:, ROPE // 2:], kpe[:, :ROPE // 2]], axis=1),
        "wqn": wq[:, :, :NOPE].reshape(Q_RANK, -1), "wqp": wqp.reshape(Q_RANK, -1),
        "wqs": np.concatenate([wqp[:, :, ROPE // 2:], wqp[:, :, :ROPE // 2]], axis=2).reshape(Q_RANK, -1),
        "wuk": inp["w_uk"][0].reshape(KV_RANK, -1), "wukT": inp["w_uk"][0].transpose(2, 1, 0),
        "wuv": inp["w_uv"][0].reshape(KV_RANK, -1), "cosq": cos, "sinq": sin,
        "od_pack": np.concatenate([by_channel(a) for a in (
            inp["conv_c_w"][0], inp["conv_c_b"][0], inp["ln_c_g"][0], inp["ln_c_b"][0], inp["state_conv_c"][0])], axis=2),
        "gqk": np.concatenate([inp["q_norm_g"][0].reshape(3, P), inp["kv_norm_g"][0].reshape(2, P)]).T,
        "page_table": inp["page_table"].reshape(1, -1),
        "cache": np.concatenate([inp["cache_ckv"].reshape(-1, KV_RANK), inp["cache_kpe"].reshape(-1, ROPE)], axis=1),
        "w_router": inp["w_router"], "b_router": inp["b_router"],
        "ln_mix_g": inp["ln_mix_g"], "ln_mix_b": inp["ln_mix_b"], "ln_ffn_g": inp["ln_ffn_g"], "ln_ffn_b": inp["ln_ffn_b"],
        "w_exp_in": inp["w_exp_in"].reshape(-1, 2 * F_EXP), "w_exp_out": inp["w_exp_out"].reshape(-1, D),
    }
    nc = bacc.Bacc("TRN2", target_bir_lowering=False, num_devices=1)
    io = {}
    arrays = {name: np.ascontiguousarray(a) for name, a in arrays.items()}
    for name, a in arrays.items():
        io[name] = nc.dram_tensor("in_" + name, list(a.shape), mybir.dt.from_np(a.dtype), kind="ExternalInput").ap()
    arrays = {"in_" + name: a for name, a in arrays.items()}
    for name, shape in (("y", [TOKP, D]), ("even_states", [P, 4, 54]), ("odd_states", [P, 4, 270]),
                        ("out_ckvT", [KV_RANK, TOK]), ("out_kpeT", [ROPE, TOK])):
        io[name] = nc.dram_tensor(name, shape, F32, kind="ExternalOutput").ap()
    for name, shape, dt in (("xm0", [TOKP, D], F32), ("xm1", [TOKP, D], F32), ("x1", [TOKP, D], F32),
                            ("yb", [(MAX_BLOCKS + 1) * P, D], F32), ("tokbuf", [(MAX_BLOCKS + 1) * P, 1], I32)):
        io[name] = nc.dram_tensor(name, shape, dt, kind="Internal").ap()
    build(nc, io)
    nc.compile()
    got = run_bass_kernel_spmd(nc, [arrays], core_ids=[0]).results[0]
    y = got["y"]
    ev, od = got["even_states"], got["odd_states"]

    def states(a, first, n):
        a = a[:, :, first:first + (1 + SEQS) * n].reshape(P, 4, 1 + SEQS, n).transpose(2, 3, 1, 0).reshape(1 + SEQS, n, 512)
        return a[None, :1], a[None, 1:]

    ca, cb, hl, cc = states(ev, 0, 2), states(ev, 18, 3), states(ev, 45, 1), states(od, 0, 30)

    def latents(a):
        return a[:, :PROMPT].T[None, None], a[:, PROMPT:].T.reshape(SEQS, 1, STEP, -1)

    ck, kp = latents(got["out_ckvT"]), latents(got["out_kpeT"])
    out = (y[:PROMPT].reshape(1, PROMPT, D), y[PROMPT:TOK].reshape(SEQS, STEP, D), ca[0], ca[1], cb[0], cb[1],
           hl[0][:, :, 0], hl[1][:, :, 0], cc[0], cc[1], ck[0], ck[1], kp[0], kp[1])
    return tuple(np.ascontiguousarray(a) for a in out)
```
